# Optimizing a Trainium2 kernel written in Bass

```python
import math
import jax, jax.numpy as jnp
from jax import lax
import numpy as np

D_MODEL = 2048
BATCH = 1
SEQ = 256
DEPTH = 2

HEAD_DIM = 64
DIFF_HEADS = 8
DIFF_QK = 2 * DIFF_HEADS * HEAD_DIM
DIFF_V_DIM = 2 * HEAD_DIM
DIFF_V = DIFF_HEADS * DIFF_V_DIM
Q_BLOCK = 128
SWA_Q_HEADS = 16
SWA_KV_HEADS = 2
SWA_GROUP = SWA_Q_HEADS // SWA_KV_HEADS
SWA_WINDOW = 128
SWA_BLOCK = 128
SWA_Q = SWA_Q_HEADS * HEAD_DIM
SWA_KV = SWA_KV_HEADS * HEAD_DIM
EVEN_SPLITS = [DIFF_QK, DIFF_QK, DIFF_V, SWA_Q, SWA_KV, SWA_KV]
EVEN_IN = sum(EVEN_SPLITS)
MIX_WIDTH = DIFF_V + SWA_Q
LRU_WIDTH = D_MODEL
LRU_BLOCKS = 8
LRU_BLOCK_DIM = LRU_WIDTH // LRU_BLOCKS
CONV_WIDTH = 4
LRU_C = 8.0
D_FF = 4 * D_MODEL
N_EVEN = (DEPTH + 1) // 2
N_ODD = DEPTH // 2
EPS = 1e-6


def rmsnorm(x, g):
    xf = x.astype(jnp.float32)
    y = xf * lax.rsqrt(jnp.mean(xf * xf, axis=-1, keepdims=True) + EPS)
    return (y * g.astype(jnp.float32)).astype(x.dtype)

def diff_attention(q, k, v, lq1, lk1, lq2, lk2, sub_g, lambda_init):
    B, S = q.shape[0], q.shape[1]
    nb = S // Q_BLOCK
    scale = HEAD_DIM ** -0.5
    f32 = jnp.float32
    lam = (jnp.exp(jnp.sum(lq1.astype(f32) * lk1.astype(f32)))
           - jnp.exp(jnp.sum(lq2.astype(f32) * lk2.astype(f32))) + lambda_init)
    qb = q.reshape(B, nb, Q_BLOCK, 2 * DIFF_HEADS, HEAD_DIM).transpose(1, 0, 2, 3, 4)
    kpos = jnp.arange(S)

    def block(args):
        qi, i = args
        s = jnp.einsum('bqhd,bkhd->bhqk', qi, k).astype(f32) * scale
        qpos = i * Q_BLOCK + jnp.arange(Q_BLOCK)
        causal = kpos[None, :] <= qpos[:, None]
        s = jnp.where(causal[None, None], s, -jnp.inf)
        p = jax.nn.softmax(s, axis=-1).reshape(B, DIFF_HEADS, 2, Q_BLOCK, S)
        w = p[:, :, 0] - lam * p[:, :, 1]
        return jnp.einsum('bhqk,bkhe->bqhe', w.astype(v.dtype), v)

    o = lax.map(block, (qb, jnp.arange(nb)))
    o = o.transpose(1, 0, 2, 3, 4).reshape(B, S, DIFF_HEADS, DIFF_V_DIM)
    o = rmsnorm(o, sub_g) * (1.0 - lambda_init)
    return o.reshape(B, S, DIFF_V)

def swa_with_sinks(q, k, v, sinks):
    B, S = q.shape[0], q.shape[1]
    nb = S // SWA_BLOCK
    f32 = jnp.float32
    qb = q.reshape(B, nb, SWA_BLOCK, SWA_KV_HEADS, SWA_GROUP, HEAD_DIM)

    def band(t):
        tb = t.reshape(B, nb, SWA_BLOCK, SWA_KV_HEADS, HEAD_DIM)
        prev = jnp.pad(tb, ((0, 0), (1, 0), (0, 0), (0, 0), (0, 0)))[:, :-1]
        return jnp.concatenate([prev, tb], axis=2)

    kb, vb = band(k), band(v)
    s = jnp.einsum('bnqhgd,bnkhd->bnhgqk', qb, kb).astype(f32) * (HEAD_DIM ** -0.5)
    qpos = jnp.arange(SWA_BLOCK) + SWA_BLOCK
    kpos = jnp.arange(2 * SWA_BLOCK)
    rel = qpos[:, None] - kpos[None, :]
    in_window = (rel >= 0) & (rel < SWA_WINDOW)
    not_pad = (jnp.arange(nb)[:, None] > 0) | (kpos[None, :] >= SWA_BLOCK)
    mask = in_window[None] & not_pad[:, None, :]
    s = jnp.where(mask[None, :, None, None], s, -jnp.inf)
    sink = sinks.astype(f32).reshape(SWA_KV_HEADS, SWA_GROUP)[None, None, :, :, None, None]
    m = jnp.maximum(jnp.max(s, axis=-1, keepdims=True), sink)
    e = jnp.exp(s - m)
    p = e / (jnp.sum(e, axis=-1, keepdims=True) + jnp.exp(sink - m))
    o = jnp.einsum('bnhgqk,bnkhd->bnqhgd', p.astype(v.dtype), vb)
    return o.reshape(B, S, SWA_Q)

def even_mixer(h, w_in, lq1, lk1, lq2, lk2, sub_g, sinks, w_out, lambda_init):
    B, S, _ = h.shape
    proj = h @ w_in
    idx = [int(v) for v in np.cumsum(EVEN_SPLITS)[:-1]]
    qa, ka, va, qs, ks, vs = jnp.split(proj, idx, axis=-1)
    a_out = diff_attention(
        qa.reshape(B, S, 2 * DIFF_HEADS, HEAD_DIM),
        ka.reshape(B, S, 2 * DIFF_HEADS, HEAD_DIM),
        va.reshape(B, S, DIFF_HEADS, DIFF_V_DIM),
        lq1, lk1, lq2, lk2, sub_g, lambda_init)
    b_out = swa_with_sinks(
        qs.reshape(B, S, SWA_Q_HEADS, HEAD_DIM),
        ks.reshape(B, S, SWA_KV_HEADS, HEAD_DIM),
        vs.reshape(B, S, SWA_KV_HEADS, HEAD_DIM),
        sinks)
    return jnp.concatenate([a_out, b_out], axis=-1) @ w_out

def causal_depthwise_conv(x, w, b):
    y = lax.conv_general_dilated(
        x, w[:, None, :], window_strides=(1,), padding=[(CONV_WIDTH - 1, 0)],
        dimension_numbers=('NWC', 'WIO', 'NWC'), feature_group_count=x.shape[-1])
    return y + b

def rglru_mixer(h, w_in, conv_w, conv_b, gate_w, gate_b, lru_lambda, w_out):
    B, S, _ = h.shape
    f32 = jnp.float32
    proj = h @ w_in
    y_branch, x_branch = jnp.split(proj, 2, axis=-1)
    y_branch = jax.nn.gelu(y_branch)
    xc = causal_depthwise_conv(x_branch, conv_w, conv_b)
    xb = xc.reshape(B, S, LRU_BLOCKS, LRU_BLOCK_DIM)
    gates = jnp.einsum('bsnd,gnde->gbsne', xb, gate_w) + gate_b[:, None, None]
    r = jax.nn.sigmoid(gates[0].astype(f32)).reshape(B, S, LRU_WIDTH)
    i = jax.nn.sigmoid(gates[1].astype(f32)).reshape(B, S, LRU_WIDTH)
    log_a = -LRU_C * r * jax.nn.softplus(-lru_lambda.astype(f32))
    a = jnp.exp(log_a)
    u = jnp.sqrt(-jnp.expm1(2.0 * log_a)) * (i * xc.astype(f32))

    def combine(left, right):
        a1, b1 = left
        a2, b2 = right
        return a1 * a2, a2 * b1 + b2

    _, hs = lax.associative_scan(combine, (a, u), axis=1)
    return (hs.astype(h.dtype) * y_branch) @ w_out

def sq_relu_mlp(h, w1, w2):
    z = jax.nn.relu(h @ w1)
    return (z * z) @ w2

def first_inputs(seed: int = 0) -> dict:
    key = jax.random.key(seed)
    ks = jax.random.split(key, 24)
    f32 = jnp.float32
    nrm = lambda k, shape, s: jax.random.normal(k, shape, f32) * s
    gain = lambda k, shape: 1.0 + 0.05 * jax.random.normal(k, shape, f32)
    a0 = jax.random.uniform(ks[14], (N_ODD, LRU_WIDTH), f32, 0.9, 0.999)
    sig = a0 ** (1.0 / LRU_C)
    return {
        "x": jax.random.normal(ks[0], (BATCH, SEQ, D_MODEL), f32),
        "even_w_in": nrm(ks[1], (N_EVEN, D_MODEL, EVEN_IN), D_MODEL ** -0.5),
        "even_lam_q1": nrm(ks[2], (N_EVEN, HEAD_DIM), 0.1),
        "even_lam_k1": nrm(ks[3], (N_EVEN, HEAD_DIM), 0.1),
        "even_lam_q2": nrm(ks[4], (N_EVEN, HEAD_DIM), 0.1),
        "even_lam_k2": nrm(ks[5], (N_EVEN, HEAD_DIM), 0.1),
        "even_subln_g": gain(ks[6], (N_EVEN, DIFF_V_DIM)),
        "even_sinks": nrm(ks[7], (N_EVEN, SWA_Q_HEADS), 1.0),
        "even_w_out": nrm(ks[8], (N_EVEN, MIX_WIDTH, D_MODEL), MIX_WIDTH ** -0.5),
        "odd_w_in": nrm(ks[9], (N_ODD, D_MODEL, 2 * LRU_WIDTH), D_MODEL ** -0.5),
        "odd_conv_w": nrm(ks[10], (N_ODD, CONV_WIDTH, LRU_WIDTH), CONV_WIDTH ** -0.5),
        "odd_conv_b": nrm(ks[11], (N_ODD, LRU_WIDTH), 0.02),
        "odd_gate_w": nrm(ks[12], (N_ODD, 2, LRU_BLOCKS, LRU_BLOCK_DIM, LRU_BLOCK_DIM), LRU_BLOCK_DIM ** -0.5),
        "odd_gate_b": nrm(ks[13], (N_ODD, 2, LRU_BLOCKS, LRU_BLOCK_DIM), 0.02),
        "odd_lru_lambda": jnp.log(sig) - jnp.log1p(-sig),
        "odd_w_out": nrm(ks[15], (N_ODD, LRU_WIDTH, D_MODEL), LRU_WIDTH ** -0.5),
        "pre_mix_g": gain(ks[16], (DEPTH, D_MODEL)),
        "post_mix_g": gain(ks[17], (DEPTH, D_MODEL)),
        "pre_mlp_g": gain(ks[18], (DEPTH, D_MODEL)),
        "post_mlp_g": gain(ks[19], (DEPTH, D_MODEL)),
        "mlp_w1": nrm(ks[20], (DEPTH, D_MODEL, D_FF), D_MODEL ** -0.5),
        "mlp_w2": nrm(ks[21], (DEPTH, D_FF, D_MODEL), D_FF ** -0.5),
    }

def first_block(x, even_w_in, even_lam_q1, even_lam_k1, even_lam_q2, even_lam_k2,
              even_subln_g, even_sinks, even_w_out, odd_w_in, odd_conv_w, odd_conv_b,
              odd_gate_w, odd_gate_b, odd_lru_lambda, odd_w_out, pre_mix_g, post_mix_g,
              pre_mlp_g, post_mlp_g, mlp_w1, mlp_w2):
    for layer in range(DEPTH):
        h = rmsnorm(x, pre_mix_g[layer])
        if layer % 2 == 0:
            e = layer // 2
            lambda_init = 0.8 - 0.6 * math.exp(-0.3 * layer)
            mix = even_mixer(h, even_w_in[e], even_lam_q1[e], even_lam_k1[e],
                             even_lam_q2[e], even_lam_k2[e], even_subln_g[e],
                             even_sinks[e], even_w_out[e], lambda_init)
        else:
            o = layer // 2
            mix = rglru_mixer(h, odd_w_in[o], odd_conv_w[o], odd_conv_b[o],
                              odd_gate_w[o], odd_gate_b[o], odd_lru_lambda[o], odd_w_out[o])
        x = x + rmsnorm(mix, post_mix_g[layer])
        f = sq_relu_mlp(rmsnorm(x, pre_mlp_g[layer]), mlp_w1[layer], mlp_w2[layer])
        x = x + rmsnorm(f, post_mlp_g[layer])
    return x


DEPTH_2 = 1

ATTN_WIDTH = D_MODEL // 2
SSM_WIDTH = D_MODEL - ATTN_WIDTH
HEAD_DIM_2 = 128
N_HEADS = ATTN_WIDTH // HEAD_DIM_2
ROT_DIM = HEAD_DIM_2 // 4
ROPE_THETA = 500000.0
DILATED_PATTERNS = ((128, 1), (512, 4), (2048, 16))
ATT_BLOCK = 128
SSM_GROUP = 16
N_SSM_GROUPS = SSM_WIDTH // SSM_GROUP
SSM_STATE = 64
DT_MIN = 1e-3
DT_MAX = 1e-1
D_FF_2 = -(-8 * D_MODEL // (3 * 256)) * 256
IN_WIDTH = 3 * ATTN_WIDTH + SSM_WIDTH
RMS_EPS = 1e-6


def _rmsnorm(t, g):
    tf = t.astype(jnp.float32)
    tf = tf * lax.rsqrt(jnp.mean(tf * tf, axis=-1, keepdims=True) + RMS_EPS)
    return (tf * g.astype(jnp.float32)).astype(t.dtype)

def _rotary_tables(seq):
    pos = jnp.arange(seq, dtype=jnp.float32)
    inv_freq = ROPE_THETA ** (-jnp.arange(0, ROT_DIM, 2, dtype=jnp.float32) / ROT_DIM)
    ang = pos[:, None] * inv_freq[None, :]
    return jnp.cos(ang)[None, :, None, :], jnp.sin(ang)[None, :, None, :]

def _apply_partial_rope(t, cos, sin):
    rot, rest = t[..., :ROT_DIM], t[..., ROT_DIM:]
    x1, x2 = rot[..., :ROT_DIM // 2], rot[..., ROT_DIM // 2:]
    return jnp.concatenate([x1 * cos - x2 * sin, x2 * cos + x1 * sin, rest], axis=-1)

def _dilated_band_attention(q, k, v, dilation, band):
    b, s, h, hd = q.shape
    L = s // dilation
    nb = -(-L // ATT_BLOCK)
    pad = nb * ATT_BLOCK - L

    def to_lattice(t):
        return t.reshape(b, L, dilation, h, hd)

    ql = jnp.pad(to_lattice(q), ((0, 0), (0, pad), (0, 0), (0, 0), (0, 0)))
    kl = jnp.pad(to_lattice(k), ((0, 0), (ATT_BLOCK, pad), (0, 0), (0, 0), (0, 0)))
    vl = jnp.pad(to_lattice(v), ((0, 0), (ATT_BLOCK, pad), (0, 0), (0, 0), (0, 0)))
    qb = ql.reshape(b, nb, ATT_BLOCK, dilation, h, hd)
    kb = kl.reshape(b, nb + 1, ATT_BLOCK, dilation, h, hd)
    vb = vl.reshape(b, nb + 1, ATT_BLOCK, dilation, h, hd)
    kw = jnp.concatenate([kb[:, :-1], kb[:, 1:]], axis=2)
    vw = jnp.concatenate([vb[:, :-1], vb[:, 1:]], axis=2)

    scores = jnp.einsum('bnqrhd,bnkrhd->bnrhqk', qb, kw)
    qi = jnp.arange(ATT_BLOCK)[:, None]
    kj = jnp.arange(2 * ATT_BLOCK)[None, :]
    dist = qi - kj + ATT_BLOCK
    key_idx = jnp.arange(nb)[:, None, None] * ATT_BLOCK + kj[None] - ATT_BLOCK
    valid = (dist >= 0) & (dist <= band) & (key_idx >= 0)
    scores = jnp.where(valid[None, :, None, None], scores, -jnp.inf)
    m = jnp.max(scores, axis=-1)
    p = jnp.exp(scores - m[..., None])
    l = jnp.sum(p, axis=-1)
    o = jnp.einsum('bnrhqk,bnkrhd->bnqrhd', p, vw)

    def from_lattice(t):
        tail = t.shape[5:]
        t = t.reshape((b, nb * ATT_BLOCK, dilation, h) + tail)[:, :L]
        return t.reshape((b, s, h) + tail)

    m = jnp.moveaxis(m, -1, 2)
    l = jnp.moveaxis(l, -1, 2)
    return from_lattice(o), from_lattice(m), from_lattice(l)

def _dilated_attention_mixer(q, k, v, cos, sin):
    b, s, _ = q.shape
    split = lambda t: t.astype(jnp.float32).reshape(b, s, N_HEADS, HEAD_DIM_2)
    qh = _apply_partial_rope(split(q), cos, sin) * (HEAD_DIM_2 ** -0.5)
    kh = _apply_partial_rope(split(k), cos, sin)
    vh = split(v)
    parts = [_dilated_band_attention(qh, kh, vh, dil, win // dil) for win, dil in DILATED_PATTERNS]
    m_all = jnp.max(jnp.stack([m for _, m, _ in parts], axis=0), axis=0)
    num = 0.0
    den = 0.0
    for o_i, m_i, l_i in parts:
        w_i = jnp.exp(m_i - m_all)
        num = num + w_i[..., None] * o_i
        den = den + w_i * l_i
    out = num / den[..., None]
    return out.reshape(b, s, ATTN_WIDTH).astype(q.dtype)

def _s5_mixer(u, a_re, a_im, log_dt, b_re, b_im, c_re, c_im, d_skip, w_glu, b_glu):
    bsz, s, _ = u.shape
    f32 = jnp.float32
    uf = u.astype(f32).reshape(bsz, s, N_SSM_GROUPS, SSM_GROUP)
    lam = lax.complex(a_re.astype(f32), a_im.astype(f32))
    dt = jnp.exp(log_dt.astype(f32))[:, None]
    a_bar = jnp.exp(lam * dt)
    b_mat = lax.complex(b_re.astype(f32), b_im.astype(f32))
    b_bar = ((a_bar - 1.0) / lam)[..., None] * b_mat
    bu = jnp.einsum('bsgp,gnp->bsgn', uf.astype(jnp.complex64), b_bar)
    a_seq = jnp.broadcast_to(a_bar, bu.shape)

    def combine(e1, e2):
        a1, x1 = e1
        a2, x2 = e2
        return a1 * a2, a2 * x1 + x2

    _, states = lax.associative_scan(combine, (a_seq, bu), axis=1)
    c_mat = lax.complex(c_re.astype(f32), c_im.astype(f32))
    y = jnp.einsum('bsgn,gpn->bsgp', states, c_mat).real + d_skip.astype(f32) * uf
    y = jax.nn.gelu(y.reshape(bsz, s, SSM_WIDTH))
    gate = jax.nn.sigmoid(y @ w_glu.astype(f32) + b_glu.astype(f32))
    return (y * gate).astype(u.dtype)

def second_inputs(seed: int = 0) -> dict:
    key = jax.random.key(seed)
    ks = jax.random.split(key, 20)
    f32 = jnp.float32
    nrm = lambda k, shape, scale: jax.random.normal(k, shape, f32) * scale
    x = jax.random.normal(ks[0], (BATCH, SEQ, D_MODEL), f32)
    norm1_g = 1.0 + nrm(ks[1], (DEPTH_2, D_MODEL), 0.02)
    w_in = nrm(ks[2], (DEPTH_2, D_MODEL, IN_WIDTH), D_MODEL ** -0.5)
    a_re = -0.5 + nrm(ks[3], (DEPTH_2, N_SSM_GROUPS, SSM_STATE), 0.01)
    a_im = (math.pi * jnp.arange(SSM_STATE, dtype=f32))[None, None, :] + nrm(ks[4], (DEPTH_2, N_SSM_GROUPS, SSM_STATE), 0.01)
    log_dt = jax.random.uniform(ks[5], (DEPTH_2, N_SSM_GROUPS), f32, math.log(DT_MIN), math.log(DT_MAX))
    b_re = nrm(ks[6], (DEPTH_2, N_SSM_GROUPS, SSM_STATE, SSM_GROUP), (2 * SSM_GROUP) ** -0.5)
    b_im = nrm(ks[7], (DEPTH_2, N_SSM_GROUPS, SSM_STATE, SSM_GROUP), (2 * SSM_GROUP) ** -0.5)
    c_re = nrm(ks[8], (DEPTH_2, N_SSM_GROUPS, SSM_GROUP, SSM_STATE), (2 * SSM_STATE) ** -0.5)
    c_im = nrm(ks[9], (DEPTH_2, N_SSM_GROUPS, SSM_GROUP, SSM_STATE), (2 * SSM_STATE) ** -0.5)
    d_skip = nrm(ks[10], (DEPTH_2, N_SSM_GROUPS, SSM_GROUP), 1.0)
    w_glu = nrm(ks[11], (DEPTH_2, SSM_WIDTH, SSM_WIDTH), SSM_WIDTH ** -0.5)
    b_glu = nrm(ks[12], (DEPTH_2, SSM_WIDTH), 0.02)
    w_out = nrm(ks[13], (DEPTH_2, ATTN_WIDTH + SSM_WIDTH, D_MODEL), (ATTN_WIDTH + SSM_WIDTH) ** -0.5)
    norm2_g = 1.0 + nrm(ks[14], (DEPTH_2, D_MODEL), 0.02)
    w_gate = nrm(ks[15], (DEPTH_2, D_MODEL, D_FF_2), D_MODEL ** -0.5)
    w_up = nrm(ks[16], (DEPTH_2, D_MODEL, D_FF_2), D_MODEL ** -0.5)
    w_down = nrm(ks[17], (DEPTH_2, D_FF_2, D_MODEL), D_FF_2 ** -0.5)
    final_g = 1.0 + nrm(ks[18], (D_MODEL,), 0.02)
    return {"x": x, "norm1_g": norm1_g, "w_in": w_in, "a_re": a_re, "a_im": a_im,
            "log_dt": log_dt, "b_re": b_re, "b_im": b_im, "c_re": c_re, "c_im": c_im,
            "d_skip": d_skip, "w_glu": w_glu, "b_glu": b_glu, "w_out": w_out,
            "norm2_g": norm2_g, "w_gate": w_gate, "w_up": w_up, "w_down": w_down,
            "final_g": final_g}

def second_block(x, norm1_g, w_in, a_re, a_im, log_dt, b_re, b_im, c_re, c_im, d_skip,
              w_glu, b_glu, w_out, norm2_g, w_gate, w_up, w_down, final_g):
    _, s, _ = x.shape
    cos, sin = _rotary_tables(s)
    h = x
    for layer in range(DEPTH_2):
        hn = _rmsnorm(h, norm1_g[layer])
        proj = hn @ w_in[layer]
        q, k, v, u = jnp.split(proj, [ATTN_WIDTH, 2 * ATTN_WIDTH, 3 * ATTN_WIDTH], axis=-1)
        attn_out = _dilated_attention_mixer(q, k, v, cos, sin)
        ssm_out = _s5_mixer(u, a_re[layer], a_im[layer], log_dt[layer], b_re[layer],
                            b_im[layer], c_re[layer], c_im[layer], d_skip[layer],
                            w_glu[layer], b_glu[layer])
        h = h + jnp.concatenate([attn_out, ssm_out], axis=-1) @ w_out[layer]
        hn = _rmsnorm(h, norm2_g[layer])
        h = h + (jax.nn.silu(hn @ w_gate[layer]) * (hn @ w_up[layer])) @ w_down[layer]
    return _rmsnorm(h, final_g)


def setup_inputs(seed=0):
    out = dict(first_inputs(seed))
    for name, value in second_inputs(seed + 1).items():
        if name != "x":
            out[name + "_2"] = value
    return out


def reference(
    x, even_w_in, even_lam_q1, even_lam_k1, even_lam_q2, even_lam_k2, even_subln_g, even_sinks,
    even_w_out, odd_w_in, odd_conv_w, odd_conv_b, odd_gate_w, odd_gate_b, odd_lru_lambda,
    odd_w_out, pre_mix_g, post_mix_g, pre_mlp_g, post_mlp_g, mlp_w1, mlp_w2, norm1_g_2, w_in_2,
    a_re_2, a_im_2, log_dt_2, b_re_2, b_im_2, c_re_2, c_im_2, d_skip_2, w_glu_2, b_glu_2,
    w_out_2, norm2_g_2, w_gate_2, w_up_2, w_down_2, final_g_2,
):
    x = first_block(
        x, even_w_in, even_lam_q1, even_lam_k1, even_lam_q2, even_lam_k2, even_subln_g,
        even_sinks, even_w_out, odd_w_in, odd_conv_w, odd_conv_b, odd_gate_w, odd_gate_b,
        odd_lru_lambda, odd_w_out, pre_mix_g, post_mix_g, pre_mlp_g, post_mlp_g, mlp_w1, mlp_w2,
    )
    return second_block(
        x, norm1_g_2, w_in_2, a_re_2, a_im_2, log_dt_2, b_re_2, b_im_2, c_re_2, c_im_2,
        d_skip_2, w_glu_2, b_glu_2, w_out_2, norm2_g_2, w_gate_2, w_up_2, w_down_2, final_g_2,
    )


_drawn_inputs = setup_inputs


def setup_inputs(seed=0):
    import zlib

    import numpy as np

    out = dict(_drawn_inputs(seed))
    spreads = {}
    factors = {'even_sinks': 3.428,
     'odd_gate_b': 8.0,
     'norm1_g_2': 8.0,
     'a_re_2': 64.0,
     'a_im_2': 57.04,
     'log_dt_2': 64.0,
     'b_re_2': 64.0,
     'b_im_2': 64.0,
     'c_re_2': 64.0,
     'c_im_2': 64.0,
     'b_glu_2': 28.19,
     'norm2_g_2': 7.657,
     'final_g_2': 7.766}
    for name, (base, spread) in spreads.items():
        noise = np.random.default_rng([zlib.crc32(name.encode()), seed]).standard_normal(out[name].shape)
        drawn = base * np.exp(spread * noise) if base else spread * noise
        out[name] = __import__('jax').numpy.asarray(drawn.astype(out[name].dtype))
    for name, factor in factors.items():
        out[name] = (out[name] * factor).astype(out[name].dtype)
    return out
```

```python
from contextlib import ExitStack, contextmanager
import math

import numpy as np
import concourse.bass as bass
from concourse import mybir

F32 = mybir.dt.float32
F32R = mybir.dt.float32r
ALU = mybir.AluOpType
ACT = mybir.ActivationFunctionType
AX_X = mybir.AxisListType.X

P = 128
SEQ = 256
M = SEQ // P
D = 2048
KT = D // P
CH = 512
KU = 4
NCH = D // CH
RAW_SLOTS, RING = 4, 2
EPS = 1e-6
LAMBDA_INIT = 0.8 - 0.6 * math.exp(0.0)
MASKED = -1e30
SSM_TILES = 32
GELU_1 = 2.0 * math.sqrt(2.0 / math.pi)
GELU_3 = GELU_1 * 0.044715

C_PRE_MIX, C_PRE_MLP, C_CONV_W = 0, 32, 64
C_CONV_B, C_GATE_B, C_LAM, C_NORM1, C_NORM2, C_BGLU, C_DSKIP = 128, 144, 176, 192, 208, 224, 232
C_ARE, C_AIM, C_LDT = 256, 288, 320
G_POST_MIX, G_POST_MLP, G_FINAL, G_ROWS = 0, 8, 16, 20
K_IDENT, K_MASK, K_SMALL = 0, 128, 128 + 4 * SEQ
K_COS, K_SIN, K_BM, K_CM = 0, 32, 64, 96
N_SMALL = 104
MASK_CAUSAL, MASK_WINDOW, MASK_DILATED, COUNT_DILATED = range(4)


SEMAPHORES = (
    "acc_zero act_step b_copied b_padded b_turned biased block_done bu_ready bu_used c_copied "
    "c_loaded c_lru_ready c_padded c_turned col_ready conv_done dve_step eps_ready exp_ready "
    "gain_ready gelu_a gelu_b h_ready hi_ready lam_abs lam_dot lam_exp lo_ready loaded lru_exp "
    "lru_ratio lru_root lru_z masks_loaded mix_ready mixed mixed_out out_ready params_loaded "
    "params_turned pool_step probs_copied probs_ready probs_turned psum_free_act psum_free_dve raw0 "
    "raw1 raw2 raw3 root_ready rot_ready rot_used rows_ready rs_ready s5_asked s5_given s5_ready "
    "s5_recip squared scores_ready split_done split_hi staged stored tot_ready turned "
    "unit_used x_ready y_done y_gelu y_read y_ready "
).split()
N_LOADS, N_PARAM_LOADS = 15, 14


class Tally:

    def __init__(self):
        self.n, self.turn, self.stride, self.evacuated_by = {}, None, {}, None

    def add(self, name, k=1):
        self.n[name] = self.n.get(name, 0) + k
        return self.at(name)

    def any(self, name, back=0):
        return self.n.get(name, 0) > back

    def at(self, name, back=0):
        value = self.n.get(name, 0) - back
        return value if self.turn is None or not self.stride.get(name) else self.turn * self.stride[name] + value

    @contextmanager
    def loop(self, turn, trips, **stride):
        before = dict(self.n)
        self.turn, self.stride = turn, stride
        yield
        self.turn, self.stride = None, {}
        for name in self.n:
            grown = self.n[name] - before.get(name, 0)
            assert grown == stride.get(name, 0), (name, grown, stride.get(name, 0))
            self.n[name] += grown * (trips - 1)


def build(nc, i, out):
    x_in = i["x"].rearrange("a (m p) d -> p (a m) d", p=P)
    out_v = out.rearrange("a (m p) d -> p (a m) d", p=P)

    def rows(ap):
        return ap.rearrange("(t p) n -> p t n", p=P)

    w_even_in, w_even_out = rows(i["even_w_in"][0]), rows(i["even_w_out"][0])
    w_odd_in, w_odd_out = rows(i["odd_w_in"][0]), rows(i["odd_w_out"][0])
    w_mlp1 = [rows(i["mlp_w1"][l]) for l in range(2)]
    w_mlp2 = [rows(i["mlp_w2"][l]) for l in range(2)]
    w_gates = i["odd_gate_w"][0].rearrange("g n (t p) e -> p g (n t) e", p=P)
    w_in2, w_glu, w_out2 = rows(i["w_in_2"][0]), rows(i["w_glu_2"][0]), rows(i["w_out_2"][0])
    w_gate2, w_up2, w_down2 = rows(i["w_gate_2"][0]), rows(i["w_up_2"][0]), rows(i["w_down_2"][0])

    with ExitStack() as ctx:
        base = 18688
        K = 1024

        def at(name, offset, shape, dt=F32):
            return nc.alloc_sbuf_tensor_at(name, [P] + shape, dt, offset=base + int(offset * K))

        raw = at("raw", 0, [RAW_SLOTS, KU * CH])
        hi = at("hi", 32, [RING, KU * CH], F32R)
        lo = at("lo", 48, [RING, KU * CH], F32R)
        xt_h, xt_l = at("xt_h", 64, [KT, SEQ], F32R), at("xt_l", 80, [KT, SEQ], F32R)
        ht_h, ht_l = at("ht_h", 96, [KT, SEQ], F32R), at("ht_l", 112, [KT, SEQ], F32R)
        xres, acc = at("xres", 128, [M, D]), at("acc", 144, [M, D])
        stg, tmp = at("stg", 160, [M, CH]), at("tmp", 164, [M, CH])
        col = at("col", 168, [3 * P])
        ident = at("ident", 169.5, [P])
        grows = at("grows", 170, [CH])
        stat = at("stat", 172, [256])
        lamv = at("lamv", 173, [4, 64])
        subg = at("subg", 174, [P])
        sink = at("sink", 174.5, [16])
        small = at("small", 174.5625, [N_SMALL])
        mask = at("mask", 175, [2, SEQ])
        scores = at("scores", 177, [2, 2, SEQ])
        probs = at("probs", 181, [2, 2, SEQ])
        probs_t = at("probs_t", 185, [2, 4, P])
        v_swa, k_swa = at("v_swa", 189, [M, P]), at("k_swa", 190, [2, SEQ])
        prow = at("prow", 190, [3, P])
        qk0, v0 = at("qk0", 96, [24, SEQ]), at("v0", 120, [M, 1024])
        gate_r, gate_i, y_br = at("gate_r", 64, [KT, SEQ]), at("gate_i", 80, [KT, SEQ]), at("y_br", 144, [KT, SEQ])
        tmp_4 = at("tmp_4", 164, [4, SEQ])
        lru_a, lru_t, lru_d = (at(n, o, [4, SEQ]) for n, o in (("lru_a", 177), ("lru_t", 181), ("lru_d", 185)))
        conv_o = at("conv_o", 181, [4, SEQ])
        c_lru = at("c_lru", 189, [16])
        qk2, v2, u2 = at("qk2", 96, [16, SEQ]), at("v2", 112, [M, 1024]), at("u2", 120, [8, SEQ])
        pw = at("pw", 192, [2, 2, SSM_TILES, 16])
        b_bar = at("b_bar", 200, [2, SSM_TILES, 16])
        b_pad, b_t, c_pad = at("b_pad", 177, [2, 4, P]), at("b_t", 181, [2, 4, P]), at("c_pad", 185, [2, 4, P])
        c_t = at("c_t", 160, [2, 4, P])
        h_re, h_im, t_1, t_2 = (at(n, 96 + 4 * j, [4, SEQ]) for j, n in enumerate(("h_re", "h_im", "t_1", "t_2")))
        rots = [at("rot0", 112, [2, 4, SEQ]), at("rot1", 72, [2, 4, SEQ])]
        rot_t = at("rot_t", 88, [2, 4, SEQ])
        c_all = at("c_all", 80, [2, 8, 64])
        glu_z = at("glu_z", 96, [8, SEQ])
        log_dt = at("log_dt", 191.5, [2])
        s5 = at("s5", 177, [24, SSM_TILES])
        b_raw = at("b_raw", 181, [2, SSM_TILES, 16])
        s5_t = at("s5_t", 185, [2, SSM_TILES, 16])
        decay = at("decay", 204, [SSM_TILES])
        assert base + int(205.5 * K) <= 229344

        pair = [ctx.enter_context(nc.psum_tensor(f"pair{k}", [P, M, CH], F32)) for k in range(2)]
        turn_ps = ctx.enter_context(nc.psum_tensor("turn_ps", [P, 4, SEQ], F32))
        misc_ps = ctx.enter_context(nc.psum_tensor("misc_ps", [P, 2, CH], F32))

        score_ps = misc_ps, pair[1]
        turn_all = turn_ps[:].rearrange("p a (b c) -> p (a b) c", c=P).rearrange("p (r j) c -> p r j c", r=2)

        sems = {name: ctx.enter_context(nc.semaphore(name)) for name in SEMAPHORES}

        SS, SSX, TOT, ROOT, RPOST, RS, LAM = 0, 8, 16, 18, 20, 22, 24
        LAMS, MAXN, SUMS, RSUM, ESINK, SUB = 26, 32, 36, 40, 48, 64
        eps_col, nsink, unused = stat[:, 127:128], stat[:, 128:144], stat[:, 144:145]

        def st(a, n=1):
            return stat[:, a:a + n]

        def attention_items(kind):
            pairs = 4 if kind == "dilated" else 8
            return ([(pr, m) for pr in range(pairs) for m in range(M)], 1 if kind == "diff" else 2,
                    64 if kind == "window" else P)

        class Program:

            TURNED = ("copy", "relu2", "gelu", "rope", "up", "kv")
            BY = {"kv": "psum_free_act", "copy": "psum_free_act", "relu2": "psum_free_act", "gelu": "psum_free_act",
                  "rope": "psum_free_act", "tokens": "psum_free_act", "silu": "psum_free_act",
                  "up": "psum_free_dve", "add": "psum_free_dve", "set": "psum_free_dve"}
            STAGED = {"kv": "psum_free_act", "copy": "psum_free_act", "up": "psum_free_dve",
                      "relu2": "staged", "gelu": "staged", "rope": "staged"}

            def __init__(self, eng):
                self.eng, self.T = eng, Tally()

            @contextmanager
            def loop(self, trips, **stride):
                with self.eng.Fori(0, trips) as turn:
                    with self.T.loop(turn, trips, **stride):
                        yield turn

            def nothing(self, *_, **__):
                pass

            setup = chunk = drain = attention = gates = s5_params = dilated_masks = s5 = glu = final = nothing

            def take_pair(self):
                k = self.T.n.get("chunk", 0) % 2
                self.T.add("chunk")
                return pair[k]

        class Sync(Program):
            def setup(self):
                sp = self.eng
                for dst, src in (
                    (ident[:], i["consts"][:, K_IDENT:K_IDENT + P]),
                    (prow[0:32, 0], i["pre_mix_g"].rearrange("l (t p) -> (l t) p", p=P)),
                    (prow[32:64, 0], i["pre_mlp_g"].rearrange("l (t p) -> (l t) p", p=P)),
                    (prow[64:128, 0], i["odd_conv_w"][0].rearrange("j (t p) -> (j t) p", p=P)),
                    (prow[0:16, 1], i["odd_conv_b"][0].rearrange("(t p) -> t p", p=P)),
                    (prow[16:48, 1], i["odd_gate_b"][0].rearrange("g n (t p) -> (g n t) p", p=P)),
                    (prow[48:64, 1], i["odd_lru_lambda"][0].rearrange("(t p) -> t p", p=P)),
                    (prow[64:80, 1], i["norm1_g_2"][0].rearrange("(t p) -> t p", p=P)),
                    (prow[80:96, 1], i["norm2_g_2"][0].rearrange("(t p) -> t p", p=P)),
                    (prow[96:104, 1], i["b_glu_2"][0].rearrange("(t p) -> t p", p=P)),
                    (prow[104:112, 1], i["d_skip_2"][0].rearrange("(t g) q -> t (g q)", g=8)),
                    (prow[0:32, 2], i["a_re_2"][0].rearrange("(t g) n -> t (g n)", g=2)),
                    (prow[32:64, 2], i["a_im_2"][0].rearrange("(t g) n -> t (g n)", g=2)),
                    (log_dt[64:96], i["log_dt_2"][0].rearrange("(t g) -> t g", g=2)),
                    (xres[:], x_in),
                ):
                    sp.dma_start(dst, src).then_inc(sems["loaded"], 16)
                for k in range(RAW_SLOTS):
                    self.unit(w_even_in[:, KU * k:KU * k + KU, 0:CH])
                for dst, src in (
                    (grows[0:8], i["post_mix_g"].rearrange("l (c n) -> (l c) n", n=CH)),
                    (grows[8:16], i["post_mlp_g"].rearrange("l (c n) -> (l c) n", n=CH)),
                    (grows[16:20], i["final_g_2"].rearrange("(c n) -> c n", n=CH)),
                    (mask[:, 0], i["consts"][:, K_MASK:K_MASK + SEQ]),
                    (mask[:, 1], i["consts"][:, K_MASK + SEQ:K_MASK + 2 * SEQ]),
                    (small[:], i["consts"][:, K_SMALL:K_SMALL + N_SMALL]),
                    (subg[:], i["even_subln_g"].partition_broadcast(P)),
                    (sink[:], i["even_sinks"].partition_broadcast(P)),
                    (lamv[:, 0], i["even_lam_q1"].partition_broadcast(P)),
                    (lamv[:, 1], i["even_lam_k1"].partition_broadcast(P)),
                    (lamv[:, 2], i["even_lam_q2"].partition_broadcast(P)),
                    (lamv[:, 3], i["even_lam_k2"].partition_broadcast(P)),
                    (b_raw[:, 0], i["b_re_2"][0].rearrange("(t g) n q -> (g n) t q", g=2)),
                    (b_raw[:, 1], i["b_im_2"][0].rearrange("(t g) n q -> (g n) t q", g=2)),
                ):
                    sp.dma_start(dst, src).then_inc(sems["params_loaded"], 16)
                self.preloaded = RAW_SLOTS

            def unit(self, src, width=CH, tiles=KU):
                u = self.T.n.get("unit", 0)
                if self.T.turn is not None or u >= RAW_SLOTS:
                    self.eng.wait_ge(sems["lo_ready"], self.T.at("unit", RAW_SLOTS - 1))
                dst = raw[:, u % RAW_SLOTS, 0:tiles * width].rearrange("p (t n) -> p t n", n=width)
                self.eng.dma_start(dst, src).then_inc(sems[f"raw{u % RAW_SLOTS}"], 16)
                self.T.add("unit")

            def chunk(self, kind, w, units=4, width=CH, order=None, **_):
                src, t0, col0 = w
                cols = slice(col0, col0 + width) if isinstance(col0, int) else bass.ds(col0, width)
                for j in range(units):
                    if self.preloaded:
                        self.preloaded -= 1
                        continue
                    k = KU * (order[j] if order else j)
                    tiles = slice(t0 + k, t0 + k + KU) if isinstance(t0, int) else bass.ds(t0 + k, KU)
                    self.unit(src[:, tiles, cols], width)

            def dilated_masks(self):
                self.eng.wait_ge(sems["mixed_out"], self.T.add("mixed_out", 32))
                for k in range(2):
                    a = K_MASK + (2 + k) * SEQ
                    self.eng.dma_start(mask[:, k], i["consts"][:, a:a + SEQ]).then_inc(sems["masks_loaded"], 16)

            def gates(self):
                for g in range(2):
                    for half in range(2):
                        self.unit(w_gates[:, g, 8 * half:8 * half + 8], 2 * P, 8)

            def s5(self):
                for half in range(2):
                    for k in range(2):
                        self.unit(w_glu[:, KU * k:KU * k + KU, half * CH:half * CH + CH])
                self.eng.wait_ge(sems["unit_used"], self.T.n["unit"] - 4)
                for ri, name in enumerate(("c_re_2", "c_im_2")):
                    self.eng.dma_start(c_all[:, ri], i[name][0].rearrange("(t g) q n -> (g q) t n", g=8)
                                       ).then_inc(sems["c_loaded"], 16)

            def final(self):
                for n in range(NCH):
                    self.eng.wait_ge(sems["out_ready"], self.T.add("out_ready"))
                    self.eng.dma_start(out_v[:, :, n * CH:(n + 1) * CH], acc[:, :, n * CH:(n + 1) * CH]
                                       ).then_inc(sems["stored"], 16)
                self.eng.wait_ge(sems["stored"], 16 * NCH)

        class Scalar(Program):
            def setup(self):
                self.eng.wait_ge(sems["loaded"], 16 * N_LOADS)
                self.eng.wait_ge(sems["eps_ready"], 1)
                self.eng.wait_ge(sems["params_turned"], self.T.add("params_turned"))
                for a, n in ((0, P + 112), (2 * P, 96)):
                    ins = nc.scalar.activation(col[:, a:a + n], misc_ps[:, 0, a:a + n], ACT.Copy)
                ins.then_inc(sems["act_step"], 1)
                self.eng.wait_ge(sems["act_step"], self.T.add("act_step"))
                nc.scalar.activation(s5[:, 0], col[:, C_LDT:C_LDT + 32], ACT.Exp).then_inc(sems["col_ready"], 1)
                self.T.add("col_ready")
                self.conv()

            def conv(self, cols=KU * CH):
                T, u = self.T, self.T.n.get("unit", 0)
                slot, r = u % RAW_SLOTS, u % RING
                self.eng.wait_ge(sems[f"raw{slot}"], T.add(f"raw{slot}", 16))
                if T.turn is not None or u >= RING:
                    self.eng.wait_ge(sems["unit_used"], T.at("unit", RING - 1))
                nc.scalar.activation(hi[:, r, 0:cols], raw[:, slot, 0:cols], ACT.Copy).then_inc(sems["hi_ready"], 1)
                T.add("unit")

            def evac(self, kind, ps, done, dst=None, width=CH):
                T, by = self.T, self.BY[kind]
                if kind == "kv":
                    self.eng.wait_ge(sems["unit_used"], done)
                    self.eng.wait_ge(sems["turned"], T.at("turned"))
                    for m in range(M):
                        for c, to in ((0, stg[:, m, 0:P]), (P, v_swa[:, m])):
                            nc.scalar.activation(to, ps[:, m, c:c + P], ACT.Copy, scale=st(RS + m))
                        for c in range(2):
                            a = nc.scalar.activation(stg[:, m, P + 64 * c:P + 64 * c + 64],
                                                     ps[:, m, 64 - 64 * c:128 - 64 * c], ACT.Copy, scale=st(RS + m))
                    a.then_inc(sems[by], 1)
                    T.add(by)
                elif by == "psum_free_act":
                    self.eng.wait_ge(sems["unit_used"], done)
                    self.eng.wait_ge(sems["turned"], T.at("turned"))
                    if kind == "gelu":
                        self.eng.wait_ge(sems["staged"], T.at("staged"))
                    func = {"relu2": ACT.Relu, "silu": ACT.Silu}.get(kind, ACT.Copy)
                    for m in range(M):
                        to = stg[:, m, 0:width] if dst is None else dst[:, m]
                        a = nc.scalar.activation(to, ps[:, m, 0:width], func, scale=st(RS + m))
                    a.then_inc(sems[by], 1)
                    T.add(by)
                else:
                    T.add(by)
                if kind == "gelu":
                    self.eng.wait_ge(sems[by], T.at(by))
                    nc.scalar.activation(tmp[:], stg[:], ACT.Square).then_inc(sems["gelu_a"], 1)
                    T.add("gelu_a")
                    self.eng.wait_ge(sems["gelu_b"], T.add("gelu_b"))
                    nc.scalar.activation(tmp[:], tmp[:], ACT.Sigmoid).then_inc(sems["gelu_a"], 1)
                    T.add("gelu_a")
                if kind in ("gelu", "relu2", "rope"):
                    T.add("staged")

            def square_sums(self, n):
                self.eng.wait_ge(sems["psum_free_dve"], self.T.at("psum_free_dve"))
                self.eng.wait_ge(sems["squared"], self.T.at("squared"))
                for m in range(M):
                    a = nc.scalar.activation(tmp[:, m], acc[:, m, n * CH:(n + 1) * CH], ACT.Square,
                                             accum_out=st(SS + 4 * m + n))
                a.then_inc(sems["squared"], 1)
                self.T.add("squared")

            def split(self, to):
                T = self.T
                T.add("turned")
                if to[0] == "conv":
                    self.eng.wait_ge(sems["conv_done"], T.add("conv_done"))
                    nc.scalar.activation(ht_h[:, to[1]:to[1] + 4], conv_o[:], ACT.Copy).then_inc(sems["split_hi"], 1)
                    T.add("split_hi")
                elif to[0] is not None:
                    self.eng.wait_ge(sems["turned"], T.at("turned"))
                    nc.scalar.activation(to[0], turn_ps[:], ACT.Copy).then_inc(sems["split_hi"], 1)
                    T.add("split_hi")
                T.add("split_done")

            def chunk(self, kind, w, units=4, width=CH, prev=None, lead=None, to=None, dst=None, n=0, next_cols=KU * CH,
                      ss=True, **_):
                T, ps = self.T, self.take_pair()
                done = T.at("unit", 1)
                if lead:
                    self.lead(lead, units)
                else:
                    self.conv(KU * width)
                    if prev:
                        self.evac(prev[0], prev[1], done, width=prev[3])
                    for _j in range(2, units):
                        self.conv(KU * width)
                    if prev:
                        self.split(prev[2])
                if next_cols:
                    self.conv(next_cols)
                if kind in self.TURNED:
                    return kind, ps, to, width
                self.evac(kind, ps, T.at("unit", 1 if next_cols else 0), dst, width)
                if kind in ("add", "set") and ss:
                    self.square_sums(n)

            def drain(self, prev):
                self.evac(prev[0], prev[1], self.T.at("unit", 1), width=prev[3])
                self.split(prev[2])

            def lead(self, lead, units):
                kind = lead[0]
                if kind == "post":
                    self.root(D)
                for n in range(4):
                    if n < lead[3]:
                        self.part(lead, n)
                    if 1 <= n and n < units:
                        self.conv()
                if kind in ("first", "post", "plain"):
                    self.root(D)
                    self.eng.wait_ge(sems["rs_ready"], self.T.add("rs_ready"))

            def root(self, width):
                self.eng.wait_ge(sems["tot_ready"], self.T.add("tot_ready"))
                ins = nc.scalar.activation(st(ROOT, M), st(TOT, M), ACT.Sqrt, scale=1.0 / width, bias=eps_col)
                ins.then_inc(sems["root_ready"], 1)
                self.T.add("root_ready")

            def part(self, lead, n):
                kind, _, c0, _, th, _ = lead
                if kind == "lru":
                    return self.lru_part(n)
                T = self.T
                if kind in ("post", "plain"):
                    self.eng.wait_ge(sems["x_ready"], T.add("x_ready"))
                if kind in ("first", "post", "plain"):
                    if T.any("squared"):
                        self.eng.wait_ge(sems["squared"], T.at("squared"))
                    for m in range(M):
                        a = nc.scalar.activation(tmp[:, m], xres[:, m, n * CH:(n + 1) * CH], ACT.Square,
                                                 accum_out=st(SSX + 4 * m + n))
                    a.then_inc(sems["squared"], 1)
                    T.add("squared")
                self.eng.wait_ge(sems["turned"], T.add("turned"))
                src = self.part_psum(n)
                if c0 is None:
                    a = nc.scalar.activation(th[:, 4 * n:4 * n + 4], src, ACT.Copy)
                else:
                    for k in range(4):
                        c = c0 + 4 * n + k
                        a = nc.scalar.activation(th[:, 4 * n + k], src[:, k], ACT.Copy, scale=col[:, c:c + 1])
                a.then_inc(sems["split_hi"], 1)
                T.add("split_hi")
                T.add("split_done")

            def part_psum(self, n):
                if n % 2 == 0:
                    return turn_ps[:]
                return pair[self.T.n["chunk"] % 2][:].rearrange("p m (k s) -> p (m k) s", s=SEQ)

            def lru_part(self, q):
                T, tiles = self.T, slice(4 * q, 4 * q + 4)
                if q == 0:
                    self.eng.wait_ge(sems["lam_abs"], T.add("lam_abs"))
                    nc.scalar.activation(tmp[:, 0, 16:32], tmp[:, 0, 0:16], ACT.Exp).then_inc(sems["lam_exp"], 1)
                    T.add("lam_exp")
                    self.eng.wait_ge(sems["c_lru_ready"], T.add("c_lru_ready"))
                self.eng.wait_ge(sems["split_done"], T.at("split_done"))
                for k in range(4):
                    t = 4 * q + k
                    nc.scalar.activation(lru_a[:, k], gate_r[:, t], ACT.Exp, scale=c_lru[:, t:t + 1])
                    a = nc.scalar.activation(lru_t[:, k], gate_r[:, t], ACT.Tanh, scale=c_lru[:, t:t + 1])
                a.then_inc(sems["lru_exp"], 1)
                T.add("lru_exp")
                self.eng.wait_ge(sems["lru_ratio"], T.add("lru_ratio"))
                nc.scalar.activation(lru_t[:], lru_t[:], ACT.Sqrt).then_inc(sems["lru_root"], 1)
                T.add("lru_root")
                self.eng.wait_ge(sems["lru_z"], T.add("lru_z"))
                nc.scalar.activation(xt_h[:, tiles], tmp_4[:], ACT.Copy).then_inc(sems["split_hi"], 1)
                T.add("split_hi")
                T.add("split_done")

            def gates(self):
                T = self.T
                for j in range(4):
                    if j < 3:
                        self.conv()
                    for b in range(2):
                        ps, g = self.take_pair(), j // 2
                        if b == 0:
                            self.eng.wait_ge(sems["block_done"], T.add("block_done"))
                        else:
                            self.eng.wait_ge(sems["unit_used"], T.n["unit"] - (1 if j < 3 else 0))
                        for k in range(4):
                            t = 8 * (j % 2) + 4 * b + k
                            c = C_GATE_B + 16 * g + t
                            a = nc.scalar.activation((gate_r, gate_i)[g][:, t],
                                                     ps[:, k // 2, (k % 2) * SEQ:(k % 2 + 1) * SEQ], ACT.Sigmoid,
                                                     bias=col[:, c:c + 1])
                        a.then_inc(sems["psum_free_act"], 1)
                        T.add("psum_free_act")
                self.conv()

            def attention(self, kind):
                T = self.T
                items, heads, per = attention_items(kind)
                if kind == "diff":
                    self.eng.wait_ge(sems["lam_dot"], T.add("lam_dot"))
                    nc.scalar.activation(st(LAMS, 2), st(LAMS, 2), ACT.Exp).then_inc(sems["lam_exp"], 1)
                    T.add("lam_exp")

                def out_of_psum(k):
                    pr, m = items[k]
                    self.eng.wait_ge(sems["mixed"], T.add("mixed"))
                    c = pr * P if kind != "dilated" else pr * 2 * P
                    if kind == "diff":
                        a = nc.scalar.activation(acc[:, m, c:c + P], pair[0][:, k % 2, 0:P], ACT.Copy)
                    else:
                        c += 1024 if kind == "window" else 0
                        for s in range(2):
                            a = nc.scalar.activation(acc[:, m, c + s * per:c + (s + 1) * per],
                                                     pair[0][:, k % 2, s * per:(s + 1) * per], ACT.Copy,
                                                     scale=st(RSUM + 2 * (k % 4) + s))
                    a.then_inc(sems["mixed_out"], 1)
                    T.add("mixed_out")

                for k, (pr, m) in enumerate(items):
                    self.eng.wait_ge(sems["biased"], T.add("biased"))
                    keys = (m + 1) * P
                    b, q = k % 2, 2 * (k % 2)
                    for s in range(2):
                        sc = scores[:, b, s, 0:keys]
                        a = nc.scalar.activation(sc, sc, ACT.Exp, bias=st(MAXN + q + s),
                                                 accum_out=st(SUMS + q + s))
                    if kind == "window":
                        for s in range(2):
                            a = nc.scalar.activation(st(ESINK + q + s), sink[:, 2 * pr + s:2 * pr + s + 1], ACT.Exp,
                                                     bias=st(MAXN + q + s))
                    a.then_inc(sems["exp_ready"], 1)
                    T.add("exp_ready")
                    if k >= 2:
                        out_of_psum(k - 2)
                out_of_psum(len(items) - 2)
                out_of_psum(len(items) - 1)
                if kind == "diff":
                    self.eng.wait_ge(sems["tot_ready"], T.add("tot_ready"))
                    ins = nc.scalar.activation(st(SUB, 16), st(SUB, 16), ACT.Sqrt, scale=1.0 / P, bias=eps_col)
                    ins.then_inc(sems["root_ready"], 1)
                    T.add("root_ready")

            def s5_params(self):
                self.eng.wait_ge(sems["s5_asked"], self.T.add("s5_asked"))
                nc.scalar.activation(decay[:], s5[:, 1], ACT.Exp)
                nc.scalar.activation(s5[:, 8], s5[:, 5], ACT.Sin)
                nc.scalar.activation(s5[:, 9], s5[:, 6], ACT.Sin).then_inc(sems["s5_given"], 1)
                self.T.add("s5_given")

            def s5(self):
                T = self.T
                for g in range(8):
                    self.eng.wait_ge(sems["b_turned"], T.add("b_turned"))
                    nc.scalar.activation(b_t[:], turn_all, ACT.Copy).then_inc(sems["b_copied"], 1)
                    T.add("b_copied")
                    self.eng.wait_ge(sems["c_turned"], T.add("c_turned"))
                    nc.scalar.activation(c_t[:, 0], turn_all[:, 0], ACT.Copy)
                    nc.scalar.activation(c_t[:, 1], turn_all[:, 1], ACT.Copy, scale=-1.0).then_inc(sems["c_copied"], 1)
                    T.add("c_copied")
                self.eng.wait_ge(sems["y_done"], T.add("y_done"))
                nc.scalar.activation(glu_z[:], u2[:], ACT.Square).then_inc(sems["gelu_a"], 1)
                T.add("gelu_a")
                self.eng.wait_ge(sems["gelu_b"], T.add("gelu_b"))
                nc.scalar.activation(glu_z[:], glu_z[:], ACT.Sigmoid).then_inc(sems["gelu_a"], 1)
                T.add("gelu_a")
                self.eng.wait_ge(sems["y_gelu"], T.add("y_gelu"))
                nc.scalar.activation(xt_h[:, 0:8], u2[:], ACT.Copy).then_inc(sems["split_hi"], 1)
                T.add("split_hi")
                T.add("split_done")

            def glu(self):
                T = self.T
                for _ in range(3):
                    self.conv()
                for half in range(2):
                    ps = self.take_pair()
                    self.eng.wait_ge(sems["unit_used"], T.at("unit", 2 if half == 0 else 0))
                    flat = ps[:].rearrange("p m (k s) -> p (m k) s", s=SEQ)
                    for e in range(4):
                        c = C_BGLU + 4 * half + e
                        a = nc.scalar.activation(glu_z[:, 4 * half + e], flat[:, e], ACT.Sigmoid, bias=col[:, c:c + 1])
                    a.then_inc(sems["psum_free_act"], 1)
                    T.add("psum_free_act")
                self.conv()
                self.eng.wait_ge(sems["y_gelu"], T.add("y_gelu"))
                nc.scalar.activation(xt_h[:, 8:16], glu_z[:], ACT.Copy).then_inc(sems["split_hi"], 1)
                T.add("split_hi")
                T.add("split_done")

            def final(self):
                for n in range(NCH):
                    self.eng.wait_ge(sems["x_ready"], self.T.add("x_ready"))
                    self.eng.wait_ge(sems["squared"], self.T.at("squared"))
                    for m in range(M):
                        a = nc.scalar.activation(tmp[:, m], xres[:, m, n * CH:(n + 1) * CH], ACT.Square,
                                                 accum_out=st(SSX + 4 * m + n))
                    a.then_inc(sems["squared"], 1)
                    self.T.add("squared")
                self.root(D)

        class Vector(Program):
            def setup(self):
                v = self.eng
                v.wait_ge(sems["loaded"], 16 * N_LOADS)
                for g in range(2):
                    a = nc.vector.tensor_copy(prow[64:96, 2, 64 * g:64 * g + 64],
                                              log_dt[64:96, g:g + 1].to_broadcast([32, 64]))
                a.then_inc(sems["rows_ready"], 1)
                self.T.add("rows_ready")
                nc.vector.memset(eps_col, EPS).then_inc(sems["eps_ready"], 1)
                self.conv()
                self.eng.wait_ge(sems["col_ready"], self.T.add("col_ready"))

            def conv(self, cols=KU * CH):
                T, u = self.T, self.T.n.get("unit", 0)
                slot, r = u % RAW_SLOTS, u % RING
                self.eng.wait_ge(sems["hi_ready"], T.at("unit", -1))
                nc.vector.tensor_tensor(lo[:, r, 0:cols], raw[:, slot, 0:cols], hi[:, r, 0:cols].bitcast(F32),
                                        ALU.subtract).then_inc(sems["lo_ready"], 1)
                T.add("unit")

            def evac(self, kind, ps, done, dst=None, width=CH):
                T, by = self.T, self.BY[kind]
                if by == "psum_free_act":
                    T.add(by)
                    if kind == "relu2":
                        self.eng.wait_ge(sems[by], T.at(by))
                        nc.vector.tensor_tensor(stg[:], stg[:], stg[:], ALU.mult).then_inc(sems["staged"], 1)
                        T.add("staged")
                    elif kind == "gelu":
                        self.eng.wait_ge(sems["gelu_a"], T.add("gelu_a"))
                        ins = nc.vector.tensor_scalar(tmp[:], tmp[:], GELU_3, GELU_1, ALU.mult, ALU.add)
                        ins.then_inc(sems["dve_step"], 1)
                        self.eng.wait_ge(sems["dve_step"], T.add("dve_step"))
                        nc.vector.tensor_tensor(tmp[:], tmp[:], stg[:], ALU.mult).then_inc(sems["gelu_b"], 1)
                        T.add("gelu_b")
                        self.eng.wait_ge(sems["gelu_a"], T.add("gelu_a"))
                        nc.vector.tensor_tensor(stg[:], stg[:], tmp[:], ALU.mult).then_inc(sems["staged"], 1)
                        T.add("staged")
                    elif kind == "rope":
                        self.rope()
                    return
                self.eng.wait_ge(sems["unit_used"], done)
                if kind == "up":
                    self.eng.wait_ge(sems["psum_free_act"], T.at("psum_free_act"))
                if kind == "add":
                    self.eng.wait_ge(sems["acc_zero"], T.at("acc_zero"))
                for m in range(M):
                    if kind == "up":
                        a = nc.vector.scalar_tensor_tensor(stg[:, m], ps[:, m], st(RS + m), stg[:, m],
                                                           ALU.mult, ALU.mult)
                    elif kind == "set":
                        a = nc.vector.tensor_copy(dst[:, m], ps[:, m])
                    else:
                        a = nc.vector.tensor_tensor(dst[:, m], ps[:, m], dst[:, m], ALU.add)
                a.then_inc(sems[by], 1)
                T.add(by)

            def rope(self):
                self.eng.wait_ge(sems["psum_free_act"], self.T.at("psum_free_act"))
                heads = stg[:].rearrange("p m (h d) -> p m h d", d=P)
                x1, x2 = heads[:, :, :, 0:16], heads[:, :, :, 16:32]
                q = tmp[:].rearrange("p m n -> p (m n)")[:, 0:512].rearrange("p (a m h d) -> p a m h d", a=4, m=M, h=4)
                for a, (xx, t) in enumerate(((x1, K_COS), (x2, K_SIN), (x2, K_COS), (x1, K_SIN))):
                    for m in range(M):
                        c = small[:, t + 16 * m:t + 16 * m + 16].unsqueeze(1).to_broadcast([P, 4, 16])
                        ins = nc.vector.tensor_tensor(q[:, a, m], xx[:, m], c, ALU.mult)
                ins.then_inc(sems["dve_step"], 1)
                self.eng.wait_ge(sems["dve_step"], self.T.add("dve_step"))
                for m in range(M):
                    nc.vector.tensor_tensor(x1[:, m], q[:, 0, m], q[:, 1, m], ALU.subtract)
                    ins = nc.vector.tensor_tensor(x2[:, m], q[:, 2, m], q[:, 3, m], ALU.add)
                ins.then_inc(sems["staged"], 1)
                self.T.add("staged")

            def split(self, to):
                T = self.T
                T.add("turned")
                if to[0] == "conv":
                    return self.causal_conv(to[1])
                if to[0] is None:
                    self.eng.wait_ge(sems["turned"], T.at("turned"))
                    a = nc.vector.tensor_copy(to[1], turn_ps[:, 0:to[1].shape[1]])
                else:
                    self.eng.wait_ge(sems["split_hi"], T.add("split_hi"))
                    a = nc.vector.tensor_tensor(to[1], turn_ps[:], to[0].bitcast(F32), ALU.subtract)
                a.then_inc(sems["split_done"], 1)
                T.add("split_done")

            def causal_conv(self, t0):
                T = self.T
                self.eng.wait_ge(sems["turned"], T.at("turned"))

                def w(j, k):
                    c = C_CONV_W + 16 * j + t0 + k
                    return col[:, c:c + 1]

                for k in range(4):
                    a = nc.vector.tensor_scalar(conv_o[:, k], turn_ps[:, k], w(3, k),
                                                col[:, C_CONV_B + t0 + k:C_CONV_B + t0 + k + 1], ALU.mult, ALU.add)
                for j in range(3):
                    a.then_inc(sems["dve_step"], 1)
                    self.eng.wait_ge(sems["dve_step"], T.add("dve_step"))
                    s = 3 - j
                    for k in range(4):
                        a = nc.vector.scalar_tensor_tensor(conv_o[:, k, s:SEQ], turn_ps[:, k, 0:SEQ - s], w(j, k),
                                                           conv_o[:, k, s:SEQ], ALU.mult, ALU.add)
                a.then_inc(sems["conv_done"], 1)
                T.add("conv_done")
                self.eng.wait_ge(sems["split_hi"], T.add("split_hi"))
                nc.vector.tensor_tensor(ht_l[:, t0:t0 + 4], conv_o[:], ht_h[:, t0:t0 + 4].bitcast(F32),
                                        ALU.subtract).then_inc(sems["split_done"], 1)
                T.add("split_done")

            def chunk(self, kind, w, units=4, width=CH, prev=None, lead=None, to=None, dst=None, n=0, next_cols=KU * CH,
                      ss=True, **_):
                T, ps = self.T, self.take_pair()
                done = T.at("unit", 1)
                if lead:
                    if kind in ("relu2", "silu"):
                        T.add("acc_zero")
                    self.lead(lead, units)
                else:
                    self.conv(KU * width)
                    if prev:
                        self.evac(prev[0], prev[1], done, width=prev[3])
                    for _j in range(2, units):
                        self.conv(KU * width)
                    if prev:
                        self.split(prev[2])
                if next_cols:
                    self.conv(next_cols)
                if kind in self.TURNED:
                    return kind, ps, to, width
                self.evac(kind, ps, T.at("unit", 1 if next_cols else 0), dst, width)
                if kind in ("add", "set") and ss:
                    T.add("squared")

            def drain(self, prev):
                self.evac(prev[0], prev[1], self.T.at("unit", 1), width=prev[3])
                self.split(prev[2])

            def lead(self, lead, units):
                kind, parts = lead[0], lead[3]
                if kind == "post":
                    self.eng.wait_ge(sems["squared"], self.T.at("squared"))
                    self.norm_factor(SS, RPOST)
                if kind in ("post", "plain"):
                    self.residual(kind, 0)
                    self.residual(kind, 1)
                    self.lo_part(lead, 0)
                    self.residual(kind, 2)
                    self.lo_part(lead, 1)
                    self.conv()
                    self.residual(kind, 3)
                    self.lo_part(lead, 2)
                    self.conv()
                    self.lo_part(lead, 3)
                    self.conv()
                else:
                    for n in range(4):
                        if n < parts:
                            self.lru_part(n) if kind == "lru" else self.lo_part(lead, n)
                        if 1 <= n < units:
                            self.conv()
                if kind in ("first", "post", "plain"):
                    self.eng.wait_ge(sems["squared"], self.T.add("squared", 4))
                    self.norm_factor(SSX, RS, "rs_ready")

            def norm_factor(self, sums, dst, tell=None):
                T = self.T
                nc.vector.tensor_reduce(st(TOT, M), st(sums, 8).rearrange("p (m n) -> p m n", m=M), AX_X,
                                        ALU.add).then_inc(sems["tot_ready"], 1)
                T.add("tot_ready")
                self.eng.wait_ge(sems["root_ready"], T.add("root_ready"))
                ins = nc.vector.reciprocal(st(dst, M), st(ROOT, M))
                if tell:
                    ins.then_inc(sems[tell], 1)
                    T.add(tell)
                else:
                    ins.then_inc(sems["dve_step"], 1)
                    self.eng.wait_ge(sems["dve_step"], T.add("dve_step"))

            def residual(self, kind, n):
                T, cols = self.T, slice(n * CH, (n + 1) * CH)
                if kind == "post":
                    self.eng.wait_ge(sems["gain_ready"], T.add("gain_ready"))
                    for m in range(M):
                        ins = nc.vector.scalar_tensor_tensor(acc[:, m, cols], acc[:, m, cols], st(RPOST + m),
                                                             misc_ps[:, n % 2], ALU.mult, ALU.mult)
                    ins.then_inc(sems["dve_step"], 1)
                    self.eng.wait_ge(sems["dve_step"], T.add("dve_step"))
                elif n == 0:
                    self.eng.wait_ge(sems["psum_free_dve"], T.at("psum_free_dve"))
                ins = nc.vector.tensor_tensor(xres[:, :, cols], xres[:, :, cols], acc[:, :, cols], ALU.add)
                ins.then_inc(sems["x_ready"], 1)
                T.add("x_ready")

            def lo_part(self, lead, n):
                _, _, c0, _, th, tl = lead
                T, src = self.T, Scalar.part_psum(self, n)
                T.add("turned")
                self.eng.wait_ge(sems["split_hi"], T.add("split_hi"))
                if c0 is None:
                    a = nc.vector.tensor_tensor(tl[:, 4 * n:4 * n + 4], src, th[:, 4 * n:4 * n + 4].bitcast(F32),
                                                ALU.subtract)
                else:
                    for k in range(4):
                        t, c = 4 * n + k, c0 + 4 * n + k
                        a = nc.vector.scalar_tensor_tensor(tl[:, t], src[:, k], col[:, c:c + 1],
                                                           th[:, t].bitcast(F32), ALU.mult, ALU.subtract)
                a.then_inc(sems["split_done"], 1)
                T.add("split_done")

            def lru_constant(self):
                T = self.T
                z = [tmp[:, 0, 16 * k:16 * k + 16] for k in range(8)]
                lam = col[:, C_LAM:C_LAM + 16]
                self.eng.wait_ge(sems["split_done"], T.at("split_done"))
                nc.vector.tensor_scalar(z[2], lam, -1.0, None, ALU.mult).then_inc(sems["dve_step"], 1)
                self.eng.wait_ge(sems["dve_step"], T.add("dve_step"))
                nc.vector.tensor_tensor(z[0], lam, z[2], ALU.min).then_inc(sems["lam_abs"], 1)
                T.add("lam_abs")
                self.eng.wait_ge(sems["lam_exp"], T.add("lam_exp"))
                nc.vector.tensor_scalar(z[3], z[1], 2.0, None, ALU.add).then_inc(sems["dve_step"], 1)
                self.eng.wait_ge(sems["dve_step"], T.add("dve_step"))
                nc.vector.reciprocal(z[4], z[3]).then_inc(sems["dve_step"], 1)
                self.eng.wait_ge(sems["dve_step"], T.add("dve_step"))
                nc.vector.tensor_tensor(z[3], z[1], z[4], ALU.mult).then_inc(sems["dve_step"], 1)
                self.eng.wait_ge(sems["dve_step"], T.add("dve_step"))
                nc.vector.tensor_tensor(z[4], z[3], z[3], ALU.mult).then_inc(sems["dve_step"], 1)
                self.eng.wait_ge(sems["dve_step"], T.add("dve_step"))
                nc.vector.tensor_scalar(z[5], z[4], 1.0 / 17, None, ALU.mult).then_inc(sems["dve_step"], 1)
                self.eng.wait_ge(sems["dve_step"], T.add("dve_step"))
                for odd in (15, 13, 11, 9, 7, 5, 3):
                    ins = nc.vector.scalar_tensor_tensor(z[5], z[5], 1.0 / odd, z[4], ALU.add, ALU.mult)
                    ins.then_inc(sems["dve_step"], 1)
                    self.eng.wait_ge(sems["dve_step"], T.add("dve_step"))
                nc.vector.scalar_tensor_tensor(z[5], z[5], 1.0, z[3], ALU.add, ALU.mult).then_inc(sems["dve_step"], 1)
                self.eng.wait_ge(sems["dve_step"], T.add("dve_step"))
                nc.vector.tensor_scalar(z[6], lam, 0.0, 8.0, ALU.min, ALU.mult).then_inc(sems["dve_step"], 1)
                self.eng.wait_ge(sems["dve_step"], T.add("dve_step"))
                ins = nc.vector.scalar_tensor_tensor(c_lru[:], z[5], -16.0, z[6], ALU.mult, ALU.add)
                ins.then_inc(sems["c_lru_ready"], 1)
                T.add("c_lru_ready")

            def lru_part(self, q):
                T, tiles = self.T, slice(4 * q, 4 * q + 4)
                if q == 0:
                    self.lru_constant()
                self.eng.wait_ge(sems["lru_exp"], T.add("lru_exp"))
                nc.vector.tensor_scalar(lru_d[:], lru_t[:], -1.0, 1.0, ALU.mult, ALU.add).then_inc(sems["dve_step"], 1)
                self.eng.wait_ge(sems["dve_step"], T.add("dve_step"))
                nc.vector.reciprocal(lru_d[:], lru_d[:]).then_inc(sems["dve_step"], 1)
                self.eng.wait_ge(sems["dve_step"], T.add("dve_step"))
                ins = nc.vector.scalar_tensor_tensor(lru_t[:], lru_t[:], -2.0, lru_d[:], ALU.mult, ALU.mult)
                ins.then_inc(sems["dve_step"], 1)
                self.eng.wait_ge(sems["dve_step"], T.add("dve_step"))
                nc.vector.tensor_scalar(lru_t[:], lru_t[:], 2.0 ** -116, None, ALU.max).then_inc(sems["lru_ratio"], 1)
                T.add("lru_ratio")
                nc.vector.tensor_tensor(tmp_4[:], ht_h[:, tiles].bitcast(F32), ht_l[:, tiles].bitcast(F32),
                                        ALU.add).then_inc(sems["dve_step"], 1)
                self.eng.wait_ge(sems["dve_step"], T.add("dve_step"))
                nc.vector.tensor_tensor(tmp_4[:], tmp_4[:], gate_i[:, tiles], ALU.mult).then_inc(sems["dve_step"], 1)
                self.eng.wait_ge(sems["dve_step"], T.add("dve_step"))
                self.eng.wait_ge(sems["lru_root"], T.add("lru_root"))
                nc.vector.tensor_tensor(tmp_4[:], tmp_4[:], lru_t[:], ALU.mult).then_inc(sems["dve_step"], 1)
                self.eng.wait_ge(sems["dve_step"], T.add("dve_step"))
                for k in range(4):
                    a = nc.vector.tensor_tensor_scan(lru_d[:, k], lru_a[:, k], tmp_4[:, k], 0.0, ALU.mult, ALU.add)
                a.then_inc(sems["dve_step"], 1)
                self.eng.wait_ge(sems["dve_step"], T.add("dve_step"))
                nc.vector.tensor_tensor(tmp_4[:], lru_d[:], y_br[:, tiles], ALU.mult).then_inc(sems["lru_z"], 1)
                T.add("lru_z")
                self.eng.wait_ge(sems["split_hi"], T.add("split_hi"))
                a = nc.vector.tensor_tensor(xt_l[:, tiles], tmp_4[:], xt_h[:, tiles].bitcast(F32), ALU.subtract)
                a.then_inc(sems["split_done"], 1)
                T.add("split_done")

            def gates(self):
                for j in range(4):
                    if j < 3:
                        self.conv()
                    for _ in range(2):
                        self.take_pair()
                        self.T.add("psum_free_act")
                self.conv()
                self.eng.wait_ge(sems["psum_free_act"], self.T.at("psum_free_act"))

            def attention(self, kind):
                T = self.T
                items, heads, per = attention_items(kind)
                if kind == "diff":
                    self.eng.wait_ge(sems["params_loaded"], 16 * N_PARAM_LOADS)
                    self.eng.wait_ge(sems["s5_ready"], T.add("s5_ready"))
                    for s in range(2):
                        a = nc.vector.tensor_tensor(probs[:, 0, s, 0:64], lamv[:, 2 * s], lamv[:, 2 * s + 1], ALU.mult)
                    a.then_inc(sems["dve_step"], 1)
                    self.eng.wait_ge(sems["dve_step"], T.add("dve_step"))
                    ins = nc.vector.tensor_reduce(st(LAMS, 2), probs[:, 0, :, 0:64], AX_X, ALU.add)
                    ins.then_inc(sems["lam_dot"], 1)
                    T.add("lam_dot")
                    self.eng.wait_ge(sems["lam_exp"], T.add("lam_exp"))
                    nc.vector.scalar_tensor_tensor(st(LAM), st(LAMS + 1), -LAMBDA_INIT, st(LAMS), ALU.add, ALU.subtract)
                    ins = nc.vector.tensor_scalar(subg[:], subg[:], 1.0 - LAMBDA_INIT, None, ALU.mult)
                    ins.then_inc(sems["dve_step"], 1)
                    self.eng.wait_ge(sems["dve_step"], T.add("dve_step"))
                if kind == "window":
                    nc.vector.tensor_scalar(nsink, sink[:], -1.0, None, ALU.mult).then_inc(sems["dve_step"], 1)
                    self.eng.wait_ge(sems["dve_step"], T.add("dve_step"))
                if kind == "dilated":
                    self.eng.wait_ge(sems["masks_loaded"], 32)
                scale = (P if kind == "dilated" else 64) ** -0.5
                which = {"diff": 0, "window": 1, "dilated": 0}[kind]

                def bias(k):
                    pr, m = items[k]
                    b, keys, q = k % 2, (m + 1) * P, 2 * (k % 2)
                    self.eng.wait_ge(sems["scores_ready"], T.add("scores_ready"))
                    if k >= 2:
                        self.eng.wait_ge(sems["probs_turned"], T.add("probs_turned"))
                    mk = mask[:, which, SEQ - keys:SEQ] if m == 0 else mask[:, which]
                    nc.vector.scalar_tensor_tensor(
                        scores[:, b, :, 0:keys], score_ps[b][:, :, 0:keys], scale,
                        mk.unsqueeze(1).to_broadcast([P, 2, keys]), ALU.mult, ALU.add).then_inc(sems["dve_step"], 1)
                    self.eng.wait_ge(sems["dve_step"], T.add("dve_step"))
                    a = nc.vector.tensor_reduce(st(MAXN + q, 2), scores[:, b, :, 0:keys], AX_X, ALU.max, negate=True)
                    if kind == "window":
                        a.then_inc(sems["dve_step"], 1)
                        self.eng.wait_ge(sems["dve_step"], T.add("dve_step"))
                        a = nc.vector.tensor_tensor(st(MAXN + q, 2), st(MAXN + q, 2), nsink[:, 2 * pr:2 * pr + 2],
                                                    ALU.min)
                    a.then_inc(sems["biased"], 1)
                    T.add("biased")

                def normalise(k):
                    pr, m = items[k]
                    b, keys, q, r = k % 2, (m + 1) * P, 2 * (k % 2), RSUM + 2 * (k % 4)
                    self.eng.wait_ge(sems["exp_ready"], T.add("exp_ready"))
                    sc, pb = scores[:, b, :, 0:keys], probs[:, b, :, 0:keys]
                    if kind == "diff":
                        nc.vector.reciprocal(st(r, 2), st(SUMS + q, 2)).then_inc(sems["dve_step"], 1)
                        self.eng.wait_ge(sems["dve_step"], T.add("dve_step"))
                        nc.vector.tensor_scalar(pb[:, 0], sc[:, 0], st(r), None, ALU.mult)
                        nc.vector.tensor_tensor(st(r + 1), st(r + 1), st(LAM), ALU.mult).then_inc(sems["dve_step"], 1)
                        self.eng.wait_ge(sems["dve_step"], T.add("dve_step"))
                        a = nc.vector.scalar_tensor_tensor(pb[:, 0], sc[:, 1], st(r + 1), pb[:, 0], ALU.mult, ALU.add)
                    elif kind == "window":
                        nc.vector.tensor_tensor(st(SUMS + q, 2), st(SUMS + q, 2), st(ESINK + q, 2),
                                                ALU.add).then_inc(sems["dve_step"], 1)
                        self.eng.wait_ge(sems["dve_step"], T.add("dve_step"))
                        a = nc.vector.reciprocal(st(r, 2), st(SUMS + q, 2))
                    else:
                        mk = mask[:, 1, SEQ - keys:SEQ] if m == 0 else mask[:, 1]
                        nc.vector.tensor_tensor(pb, sc, mk.unsqueeze(1).to_broadcast([P, 2, keys]),
                                                ALU.mult).then_inc(sems["dve_step"], 1)
                        self.eng.wait_ge(sems["dve_step"], T.add("dve_step"))
                        nc.vector.tensor_reduce(st(SUMS + q, 2), pb, AX_X, ALU.add).then_inc(sems["dve_step"], 1)
                        self.eng.wait_ge(sems["dve_step"], T.add("dve_step"))
                        a = nc.vector.reciprocal(st(r, 2), st(SUMS + q, 2))
                    a.then_inc(sems["probs_ready"], 1)
                    T.add("probs_ready")

                def copy_turned(k):
                    m = items[k][1]
                    n = heads * (m + 1)
                    if k >= len(items) - 2:
                        self.eng.wait_ge(sems["probs_turned"], T.add("probs_turned"))
                    if k >= 2:
                        self.eng.wait_ge(sems["mixed"], T.add("mixed"))
                    nc.vector.tensor_copy(probs_t[:, k % 2, 0:n],
                                          turn_ps[:, 2 * (k % 2):2 * (k % 2) + 2].rearrange(
                                              "p a (b c) -> p (a b) c", c=P)[:, 0:n]).then_inc(sems["probs_copied"], 1)
                    T.add("probs_copied")

                bias(0)
                for k in range(len(items)):
                    if k + 1 < len(items):
                        bias(k + 1)
                    normalise(k)
                    if k:
                        copy_turned(k - 1)
                copy_turned(len(items) - 1)
                T.add("mixed", 2)
                T.add("mixed_out", len(items))
                if kind == "diff":
                    self.eng.wait_ge(sems["mixed_out"], T.at("mixed_out"))
                    for m in range(M):
                        o, sq = acc[:, m, 0:1024], (stg, tmp)[m][:].rearrange("p m n -> p (m n)")
                        nc.vector.tensor_tensor(sq, o, o, ALU.mult).then_inc(sems["dve_step"], 1)
                        self.eng.wait_ge(sems["dve_step"], T.add("dve_step"))
                        a = nc.vector.tensor_reduce(st(SUB + 8 * m, 8), sq.rearrange("p (h d) -> p h d", d=P), AX_X,
                                                    ALU.add)
                    a.then_inc(sems["tot_ready"], 1)
                    T.add("tot_ready")
                    self.eng.wait_ge(sems["root_ready"], T.add("root_ready"))
                    nc.vector.reciprocal(st(SUB, 16), st(SUB, 16)).then_inc(sems["dve_step"], 1)
                    self.eng.wait_ge(sems["dve_step"], T.add("dve_step"))
                    for m in range(M):
                        o = acc[:, m, 0:1024].rearrange("p (h d) -> p h d", d=P)
                        ins = nc.vector.tensor_tensor(
                            o, o, st(SUB + 8 * m, 8).unsqueeze(2).to_broadcast([P, 8, P]), ALU.mult)
                        ins.then_inc(sems["dve_step"], 1)
                        self.eng.wait_ge(sems["dve_step"], T.add("dve_step"))
                        a = nc.vector.tensor_tensor(o, o, subg[:].unsqueeze(1).to_broadcast([P, 8, P]), ALU.mult)
                    a.then_inc(sems["dve_step"], 1)
                    self.eng.wait_ge(sems["dve_step"], T.add("dve_step"))
                else:
                    self.eng.wait_ge(sems["mixed_out"], T.at("mixed_out"))
                    nc.vector.memset(unused, 0.0).then_inc(sems["mix_ready"], 1)
                    T.add("mix_ready")

            def s5_params(self):
                self.eng.wait_ge(sems["s5_asked"], self.T.add("s5_asked"))
                nc.vector.reciprocal(s5[:, 11], s5[:, 10]).then_inc(sems["s5_recip"], 1)

            def s5(self):
                T = self.T
                for g in range(8):
                    rot = rots[g % 2]
                    c, s = rot[:, 0], rot[:, 1]
                    xr, xi = (ps[:].rearrange("p m (k s) -> p (m k) s", s=SEQ) for ps in pair)
                    self.eng.wait_ge(sems["bu_ready"], T.add("bu_ready"))
                    self.eng.wait_ge(sems["rot_ready"], T.add("rot_ready"))
                    if T.any("y_ready"):
                        self.eng.wait_ge(sems["y_ready"], T.at("y_ready"))
                    nc.vector.tensor_tensor(t_1[:], xr, c, ALU.mult)
                    nc.vector.tensor_tensor(t_2[:], xi, s, ALU.mult)
                    nc.vector.tensor_tensor(h_im[:], xi, c, ALU.mult)
                    nc.vector.tensor_tensor(h_re[:], xr, s, ALU.mult).then_inc(sems["bu_used"], 1)
                    self.eng.wait_ge(sems["bu_used"], T.add("bu_used"))
                    nc.vector.tensor_tensor(t_1[:], t_1[:], t_2[:], ALU.add)
                    nc.vector.tensor_tensor(h_im[:], h_im[:], h_re[:], ALU.subtract).then_inc(sems["dve_step"], 1)
                    self.eng.wait_ge(sems["dve_step"], T.add("dve_step"))
                    for src, dst in ((t_1, t_2), (h_im, h_re)):
                        for j in range(4):
                            t = 4 * g + j
                            a = nc.vector.tensor_tensor_scan(dst[:, j], decay[:, t:t + 1].to_broadcast([P, SEQ]),
                                                             src[:, j], 0.0, ALU.mult, ALU.add)
                    a.then_inc(sems["dve_step"], 1)
                    self.eng.wait_ge(sems["dve_step"], T.add("dve_step"))
                    nc.vector.tensor_tensor(t_1[:], t_2[:], c, ALU.mult)
                    nc.vector.tensor_tensor(h_im[:], h_re[:], s, ALU.mult)
                    nc.vector.tensor_tensor(t_2[:], t_2[:], s, ALU.mult)
                    nc.vector.tensor_tensor(h_re[:], h_re[:], c, ALU.mult).then_inc(sems["rot_used"], 1)
                    self.eng.wait_ge(sems["rot_used"], T.add("rot_used"))
                    nc.vector.tensor_tensor(t_1[:], t_1[:], h_im[:], ALU.subtract)
                    nc.vector.tensor_tensor(h_re[:], h_re[:], t_2[:], ALU.add).then_inc(sems["h_ready"], 1)
                    T.add("h_ready")
                    T.add("y_ready")
                    if g:
                        self.skip(g - 1, 1)
                self.skip(7, 0)
                self.eng.wait_ge(sems["gelu_a"], T.add("gelu_a"))
                ins = nc.vector.tensor_scalar(glu_z[:], glu_z[:], GELU_3, GELU_1, ALU.mult, ALU.add)
                ins.then_inc(sems["dve_step"], 1)
                self.eng.wait_ge(sems["dve_step"], T.add("dve_step"))
                nc.vector.tensor_tensor(glu_z[:], glu_z[:], u2[:], ALU.mult).then_inc(sems["gelu_b"], 1)
                T.add("gelu_b")
                self.eng.wait_ge(sems["gelu_a"], T.add("gelu_a"))
                nc.vector.tensor_tensor(u2[:], u2[:], glu_z[:], ALU.mult).then_inc(sems["y_gelu"], 1)
                T.add("y_gelu")
                self.eng.wait_ge(sems["split_hi"], T.add("split_hi"))
                ins = nc.vector.tensor_tensor(xt_l[:, 0:8], u2[:], xt_h[:, 0:8].bitcast(F32), ALU.subtract)
                ins.then_inc(sems["split_done"], 1)
                T.add("split_done")

            def skip(self, g, back):
                self.eng.wait_ge(sems["y_ready"], self.T.at("y_ready", back))
                c = C_DSKIP + g
                a = nc.vector.scalar_tensor_tensor(u2[:, g], u2[:, g], col[:, c:c + 1], misc_ps[:, g % 2, 0:SEQ],
                                                   ALU.mult, ALU.add)
                if g == 7:
                    a.then_inc(sems["y_done"], 1)
                    self.T.add("y_done")
                else:
                    a.then_inc(sems["y_read"], 1)
                    self.T.add("y_read")

            def glu(self):
                T = self.T
                for _ in range(3):
                    self.conv()
                for _ in range(2):
                    self.take_pair()
                    T.add("psum_free_act")
                self.conv()
                self.eng.wait_ge(sems["psum_free_act"], T.at("psum_free_act"))
                nc.vector.tensor_tensor(glu_z[:], glu_z[:], u2[:], ALU.mult).then_inc(sems["y_gelu"], 1)
                T.add("y_gelu")
                self.eng.wait_ge(sems["split_hi"], T.add("split_hi"))
                ins = nc.vector.tensor_tensor(xt_l[:, 8:16], glu_z[:], xt_h[:, 8:16].bitcast(F32), ALU.subtract)
                ins.then_inc(sems["split_done"], 1)
                T.add("split_done")

            def final(self):
                T = self.T
                for n in range(NCH):
                    self.residual("plain", n)
                self.eng.wait_ge(sems["squared"], T.add("squared", 4))
                self.norm_factor(SSX, RS)
                for n in range(NCH):
                    self.eng.wait_ge(sems["gain_ready"], T.add("gain_ready"))
                    cols = slice(n * CH, (n + 1) * CH)
                    for m in range(M):
                        a = nc.vector.scalar_tensor_tensor(acc[:, m, cols], xres[:, m, cols], st(RS + m),
                                                           misc_ps[:, n % 2], ALU.mult, ALU.mult)
                    a.then_inc(sems["out_ready"], 1)
                    T.add("out_ready")

        class Tensor(Program):
            def setup(self):
                pe = self.eng
                pe.wait_ge(sems["loaded"], 16 * N_LOADS)
                self.eng.wait_ge(sems["rows_ready"], self.T.add("rows_ready"))
                for k, n in enumerate((P, 112, 96)):
                    a = nc.tensor.transpose(misc_ps[:, 0, k * P:k * P + n], prow[0:n, k], ident[0:n, 0:n])
                a.then_inc(sems["params_turned"], 1)
                self.T.add("params_turned")

            def unit(self, xh, xl, ps, t0, first, last, width):
                T = self.T
                r = T.n.get("unit", 0) % RING
                self.eng.wait_ge(sems["lo_ready"], T.at("unit", -1))
                h, l = (w[:, r, 0:KU * width].rearrange("p (t n) -> p t n", t=KU) for w in (hi, lo))
                for k in range(KU):
                    for m in range(M):
                        tok = slice(m * P, (m + 1) * P)
                        s, e = first and k == 0, last and k == KU - 1
                        to = ps[:, m, 0:width]
                        nc.tensor.matmul(to, xh[:, t0 + k, tok], h[:, k], start=s, stop=False)
                        nc.tensor.matmul(to, xl[:, t0 + k, tok], h[:, k], start=False, stop=False)
                        mm = nc.tensor.matmul(to, xh[:, t0 + k, tok], l[:, k], start=False, stop=e)
                mm.then_inc(sems["unit_used"], 1)
                T.add("unit")

            def pair_free(self):
                for name in ("psum_free_act", "psum_free_dve"):
                    if self.T.any(name, 1 if self.last_by == name else 0):
                        self.eng.wait_ge(sems[name], self.T.at(name, 1 if self.last_by == name else 0))

            last_by = None

            def turn(self, prev):
                self.eng.wait_ge(sems[self.STAGED[prev[0]]], self.T.at(self.STAGED[prev[0]]))
                self.eng.wait_ge(sems["split_done"], self.T.at("split_done"))
                tiles = prev[2][2] if len(prev[2]) > 2 else 4
                for k in range(tiles):
                    for m in range(M):
                        a = nc.tensor.transpose(turn_ps[:, k, m * P:(m + 1) * P], stg[:, m, k * P:(k + 1) * P],
                                                ident[:])
                a.then_inc(sems["turned"], 1)
                self.T.add("turned")
                self.T.add("split_done")

            def chunk(self, kind, w, x=None, units=4, width=CH, prev=None, lead=None, to=None, order=None, **_):
                T, ps = self.T, self.take_pair()
                self.pair_free()
                if lead:
                    self.lead_first(lead)
                for j in range(units):
                    if prev and j == min(2, units - 2):
                        self.turn(prev)
                    if prev and kind == "add" and j == units - 1:
                        self.eng.wait_ge(sems["split_done"], T.at("split_done"))
                    if lead and j < lead[3]:
                        done = T.n["lead_base"] + j + 1
                        self.eng.wait_ge(sems["split_done"], done)
                    k = order[j] if order else j
                    self.unit(x[0], x[1], ps, KU * k, j == 0, j == units - 1, width)
                    if lead and lead[0] != "lru" and j < 2 and j + 2 < lead[3]:
                        self.turn_part(lead, j + 2)
                self.last_by = self.BY[kind]
                T.add(self.last_by)
                if kind in ("relu2", "gelu", "rope"):
                    T.add("staged")
                return (kind, ps, to, width) if kind in self.TURNED else None

            def drain(self, prev):
                self.turn(prev)

            def lead_first(self, lead):
                T, kind = self.T, lead[0]
                T.n["lead_base"] = T.n.get("split_done", 0)
                if kind == "lru":
                    T.add("split_done", 4)
                    return
                if kind == "turn":
                    self.eng.wait_ge(sems["mix_ready"], T.add("mix_ready"))
                if kind == "post":
                    self.gain(lead[1], 0)
                    self.gain(lead[1], 1)
                self.turn_part(lead, 0)
                if kind == "post":
                    self.gain(lead[1], 2)
                if lead[3] > 1:
                    self.turn_part(lead, 1)
                if kind == "post":
                    self.gain(lead[1], 3)

            def gain(self, row0, n):
                T = self.T
                if n == 0:
                    self.eng.wait_ge(sems["params_loaded"], 16 * N_PARAM_LOADS)
                    T.n["gain_base"] = T.n.get("x_ready", 0)
                else:
                    if n >= 2:
                        self.eng.wait_ge(sems["x_ready"], T.n["gain_base"] + n - 1)
                r = row0 + n
                nc.tensor.matmul(misc_ps[:, n % 2], ident[0:G_ROWS, r:r + 1].to_broadcast([G_ROWS, P]),
                                 grows[0:G_ROWS], start=True, stop=True).then_inc(sems["gain_ready"], 1)
                T.add("gain_ready")

            def turn_part(self, lead, n):
                T, kind = self.T, lead[0]
                if kind in ("post", "plain"):
                    self.eng.wait_ge(sems["x_ready"], T.add("x_ready"))
                if n >= 2:
                    self.eng.wait_ge(sems["split_done"], T.n["lead_base"] + n - 1)
                elif n == 0:
                    if T.any("split_done"):
                        self.eng.wait_ge(sems["split_done"], T.at("split_done"))
                else:
                    if T.any("psum_free_act"):
                        self.eng.wait_ge(sems["psum_free_act"], T.at("psum_free_act"))
                    if T.any("psum_free_dve"):
                        self.eng.wait_ge(sems["psum_free_dve"], T.at("psum_free_dve"))
                src = acc if kind == "turn" else xres
                to = Scalar.part_psum(self, n)
                for k in range(4):
                    for m in range(M):
                        c = n * CH + k * P
                        a = nc.tensor.transpose(to[:, k, m * P:(m + 1) * P], src[:, m, c:c + P], ident[:])
                a.then_inc(sems["turned"], 1)
                T.add("turned")
                T.add("split_done")

            def gates(self):
                T = self.T
                for j in range(4):
                    r = T.n["unit"] % RING
                    self.eng.wait_ge(sems["lo_ready"], T.at("unit", -1))
                    h, l = (w[:, r].rearrange("p (n t e) -> p n t e", n=4, t=2) for w in (hi, lo))
                    for b in range(2):
                        ps = self.take_pair()
                        self.pair_free()
                        for k in range(2):
                            n = 2 * b + k
                            for e in range(2):
                                to, out_cols = ps[:, k, e * SEQ:(e + 1) * SEQ], slice(e * P, (e + 1) * P)
                                for t in range(2):
                                    x = 8 * (j % 2) + 2 * n + t
                                    xh, xl = ht_h[:, x], ht_l[:, x]
                                    nc.tensor.matmul(to, h[:, n, t, out_cols], xh, start=t == 0, stop=False)
                                    nc.tensor.matmul(to, h[:, n, t, out_cols], xl, start=False, stop=False)
                                    a = nc.tensor.matmul(to, l[:, n, t, out_cols], xh, start=False, stop=t == 1)
                        if b == 0:
                            a.then_inc(sems["block_done"], 1)
                            T.add("block_done")
                        else:
                            a.then_inc(sems["unit_used"], 1)
                            T.add("unit")
                        self.last_by = "psum_free_act"
                        T.add("psum_free_act")
                self.eng.wait_ge(sems["psum_free_act"], T.at("psum_free_act"))

            def attention(self, kind):
                T = self.T
                items, heads, per = attention_items(kind)
                self.eng.wait_ge(sems["split_done"], T.at("split_done"))
                self.eng.wait_ge(sems["psum_free_act"], T.at("psum_free_act"))
                if kind != "diff":
                    self.eng.wait_ge(sems["mixed_out"], T.at("mixed_out"))

                def score(k):
                    pr, m = items[k]
                    keys, tok = (m + 1) * P, slice(m * P, (m + 1) * P)
                    if k >= 2:
                        self.eng.wait_ge(sems["biased"], T.add("biased"))
                    for s in range(2):
                        half = slice(64 * s, 64 * s + 64)
                        if kind == "diff":
                            q, kk = qk0[half, pr, tok], qk0[half, 8 + pr, 0:keys]
                        elif kind == "window":
                            q, kk = qk0[half, 16 + pr, tok], k_swa[half, int(s != pr // 4), 0:keys]
                        else:
                            q, kk = qk2[:, 2 * pr + s, tok], qk2[:, 8 + 2 * pr + s, 0:keys]
                        a = nc.tensor.matmul(score_ps[k % 2][:, s, 0:keys], q, kk, start=True, stop=True)
                    a.then_inc(sems["scores_ready"], 1)
                    T.add("scores_ready")

                def turn_probs(k):
                    m = items[k][1]
                    self.eng.wait_ge(sems["probs_ready"], T.add("probs_ready"))
                    src = scores if kind == "window" else probs
                    to = turn_ps[:, 2 * (k % 2):2 * (k % 2) + 2].rearrange("p a (b c) -> p (a b) c", c=P)
                    for s in range(heads):
                        for t in range(m + 1):
                            a = nc.tensor.transpose(to[:, s * (m + 1) + t], src[:, k % 2, s, t * P:(t + 1) * P],
                                                    ident[:])
                    a.then_inc(sems["probs_turned"], 1)
                    T.add("probs_turned")

                def mix(k):
                    pr, m = items[k]
                    self.eng.wait_ge(sems["probs_copied"], T.add("probs_copied"))
                    if k >= 2:
                        self.eng.wait_ge(sems["mixed_out"], T.add("mixed_out"))
                    for s in range(heads):
                        for t in range(m + 1):
                            if kind == "diff":
                                v = v0[:, t, pr * P:(pr + 1) * P]
                            elif kind == "window":
                                v = v_swa[:, t, 64 * (pr // 4):64 * (pr // 4) + 64]
                            else:
                                v = v2[:, t, (2 * pr + s) * P:(2 * pr + s + 1) * P]
                            a = nc.tensor.matmul(pair[0][:, k % 2, s * per:s * per + per],
                                                 probs_t[:, k % 2, s * (m + 1) + t], v, start=t == 0, stop=t == m)
                    a.then_inc(sems["mixed"], 1)
                    T.add("mixed")

                score(0)
                score(1)
                for k in range(len(items)):
                    turn_probs(k)
                    if k + 2 < len(items):
                        score(k + 2)
                    if k:
                        mix(k - 1)
                mix(len(items) - 1)
                T.add("mixed_out", 2)
                self.eng.wait_ge(sems["biased"], T.add("biased", 2))
                self.eng.wait_ge(sems["mixed_out"], T.at("mixed_out"))

            def s5(self):
                T = self.T

                def turn_b(g):
                    self.eng.wait_ge(sems["b_padded"], T.add("b_padded"))
                    if T.any("c_copied"):
                        self.eng.wait_ge(sems["c_copied"], T.at("c_copied"))
                    for ri in range(2):
                        for j in range(4):
                            a = nc.tensor.transpose(turn_all[:, ri, j], b_pad[:, ri, j], ident[:])
                    a.then_inc(sems["b_turned"], 1)
                    T.add("b_turned")

                def turn_c(g):
                    self.eng.wait_ge(sems["c_padded"], T.add("c_padded"))
                    self.eng.wait_ge(sems["b_copied"], T.at("b_copied"))
                    for ri in range(2):
                        for j in range(4):
                            a = nc.tensor.transpose(turn_all[:, ri, j], c_pad[:, ri, j], ident[:])
                    a.then_inc(sems["c_turned"], 1)
                    T.add("c_turned")
                    T.add("c_copied")

                def bu(g):
                    self.eng.wait_ge(sems["b_copied"], T.add("b_copied"))
                    if T.any("bu_used"):
                        self.eng.wait_ge(sems["bu_used"], T.at("bu_used"))
                    for ri in range(2):
                        to = pair[ri][:].rearrange("p m (k s) -> p (m k) s", s=SEQ)
                        for j in range(4):
                            a = nc.tensor.matmul(to[:, j], b_t[:, ri, j], u2[:, g], start=True, stop=True)
                    a.then_inc(sems["bu_ready"], 1)
                    T.add("bu_ready")
                    T.add("bu_used")

                def y(g):
                    self.eng.wait_ge(sems["h_ready"], T.add("h_ready"))
                    self.eng.wait_ge(sems["c_copied"], T.at("c_copied"))
                    if g >= 2:
                        self.eng.wait_ge(sems["y_read"], T.add("y_read"))
                    for j in range(4):
                        for ri, h in enumerate((t_1, h_re)):
                            a = nc.tensor.matmul(misc_ps[:, g % 2, 0:SEQ], c_t[:, ri, j], h[:, j],
                                                 start=j == 0 and ri == 0, stop=j == 3 and ri == 1)
                    a.then_inc(sems["y_ready"], 1)
                    T.add("y_ready")

                turn_b(0)
                bu(0)
                turn_c(0)
                for g in range(8):
                    if g < 7:
                        turn_b(g + 1)
                        bu(g + 1)
                    y(g)
                    if g < 7:
                        turn_c(g + 1)
                T.add("split_done")
                self.eng.wait_ge(sems["y_done"], T.add("y_done"))
                self.eng.wait_ge(sems["split_done"], T.at("split_done"))

            def glu(self):
                T = self.T
                for half in range(2):
                    ps = self.take_pair()
                    flat = ps[:].rearrange("p m (k s) -> p (m k) s", s=SEQ)
                    for kk in range(2):
                        r = T.n["unit"] % RING
                        self.eng.wait_ge(sems["lo_ready"], T.at("unit", -1))
                        h, l = (w[:, r].rearrange("p (t n) -> p t n", t=KU) for w in (hi, lo))
                        for e in range(4):
                            cols = slice(e * P, (e + 1) * P)
                            for k in range(KU):
                                t = KU * kk + k
                                first, last = kk == 0 and k == 0 and e % 2 == 0, kk == 1 and k == KU - 1
                                nc.tensor.matmul(flat[:, e], h[:, k, cols], xt_h[:, t], start=first, stop=False,
                                                 skip_group_check=True)
                                nc.tensor.matmul(flat[:, e], h[:, k, cols], xt_l[:, t], start=False, stop=False,
                                                 skip_group_check=True)
                                a = nc.tensor.matmul(flat[:, e], l[:, k, cols], xt_h[:, t], start=False, stop=last,
                                                     skip_group_check=True)
                        a.then_inc(sems["unit_used"], 1)
                        T.add("unit")
                    self.last_by = "psum_free_act"
                    T.add("psum_free_act")
                self.eng.wait_ge(sems["split_done"], T.add("split_done"))

            def final(self):
                T = self.T
                for n in range(NCH):
                    if n >= 2:
                        self.eng.wait_ge(sems["out_ready"], T.add("out_ready"))
                    r = G_FINAL + n
                    nc.tensor.matmul(misc_ps[:, n % 2], ident[0:G_ROWS, r:r + 1].to_broadcast([G_ROWS, P]),
                                     grows[0:G_ROWS], start=True, stop=True).then_inc(sems["gain_ready"], 1)
                    T.add("gain_ready")

        class Pool(Program):
            def tt(self, out, a, b, op):
                nc.gpsimd.tensor_tensor(out, a, b, op).then_inc(sems["pool_step"], 1)
                self.eng.wait_ge(sems["pool_step"], self.T.add("pool_step"))

            def ts(self, out, a, s1, s2, op0, op1=ALU.bypass):
                nc.gpsimd.tensor_scalar(out, a, s1, s2, op0, op1).then_inc(sems["pool_step"], 1)
                self.eng.wait_ge(sems["pool_step"], self.T.add("pool_step"))

            def cmul(self, dst, a, b, t):
                self.tt(t[0], a[0], b[0], ALU.mult)
                self.tt(t[1], a[1], b[1], ALU.mult)
                self.tt(t[0], t[0], t[1], ALU.subtract)
                self.tt(t[1], a[0], b[1], ALU.mult)
                self.tt(dst[1], a[1], b[0], ALU.mult)
                self.tt(dst[1], dst[1], t[1], ALU.add)
                nc.gpsimd.tensor_copy(dst[0], t[0]).then_inc(sems["pool_step"], 1)
                self.eng.wait_ge(sems["pool_step"], self.T.add("pool_step"))

            def setup(self):
                T = self.T
                self.eng.wait_ge(sems["col_ready"], T.add("col_ready"))
                dt, zr, zi, k, q, th, th2, _, sn, sh, den, rden, ar, ai, nr, fr, fi, pr, pi, t1, t2, t3 = (
                    s5[:, n] for n in range(22))
                are, aim = col[:, C_ARE:C_ARE + 32], col[:, C_AIM:C_AIM + 32]
                self.tt(zr, are, dt, ALU.mult)
                self.tt(zi, aim, dt, ALU.mult)
                magic = 1.5 * 2.0 ** 23
                self.ts(k, zi, 1.0 / (2.0 * math.pi), magic, ALU.mult, ALU.add)
                self.ts(k, k, magic, None, ALU.subtract)
                c1, c2 = 6.28125, 1.93500518798828125e-3
                c3 = 2.0 * math.pi - c1 - c2
                self.ts(th, k, c1, None, ALU.mult)
                self.tt(th, zi, th, ALU.subtract)
                for c in (c2, c3):
                    self.ts(q, k, c, None, ALU.mult)
                    self.tt(th, th, q, ALU.subtract)
                self.ts(th, th, 3.14159, -3.14159, ALU.min, ALU.max)
                self.ts(th2, th, 0.5, None, ALU.mult)
                self.tt(t1, are, are, ALU.mult)
                self.tt(t2, aim, aim, ALU.mult)
                nc.gpsimd.tensor_tensor(den, t1, t2, ALU.add).then_inc(sems["s5_asked"], 1)
                T.add("s5_asked")
                self.eng.wait_ge(sems["s5_given"], T.add("s5_given"))
                self.eng.wait_ge(sems["s5_recip"], T.add("s5_recip"))
                self.eng.wait_ge(sems["params_loaded"], 16 * N_PARAM_LOADS)
                cs = th2
                self.tt(t1, sh, sh, ALU.mult)
                self.ts(cs, t1, -2.0, 1.0, ALU.mult, ALU.add)
                self.tt(ar, decay[:], cs, ALU.mult)
                self.tt(ai, decay[:], sn, ALU.mult)
                self.ts(nr, ar, 1.0, None, ALU.subtract)
                self.tt(t1, nr, are, ALU.mult)
                self.tt(t2, ai, aim, ALU.mult)
                self.tt(t1, t1, t2, ALU.add)
                self.tt(fr, t1, rden, ALU.mult)
                self.tt(t1, ai, are, ALU.mult)
                self.tt(t2, nr, aim, ALU.mult)
                self.tt(t1, t1, t2, ALU.subtract)
                self.tt(fi, t1, rden, ALU.mult)

                def spread(a, n):
                    return a.unsqueeze(2).to_broadcast([P, SSM_TILES, n])

                self.cmul((b_bar[:, 0], b_bar[:, 1]), (b_raw[:, 0], b_raw[:, 1]), (spread(fr, 16), spread(fi, 16)),
                          (s5_t[:, 0], s5_t[:, 1]))
                nc.gpsimd.tensor_copy(pr, cs).then_inc(sems["pool_step"], 1)
                self.eng.wait_ge(sems["pool_step"], T.add("pool_step"))
                nc.gpsimd.tensor_copy(pi, sn).then_inc(sems["pool_step"], 1)
                self.eng.wait_ge(sems["pool_step"], T.add("pool_step"))
                for level in range(2):
                    re, im = pw[:, level, 0], pw[:, level, 1]
                    nc.gpsimd.memset(re[:, :, 0:1], 1.0)
                    nc.gpsimd.memset(im[:, :, 0:1], 0.0).then_inc(sems["pool_step"], 1)
                    self.eng.wait_ge(sems["pool_step"], T.add("pool_step"))
                    for e in range(4):
                        n = 2 ** e
                        self.cmul((re[:, :, n:2 * n], im[:, :, n:2 * n]), (re[:, :, 0:n], im[:, :, 0:n]),
                                  (spread(pr, n), spread(pi, n)), (s5_t[:, 0, :, 0:n], s5_t[:, 1, :, 0:n]))
                        self.tt(t1, pr, pr, ALU.mult)
                        self.tt(t2, pi, pi, ALU.mult)
                        self.tt(t3, pr, pi, ALU.mult)
                        self.tt(pr, t1, t2, ALU.subtract)
                        self.ts(pi, t3, 2.0, None, ALU.mult)
                nc.gpsimd.tensor_copy(t1, pr).then_inc(sems["s5_ready"], 1)
                T.add("s5_ready")

            @contextmanager
            def loop(self, trips, **_):
                yield 0

            def chunk(self, kind, w, lead=None, **_):
                if lead and lead[0] in ("post", "plain"):
                    self.T.add("x_ready", 4)
                    if kind in ("relu2", "silu"):
                        self.eng.wait_ge(sems["x_ready"], self.T.at("x_ready"))
                        nc.gpsimd.memset(acc[:], 0.0).then_inc(sems["acc_zero"], 1)
                        self.T.add("acc_zero")

            def pad_b(self, g):
                T = self.T
                if T.any("b_turned"):
                    self.eng.wait_ge(sems["b_turned"], T.at("b_turned"))
                for ri in range(2):
                    a = nc.gpsimd.tensor_tensor(
                        b_pad[:, ri].rearrange("p j (c q) -> p j c q", q=16),
                        b_bar[:, ri, 4 * g:4 * g + 4].unsqueeze(2).to_broadcast([P, 4, 8, 16]),
                        small[:, K_BM:K_BM + 32].rearrange("p (j c) -> p j c", j=4).unsqueeze(3).to_broadcast(
                            [P, 4, 8, 16]), ALU.mult)
                a.then_inc(sems["b_padded"], 1)
                T.add("b_padded")
                T.add("b_turned")

            def pad_c(self, g):
                T = self.T
                if T.any("c_turned"):
                    self.eng.wait_ge(sems["c_turned"], T.at("c_turned"))
                for ri in range(2):
                    a = nc.gpsimd.tensor_tensor(
                        c_pad[:, ri].rearrange("p j (c n) -> p (j c) n", n=64),
                        c_all[:, ri, g].unsqueeze(1).to_broadcast([P, 8, 64]),
                        small[:, K_CM:K_CM + 8].unsqueeze(2).to_broadcast([P, 8, 64]), ALU.mult)
                a.then_inc(sems["c_padded"], 1)
                T.add("c_padded")
                T.add("c_turned")

            def rotation(self, g):
                T = self.T
                if T.any("rot_ready"):
                    self.eng.wait_ge(sems["rot_ready"], T.at("rot_ready"))
                if g >= 2:
                    self.eng.wait_ge(sems["rot_used"], T.add("rot_used"))
                to = rots[g % 2]
                re, im = (to[:, k].rearrange("p j (a b) -> p j a b", b=16) for k in range(2))
                t1, t2 = (rot_t[:, k].rearrange("p j (a b) -> p j a b", b=16) for k in range(2))
                tiles = slice(4 * g, 4 * g + 4)
                fr, fi = (pw[:, 0, k, tiles].unsqueeze(2).to_broadcast([P, 4, 16, 16]) for k in range(2))
                cr, ci = (pw[:, 1, k, tiles].unsqueeze(3).to_broadcast([P, 4, 16, 16]) for k in range(2))
                nc.gpsimd.tensor_tensor(re, cr, fr, ALU.mult)
                nc.gpsimd.tensor_tensor(t1, ci, fi, ALU.mult)
                nc.gpsimd.tensor_tensor(im, ci, fr, ALU.mult)
                nc.gpsimd.tensor_tensor(t2, cr, fi, ALU.mult).then_inc(sems["pool_step"], 1)
                self.eng.wait_ge(sems["pool_step"], T.add("pool_step"))
                nc.gpsimd.tensor_tensor(re, re, t1, ALU.subtract)
                nc.gpsimd.tensor_tensor(im, im, t2, ALU.add).then_inc(sems["rot_ready"], 1)
                T.add("rot_ready")

            def s5(self):
                self.eng.wait_ge(sems["mix_ready"], self.T.add("mix_ready", 2))
                self.eng.wait_ge(sems["c_loaded"], 32)
                for g in range(8):
                    self.pad_b(g)
                    self.pad_c(g)
                    self.rotation(g)

        XT, HT = (xt_h, xt_l), (ht_h, ht_l)

        def acc_cols(n):
            return acc[:, :, n * CH:(n + 1) * CH]

        def ht_part(j):
            return ht_h[:, 4 * j:4 * j + 4], ht_l[:, 4 * j:4 * j + 4]

        def mlp_group(e, w1, w2, g, lead=None):
            prev = None
            for j in range(4):
                prev = e.chunk("relu2", (w1, 0, g * D + j * CH), x=XT, to=ht_part(j), prev=prev,
                               lead=lead if j == 0 else None)
            for n in range(NCH):
                e.chunk("add", (w2, g * KT, n * CH), x=HT, dst=acc_cols(n), n=n, prev=prev if n == 0 else None)

        MLP_STRIDE = dict(unit=32, chunk=8, raw0=128, raw1=128, raw2=128, raw3=128, psum_free_act=4, psum_free_dve=4,
                          staged=4, turned=4, split_hi=4, split_done=4, squared=4)

        def mlp_stage(e, layer, lead):
            mlp_group(e, w_mlp1[layer], w_mlp2[layer], 0, lead)
            with e.loop(3, **MLP_STRIDE) as g:
                mlp_group(e, w_mlp1[layer], w_mlp2[layer], g + 1)

        def swiglu_group(e, g, hidden, lead=None, last=False):
            prev = None
            for j in range(hidden):
                c = g * D + j * CH
                e.chunk("silu", (w_gate2, 0, c), x=XT, prev=prev, lead=lead if j == 0 else None)
                prev = e.chunk("up", (w_up2, 0, c), x=XT, to=ht_part(j))
            for n in range(NCH):
                e.chunk("add", (w_down2, g * KT, n * CH), x=HT, dst=acc_cols(n), n=n, units=hidden, ss=False,
                        prev=prev if n == 0 else None, next_cols=0 if last and n == NCH - 1 else KU * CH)

        def model(e):
            e.setup()
            prev = None
            for c in range(9):
                w = (w_even_in, 0, c * CH)
                if c == 3:
                    e.s5_params()
                if c in (4, 5):
                    prev = e.chunk("tokens", w, x=XT, prev=prev, dst=v0[:, :, (c - 4) * CH:(c - 3) * CH])
                elif c == 8:
                    prev = e.chunk("kv", w, x=XT, prev=prev, width=SEQ, to=(None, k_swa[:], 2))
                else:
                    t = 4 * c if c < 4 else 16 + 4 * (c - 6)
                    prev = e.chunk("copy", w, x=XT, prev=prev, to=(None, qk0[:, t:t + 4]),
                                   lead=("first", None, C_PRE_MIX, 4) + XT if c == 0 else None,
                                   next_cols=KU * SEQ if c == 7 else KU * CH)
            e.drain(prev)
            e.attention("diff")
            e.attention("window")
            for n in range(NCH):
                e.chunk("set", (w_even_out, 0, n * CH), x=XT, dst=acc_cols(n), n=n,
                        lead=("turn", None, None, 4) + XT if n == 0 else None)
            mlp_stage(e, 0, ("post", G_POST_MIX, C_PRE_MLP, 4) + XT)
            prev = None
            for c in range(8):
                kind, to = ("gelu", (None, y_br[:, 4 * c:4 * c + 4])) if c < 4 else ("copy", ("conv", 4 * (c - 4)))
                prev = e.chunk(kind, (w_odd_in, 0, c * CH), x=XT, prev=prev, to=to,
                               lead=("post", G_POST_MLP, C_PRE_MIX + KT, 4) + XT if c == 0 else None)
            e.drain(prev)
            e.gates()
            for n in range(NCH):
                e.chunk("set", (w_odd_out, 0, n * CH), x=XT, dst=acc_cols(n), n=n,
                        lead=("lru", None, None, 4) + XT if n == 0 else None)
            mlp_stage(e, 1, ("post", G_POST_MIX + NCH, C_PRE_MLP + KT, 4) + XT)
            e.dilated_masks()
            prev = None
            for c in range(8):
                w, lead = (w_in2, 0, c * CH), ("post", G_POST_MLP + NCH, C_NORM1, 4) + XT if c == 0 else None
                if c in (4, 5):
                    prev = e.chunk("tokens", w, x=XT, prev=prev, dst=v2[:, :, (c - 4) * CH:(c - 3) * CH])
                elif c < 4:
                    prev = e.chunk("rope", w, x=XT, prev=prev, to=(None, qk2[:, 4 * c:4 * c + 4]), lead=lead)
                else:
                    prev = e.chunk("copy", w, x=XT, prev=prev, to=(None, u2[:, 4 * (c - 6):4 * (c - 6) + 4]))
            e.drain(prev)
            e.attention("dilated")
            e.s5()
            e.glu()
            for n in range(NCH):
                e.chunk("set", (w_out2, 0, n * CH), x=XT, dst=acc_cols(n), n=n, ss=False,
                        lead=("turn", None, None, 2) + XT if n == 0 else None)
            swiglu_group(e, 0, 4, lead=("plain", None, C_NORM2, 4) + XT)
            swiglu_group(e, 1, 4)
            swiglu_group(e, 2, 3, last=True)
            e.final()

        block = ctx.enter_context(nc.Block())

        @block.sync
        def _(sp):
            model(Sync(sp))

        @block.scalar
        def _(act):
            model(Scalar(act))

        @block.vector
        def _(dve):
            model(Vector(dve))

        @block.tensor
        def _(pe):
            model(Tensor(pe))

        @block.gpsimd
        def _(pool):
            model(Pool(pool))


def shape_constants():
    f32 = np.float32
    q, k = np.arange(P)[:, None], np.arange(SEQ)[None, :]
    dist = q + P - k
    causal = dist >= 0
    count = ((dist <= 128).astype(int) + (dist % 4 == 0) + (dist % 16 == 0)) * causal
    masks = [np.where(causal, 0.0, MASKED), np.where(causal & (dist < 128), 0.0, MASKED),
             np.where(count > 0, 0.0, MASKED), count]
    inv_freq = f32(500000.0) ** (-np.arange(0, 32, 2, dtype=f32) / f32(32))
    angle = np.arange(SEQ, dtype=f32)[:, None] * inv_freq[None, :]
    tables = [np.concatenate([t[0:P], t[P:]], axis=1) for t in (np.cos(angle), np.sin(angle))]
    p = np.arange(P)[:, None]
    j, c = np.divmod(np.arange(32), 8)
    b_place = (c // 2 == j) & (c % 2 == p // 64)
    j, par = np.divmod(np.arange(8), 2)
    c_place = p // 16 == 2 * j + par
    return np.concatenate([np.eye(P)] + masks + tables + [b_place, c_place], axis=1).astype(f32)


_INS = ("x even_w_in even_lam_q1 even_lam_k1 even_lam_q2 even_lam_k2 even_subln_g even_sinks even_w_out odd_w_in "
        "odd_conv_w odd_conv_b odd_gate_w odd_gate_b odd_lru_lambda odd_w_out pre_mix_g post_mix_g pre_mlp_g "
        "post_mlp_g mlp_w1 mlp_w2 norm1_g_2 w_in_2 a_re_2 a_im_2 log_dt_2 b_re_2 b_im_2 c_re_2 c_im_2 d_skip_2 "
        "w_glu_2 b_glu_2 w_out_2 norm2_g_2 w_gate_2 w_up_2 w_down_2 final_g_2").split()


def kernel(**inputs):
    import concourse.bacc as bacc
    from concourse.bass_utils import run_bass_kernel_spmd

    nc = bacc.Bacc("TRN2", target_bir_lowering=False, num_devices=1)
    arrays = {f"in_{name}": np.ascontiguousarray(inputs[name]) for name in _INS}
    arrays["in_consts"] = shape_constants()
    aps = {name[3:]: nc.dram_tensor(name, a.shape, mybir.dt.from_np(a.dtype), kind="ExternalInput").ap()
           for name, a in arrays.items()}
    out = nc.dram_tensor("out", (1, SEQ, D), F32, kind="ExternalOutput").ap()
    build(nc, aps, out)
    return run_bass_kernel_spmd(nc, [arrays], core_ids=[0]).results[0]["out"]
```

```python
from collections import namedtuple
from contextlib import ExitStack, contextmanager
import math

import numpy as np
import concourse.bass as bass
from concourse import mybir

F32 = mybir.dt.float32
F32R = mybir.dt.float32r
ALU = mybir.AluOpType
ACT = mybir.ActivationFunctionType
AX_X = mybir.AxisListType.X

P = 128
SEQ = 256
M = SEQ // P
D = 2048
KT = D // P
CH = 512
KU = 4
NCH = D // CH
RAW_SLOTS, RING = 4, 2
EPS = 1e-6
LAMBDA_INIT = 0.8 - 0.6 * math.exp(0.0)
MASKED = -1e30
SSM_TILES = 32
GELU_1 = 2.0 * math.sqrt(2.0 / math.pi)
GELU_3 = GELU_1 * 0.044715

C_PRE_MIX, C_PRE_MLP, C_CONV_W = 0, 32, 64
C_CONV_B, C_GATE_B, C_LAM, C_NORM1, C_NORM2, C_BGLU, C_DSKIP = 128, 144, 176, 192, 208, 224, 232
C_ARE, C_AIM, C_LDT = 256, 288, 320
G_POST_MIX, G_POST_MLP, G_FINAL, G_ROWS = 0, 8, 16, 20
K_IDENT, K_MASK, K_SMALL = 0, 128, 128 + 4 * SEQ
K_COS, K_SIN, K_BM, K_CM = 0, 32, 64, 96
N_SMALL = 104

SEMAPHORES = {
    "loaded": "x, the identity and the first parameters are in SBUF (16 a DMA)",
    "params_loaded": "the other parameters are in SBUF (16 a DMA)",
    "masks_loaded": "the dilated attention's mask and counts are in SBUF",
    "c_loaded": "S5's C is in SBUF",
    "raw0": "a unit is loaded into slot 0 of the ring (16 a DMA)",
    "raw1": "the same for slot 1",
    "raw2": "the same for slot 2",
    "raw3": "the same for slot 3",
    "stored": "a piece of the output is in DRAM",
    "rows_ready": "dt's rows stand beside the other parameters' rows",
    "eps_ready": "eps_col is written",
    "params_turned": "the parameters are turned in PSUM",
    "col_ready": "the turned parameters, and exp(log dt), are in SBUF",
    "hi_ready": "scalar: the hi part of a unit is written",
    "lo_ready": "vector: the lo part of a unit is written, its slot of the ring is free",
    "unit_used": "tensor: the products with a unit are done, its hi and lo slots are free",
    "psum_free_act": "scalar has read a chunk out of its PSUM pair",
    "psum_free_dve": "vector has read a chunk out of its PSUM pair",
    "staged": "vector: a chunk is staged for its turn (squared, gelu or rotary applied)",
    "turned": "tensor: a staged chunk, or a part of x, is turned in PSUM",
    "split_hi": "scalar: the hi part of turned features is written",
    "split_done": "vector: their lo part too, the turned PSUM is free",
    "squared": "scalar: sums of squares of a chunk are written, tmp is free",
    "tot_ready": "vector: the tokens' sums of squares are added up",
    "root_ready": "scalar: root of the mean square + eps",
    "rs_ready": "vector: its reciprocal, the stage's rms factors",
    "gain_ready": "tensor: a chunk of a gain is spread over the partitions",
    "x_ready": "vector: a chunk of the residual stream is up to date",
    "acc_zero": "gpsimd: acc is zero for an MLP's sums",
    "gained": "vector: a chunk of x times the final gain is in acc",
    "out_ready_dve": "vector: the first half of the features of a token tile is normed",
    "out_ready_act": "scalar: the second half",
    "gelu_a": "scalar: the square, and then the sigmoid, of a gelu",
    "gelu_b": "vector: the sigmoid's argument",
    "lam_dot": "vector: the dot products of lambda's vectors",
    "lam_exp": "scalar: exp of lambda's products, or exp(-|lru lambda|)",
    "scores_ready": "tensor: an item's scores are in PSUM",
    "biased": "vector: they are scaled, masked, and their maximum is taken; their banks are free",
    "exp_ready": "scalar: exp and its sums",
    "probs_ready": "vector: what is multiplied with v is there",
    "probs_turned": "tensor: it is turned in PSUM",
    "probs_copied": "vector: and copied to SBUF",
    "mixed": "tensor: the product with v is in PSUM",
    "mixed_out": "scalar: and in acc",
    "mix_ready": "vector: a mixer's whole output is in acc",
    "head_factors": "vector: 1 / rms of each head's output",
    "normed": "gpsimd: the heads' outputs are normed",
    "conv_begun": "scalar: the convolution's first tap and its bias",
    "conv_done": "vector: the other taps",
    "block_done": "tensor: the first half of a unit of the gates",
    "lam_abs": "vector: -|lru lambda|",
    "c_lru_ready": "vector: -8 softplus(-lambda)",
    "gated": "gpsimd: input gate times xc of a part",
    "lru_exp": "scalar: a and tanh(log a) of a part",
    "lru_square": "scalar: a^2",
    "lru_ratio": "vector: a^2 - 1",
    "lru_root": "scalar: sqrt(1 - a^2)",
    "lru_z": "vector: the scan times the y branch",
    "s5_asked": "gpsimd: the arguments of S5's exp and sin, and |lambda|^2",
    "s5_given": "scalar: their exp and sin",
    "s5_recip": "vector: 1 / |lambda|^2",
    "s5_ready": "gpsimd: decays, powers and the scaled B",
    "b_padded": "gpsimd: B of a group at its places among zeros",
    "b_turned": "tensor: turned in PSUM",
    "b_copied": "scalar: and in SBUF",
    "c_padded": "gpsimd: the same for C",
    "c_turned": "tensor: turned in PSUM",
    "c_copied": "scalar: and in SBUF",
    "bu_ready": "tensor: B u of a group is in PSUM",
    "bu_used": "vector: it is read",
    "rot_ready": "gpsimd: a group's rotations exp(i theta t)",
    "rot_used": "vector: they are read",
    "h_ready": "vector: a group's states",
    "y_ready": "tensor: C h of a group is in PSUM",
    "y_read": "vector: y = C h + D u of a group is in u2",
    "y_done": "vector: the last group's too",
    "y_gelu": "vector: gelu of half of y",
    "glu_half": "vector: a half of y times its gate",
    "act_step": "scalar: one instruction's output is there for its next",
    "dve_step": "the same for vector",
    "pool_step": "the same for gpsimd",
}
N_LOADS, N_PARAM_LOADS = 15, 14


Lead = namedtuple("Lead", "kind gain_row gain_col parts x_hi x_lo")
Pending = namedtuple("Pending", "kind ps to width")


class Tally:

    def __init__(self):
        self.n, self.turn, self.stride, self.evacuated_by = {}, None, {}, None

    def add(self, name, k=1):
        self.n[name] = self.n.get(name, 0) + k
        return self.at(name)

    def any(self, name, back=0):
        return self.n.get(name, 0) > back

    def at(self, name, back=0):
        value = self.n.get(name, 0) - back
        return value if self.turn is None or not self.stride.get(name) else self.turn * self.stride[name] + value

    @contextmanager
    def loop(self, turn, trips, **stride):
        before = dict(self.n)
        self.turn, self.stride = turn, stride
        yield
        self.turn, self.stride = None, {}
        for name in self.n:
            grown = self.n[name] - before.get(name, 0)
            assert grown == stride.get(name, 0), (name, grown, stride.get(name, 0))
            self.n[name] += grown * (trips - 1)


def build(nc, i, out):
    x_in = i["x"].rearrange("a (m p) d -> p (a m) d", p=P)
    out_v = out.rearrange("a (m p) d -> p (a m) d", p=P)

    def rows(ap):
        return ap.rearrange("(t p) n -> p t n", p=P)

    w_even_in, w_even_out = rows(i["even_w_in"][0]), rows(i["even_w_out"][0])
    w_odd_in, w_odd_out = rows(i["odd_w_in"][0]), rows(i["odd_w_out"][0])
    w_mlp1 = [rows(i["mlp_w1"][l]) for l in range(2)]
    w_mlp2 = [rows(i["mlp_w2"][l]) for l in range(2)]
    w_gates = i["odd_gate_w"][0].rearrange("g n (t p) e -> p g (n t) e", p=P)
    w_in2, w_glu, w_out2 = rows(i["w_in_2"][0]), rows(i["w_glu_2"][0]), rows(i["w_out_2"][0])
    w_gate2, w_up2, w_down2 = rows(i["w_gate_2"][0]), rows(i["w_up_2"][0]), rows(i["w_down_2"][0])

    with ExitStack() as ctx:
        base = 18688
        K = 1024

        def at(name, offset, shape, dt=F32):
            return nc.alloc_sbuf_tensor_at(name, [P] + shape, dt, offset=base + int(offset * K))

        raw = at("raw", 0, [RAW_SLOTS, KU * CH])
        hi = at("hi", 32, [RING, KU * CH], F32R)
        lo = at("lo", 48, [RING, KU * CH], F32R)
        xt_h, xt_l = at("xt_h", 64, [KT, SEQ], F32R), at("xt_l", 80, [KT, SEQ], F32R)
        ht_h, ht_l = at("ht_h", 96, [KT, SEQ], F32R), at("ht_l", 112, [KT, SEQ], F32R)
        xres, acc = at("xres", 128, [M, D]), at("acc", 144, [M, D])
        stg, tmp = at("stg", 160, [M, CH]), at("tmp", 164, [M, CH])
        col = at("col", 168, [3 * P])
        ident = at("ident", 169.5, [P])
        grows = at("grows", 170, [CH])
        stat = at("stat", 172, [256])
        lamv = at("lamv", 173, [4, 64])
        subg = at("subg", 174, [P])
        sink = at("sink", 174.5, [16])
        small = at("small", 174.5625, [N_SMALL])
        mask = at("mask", 175, [2, SEQ])
        scores = at("scores", 177, [2, 2, SEQ])
        probs = at("probs", 181, [2, 2, SEQ])
        probs_t = at("probs_t", 185, [2, 4, P])
        v_swa, k_swa = at("v_swa", 189, [M, P]), at("k_swa", 190, [2, SEQ])
        prow = at("prow", 190, [3, P])
        qk0, v0 = at("qk0", 96, [24, SEQ]), at("v0", 120, [M, 1024])
        gate_r, gate_i, y_br = at("gate_r", 64, [KT, SEQ]), at("gate_i", 80, [KT, SEQ]), at("y_br", 144, [KT, SEQ])
        lru_a = [at("lru_a0", 177, [4, SEQ]), at("lru_a1", 181, [4, SEQ])]
        lru_s, lru_h = [at("lru_s0", 185, [4, SEQ]), at("lru_s1", 164, [4, SEQ])], at("lru_h", 96, [4, SEQ])
        xc_4 = at("xc_4", 160, [4, SEQ])
        conv_o = at("conv_o", 181, [4, SEQ])
        c_lru = at("c_lru", 189, [16])
        qk2, v2, u2 = at("qk2", 96, [16, SEQ]), at("v2", 112, [M, 1024]), at("u2", 120, [8, SEQ])
        pw = at("pw", 192, [2, 2, SSM_TILES, 16])
        b_bar = at("b_bar", 200, [2, SSM_TILES, 16])
        b_pad, b_t, c_pad = at("b_pad", 177, [2, 4, P]), at("b_t", 181, [2, 4, P]), at("c_pad", 185, [2, 4, P])
        c_t = at("c_t", 160, [2, 4, P])
        g_re, g_im, t_1, t_2 = (at(n, 96 + 4 * j, [4, SEQ]) for j, n in enumerate(("g_re", "g_im", "t_1", "t_2")))
        states = [[at(f"h_{n}{k}", o, [4, SEQ]) for n, o in (("re", a), ("im", b))]
                  for k, (a, b) in enumerate(((64, 68), (84, 164)))]
        rots = [at("rot0", 72, [2, 4, SEQ]), at("rot1", 112, [2, 4, SEQ])]
        rot_t = at("rot_t", 88, [2, 4, SEQ])
        c_all = at("c_all", 80, [2, 8, 64])
        glu_z = [at("glu_z0", 148, [4, SEQ]), at("glu_z1", 156, [4, SEQ])]
        log_dt = at("log_dt", 191.5, [2])
        s5 = at("s5", 177, [24, SSM_TILES])
        b_raw = at("b_raw", 181, [2, SSM_TILES, 16])
        s5_t = at("s5_t", 185, [2, SSM_TILES, 16])
        decay = at("decay", 204, [SSM_TILES])
        assert base + int(205.5 * K) <= 229344

        pair = [ctx.enter_context(nc.psum_tensor(f"pair{k}", [P, M, CH], F32)) for k in range(2)]
        turn_ps = ctx.enter_context(nc.psum_tensor("turn_ps", [P, 4, SEQ], F32))
        misc_ps = ctx.enter_context(nc.psum_tensor("misc_ps", [P, 2, CH], F32))

        score_ps = misc_ps, pair[1]
        turn_all = turn_ps[:].rearrange("p a (b c) -> p (a b) c", c=P).rearrange("p (r j) c -> p r j c", r=2)

        sems = {name: ctx.enter_context(nc.semaphore(name)) for name in SEMAPHORES}

        SS, SSX, TOT, ROOT, RPOST, RS, LAM = 0, 8, 16, 18, 20, 22, 24
        LAMS, MAXN, SUMS, RSUM, ESINK, SUB = 26, 32, 36, 40, 48, 64
        eps_col, nsink, unused = stat[:, 127:128], stat[:, 128:144], stat[:, 144:145]

        def st(a, n=1):
            return stat[:, a:a + n]

        def attention_items(kind):
            pairs = 4 if kind == "dilated" else 8
            return ([(pr, m) for pr in range(pairs) for m in range(M)], 1 if kind == "diff" else 2,
                    64 if kind == "window" else P)

        class Program:

            TURNED = ("copy", "relu2", "gelu", "rope", "up", "kv")
            BY = {"kv": "psum_free_act", "copy": "psum_free_act", "relu2": "psum_free_act", "gelu": "psum_free_act",
                  "rope": "psum_free_act", "tokens": "psum_free_act", "silu": "psum_free_act",
                  "up": "psum_free_dve", "add": "psum_free_dve", "set": "psum_free_dve"}
            STAGED = {"kv": "psum_free_act", "copy": "psum_free_act", "up": "psum_free_dve",
                      "relu2": "staged", "gelu": "staged", "rope": "staged"}

            def __init__(self, eng):
                self.eng, self.T = eng, Tally()
                self.ahead = 1

            @contextmanager
            def loop(self, trips, **stride):
                with self.eng.Fori(0, trips) as turn:
                    with self.T.loop(turn, trips, **stride):
                        yield turn

            def nothing(self, *_, **__):
                pass

            setup = chunk = drain = attention = gates = s5_params = dilated_masks = s5 = glu = final = nothing

            def take_pair(self):
                k = self.T.n.get("chunk", 0) % 2
                self.T.add("chunk")
                return pair[k]

        class Sync(Program):
            def setup(self):
                sp = self.eng
                for dst, src in (
                    (xres[:], x_in),
                    (ident[:], i["consts"][:, K_IDENT:K_IDENT + P]),
                    (prow[0:32, 0], i["pre_mix_g"].rearrange("l (t p) -> (l t) p", p=P)),
                    (prow[32:64, 0], i["pre_mlp_g"].rearrange("l (t p) -> (l t) p", p=P)),
                    (prow[64:128, 0], i["odd_conv_w"][0].rearrange("j (t p) -> (j t) p", p=P)),
                    (prow[0:16, 1], i["odd_conv_b"][0].rearrange("(t p) -> t p", p=P)),
                    (prow[16:48, 1], i["odd_gate_b"][0].rearrange("g n (t p) -> (g n t) p", p=P)),
                    (prow[48:64, 1], i["odd_lru_lambda"][0].rearrange("(t p) -> t p", p=P)),
                    (prow[64:80, 1], i["norm1_g_2"][0].rearrange("(t p) -> t p", p=P)),
                    (prow[80:96, 1], i["norm2_g_2"][0].rearrange("(t p) -> t p", p=P)),
                    (prow[96:104, 1], i["b_glu_2"][0].rearrange("(t p) -> t p", p=P)),
                    (prow[104:112, 1], i["d_skip_2"][0].rearrange("(t g) q -> t (g q)", g=8)),
                    (prow[0:32, 2], i["a_re_2"][0].rearrange("(t g) n -> t (g n)", g=2)),
                    (prow[32:64, 2], i["a_im_2"][0].rearrange("(t g) n -> t (g n)", g=2)),
                    (log_dt[64:96], i["log_dt_2"][0].rearrange("(t g) -> t g", g=2)),
                ):
                    sp.dma_start(dst, src).then_inc(sems["loaded"], 16)
                for k in range(RAW_SLOTS):
                    self.unit(w_even_in[:, KU * k:KU * k + KU, 0:CH])
                for dst, src in (
                    (grows[0:8], i["post_mix_g"].rearrange("l (c n) -> (l c) n", n=CH)),
                    (grows[8:16], i["post_mlp_g"].rearrange("l (c n) -> (l c) n", n=CH)),
                    (grows[16:20], i["final_g_2"].rearrange("(c n) -> c n", n=CH)),
                    (mask[:, 0], i["consts"][:, K_MASK:K_MASK + SEQ]),
                    (mask[:, 1], i["consts"][:, K_MASK + SEQ:K_MASK + 2 * SEQ]),
                    (small[:], i["consts"][:, K_SMALL:K_SMALL + N_SMALL]),
                    (subg[:], i["even_subln_g"].partition_broadcast(P)),
                    (sink[:], i["even_sinks"].partition_broadcast(P)),
                    (lamv[:, 0], i["even_lam_q1"].partition_broadcast(P)),
                    (lamv[:, 1], i["even_lam_k1"].partition_broadcast(P)),
                    (lamv[:, 2], i["even_lam_q2"].partition_broadcast(P)),
                    (lamv[:, 3], i["even_lam_k2"].partition_broadcast(P)),
                    (b_raw[:, 0], i["b_re_2"][0].rearrange("(t g) n q -> (g n) t q", g=2)),
                    (b_raw[:, 1], i["b_im_2"][0].rearrange("(t g) n q -> (g n) t q", g=2)),
                ):
                    sp.dma_start(dst, src).then_inc(sems["params_loaded"], 16)
                self.preloaded = RAW_SLOTS

            def unit(self, src, width=CH, tiles=KU):
                u = self.T.n.get("unit", 0)
                if self.T.turn is not None or u >= RAW_SLOTS:
                    self.eng.wait_ge(sems["lo_ready"], self.T.at("unit", RAW_SLOTS - 1))
                dst = raw[:, u % RAW_SLOTS, 0:tiles * width].rearrange("p (t n) -> p t n", n=width)
                self.eng.dma_start(dst, src).then_inc(sems[f"raw{u % RAW_SLOTS}"], 16)
                self.T.add("unit")

            def chunk(self, kind, w, units=4, width=CH, **_):
                src, t0, col0 = w
                cols = slice(col0, col0 + width) if isinstance(col0, int) else bass.ds(col0, width)
                for j in range(units):
                    if self.preloaded:
                        self.preloaded -= 1
                        continue
                    k = KU * j
                    tiles = slice(t0 + k, t0 + k + KU) if isinstance(t0, int) else bass.ds(t0 + k, KU)
                    self.unit(src[:, tiles, cols], width)

            def dilated_masks(self):
                self.eng.wait_ge(sems["mixed_out"], self.T.add("mixed_out", 32))
                for k in range(2):
                    a = K_MASK + (2 + k) * SEQ
                    self.eng.dma_start(mask[:, k], i["consts"][:, a:a + SEQ]).then_inc(sems["masks_loaded"], 16)

            def gates(self):
                for g in range(2):
                    for half in range(2):
                        self.unit(w_gates[:, g, 8 * half:8 * half + 8], 2 * P, 8)

            def s5(self):
                for half in range(2):
                    for k in range(2):
                        self.unit(w_glu[:, KU * k:KU * k + KU, half * CH:half * CH + CH])
                self.eng.wait_ge(sems["unit_used"], self.T.n["unit"] - 4)
                for ri, name in enumerate(("c_re_2", "c_im_2")):
                    self.eng.dma_start(c_all[:, ri], i[name][0].rearrange("(t g) q n -> (g q) t n", g=8)
                                       ).then_inc(sems["c_loaded"], 16)

            def final(self):
                for m in range(M):
                    for half, who in enumerate(("out_ready_dve", "out_ready_act")):
                        self.eng.wait_ge(sems[who], self.T.add(who))
                        cols = slice(half * D // 2, (half + 1) * D // 2)
                        self.eng.dma_start(out_v[:, m, cols], acc[:, m, cols]).then_inc(sems["stored"], 16)
                self.eng.wait_ge(sems["stored"], 16 * 2 * M)

        class Scalar(Program):
            unsquared = None

            def setup(self):
                self.eng.wait_ge(sems["loaded"], 16 * N_LOADS)
                self.eng.wait_ge(sems["eps_ready"], 1)
                self.eng.wait_ge(sems["params_turned"], self.T.add("params_turned"))
                for a, n in ((0, P + 112), (2 * P, 96)):
                    ins = nc.scalar.activation(col[:, a:a + n], misc_ps[:, 0, a:a + n], ACT.Copy)
                ins.then_inc(sems["act_step"], 1)
                self.eng.wait_ge(sems["act_step"], self.T.add("act_step"))
                nc.scalar.activation(s5[:, 0], col[:, C_LDT:C_LDT + 32], ACT.Exp).then_inc(sems["col_ready"], 1)
                self.T.add("col_ready")
                self.conv()

            def conv(self, cols=KU * CH):
                T, u = self.T, self.T.n.get("unit", 0)
                slot, r = u % RAW_SLOTS, u % RING
                self.eng.wait_ge(sems[f"raw{slot}"], T.add(f"raw{slot}", 16))
                if T.turn is not None or u >= RING:
                    self.eng.wait_ge(sems["unit_used"], T.at("unit", RING - 1))
                nc.scalar.activation(hi[:, r, 0:cols], raw[:, slot, 0:cols], ACT.Copy).then_inc(sems["hi_ready"], 1)
                T.add("unit")

            def evac(self, kind, ps, done, dst=None, width=CH):
                T, by = self.T, self.BY[kind]
                if kind == "kv":
                    self.eng.wait_ge(sems["unit_used"], done)
                    self.eng.wait_ge(sems["turned"], T.at("turned"))
                    for m in range(M):
                        for c, to in ((0, stg[:, m, 0:P]), (P, v_swa[:, m])):
                            nc.scalar.activation(to, ps[:, m, c:c + P], ACT.Copy, scale=st(RS + m))
                        for c in range(2):
                            a = nc.scalar.activation(stg[:, m, P + 64 * c:P + 64 * c + 64],
                                                     ps[:, m, 64 - 64 * c:128 - 64 * c], ACT.Copy, scale=st(RS + m))
                    a.then_inc(sems[by], 1)
                    T.add(by)
                elif by == "psum_free_act":
                    self.eng.wait_ge(sems["unit_used"], done)
                    self.eng.wait_ge(sems["turned"], T.at("turned"))
                    if kind == "gelu":
                        self.eng.wait_ge(sems["staged"], T.at("staged"))
                    func = {"relu2": ACT.Relu, "silu": ACT.Silu}.get(kind, ACT.Copy)
                    for m in range(M):
                        to = stg[:, m, 0:width] if dst is None else dst[:, m]
                        a = nc.scalar.activation(to, ps[:, m, 0:width], func, scale=st(RS + m))
                    a.then_inc(sems[by], 1)
                    T.add(by)
                else:
                    T.add(by)
                if kind == "gelu":
                    self.eng.wait_ge(sems[by], T.at(by))
                    nc.scalar.activation(tmp[:], stg[:], ACT.Square).then_inc(sems["gelu_a"], 1)
                    T.add("gelu_a")
                    self.eng.wait_ge(sems["gelu_b"], T.add("gelu_b"))
                    nc.scalar.activation(tmp[:], tmp[:], ACT.Sigmoid).then_inc(sems["gelu_a"], 1)
                    T.add("gelu_a")
                if kind in ("gelu", "relu2", "rope"):
                    T.add("staged")

            def square_sums(self, n, final=False):
                if final:
                    self.eng.wait_ge(sems["x_ready"], self.T.add("x_ready"))
                self.eng.wait_ge(sems["psum_free_dve"], self.T.at("psum_free_dve"))
                self.eng.wait_ge(sems["squared"], self.T.at("squared"))
                src, sums = (xres, SSX) if final else (acc, SS)
                for m in range(M):
                    a = nc.scalar.activation(tmp[:, m], src[:, m, n * CH:(n + 1) * CH], ACT.Square,
                                             accum_out=st(sums + 4 * m + n))
                a.then_inc(sems["squared"], 1)
                self.T.add("squared")

            def split(self, to, next_cols=0):
                T = self.T
                T.add("turned")
                if to[0] == "conv":
                    self.eng.wait_ge(sems["turned"], T.at("turned"))
                    self.eng.wait_ge(sems["split_done"], T.at("split_done"))
                    for k in range(4):
                        w, b = C_CONV_W + 48 + to[1] + k, C_CONV_B + to[1] + k
                        a = nc.scalar.activation(conv_o[:, k], turn_ps[:, k], ACT.Identity, scale=col[:, w:w + 1],
                                                 bias=col[:, b:b + 1])
                    a.then_inc(sems["conv_begun"], 1)
                    if next_cols:
                        self.conv(next_cols)
                    self.eng.wait_ge(sems["conv_done"], T.add("conv_done"))
                    nc.scalar.activation(ht_h[:, to[1]:to[1] + 4], conv_o[:], ACT.Copy).then_inc(sems["split_hi"], 1)
                    T.add("split_hi")
                elif to[0] is not None:
                    self.eng.wait_ge(sems["turned"], T.at("turned"))
                    nc.scalar.activation(to[0], turn_ps[:], ACT.Copy).then_inc(sems["split_hi"], 1)
                    T.add("split_hi")
                T.add("split_done")

            def chunk(self, kind, w, units=4, width=CH, prev=None, lead=None, to=None, dst=None, n=0, next_cols=KU * CH,
                      ss=True, more=False, final=False, **_):
                T, ps = self.T, self.take_pair()
                done = T.at("unit", 1)
                if lead:
                    self.lead(lead, units)
                else:
                    if self.ahead == 1:
                        self.conv(KU * width)
                    if prev:
                        self.evac(prev.kind, prev.ps, done, width=prev.width)
                    for _j in range(2, units):
                        self.conv(KU * width)
                        if self.unsquared is not None:
                            self.square_sums(self.unsquared, final)
                            self.unsquared = None
                    if prev:
                        self.split(prev.to, next_cols)
                if next_cols and not (prev and prev.to[0] == "conv"):
                    self.conv(next_cols)
                self.ahead = 1
                if kind in self.TURNED:
                    return Pending(kind, ps, to, width)
                if more:
                    self.conv()
                    self.ahead = 2
                self.evac(kind, ps, T.at("unit", self.ahead if next_cols else 0), dst, width)
                if kind in ("add", "set") and (ss or final):
                    if more:
                        self.unsquared = n
                    else:
                        self.square_sums(n, final)

            def drain(self, prev):
                self.evac(prev.kind, prev.ps, self.T.at("unit", 1), width=prev.width)
                self.split(prev.to)

            def lead(self, lead, units):
                kind = lead.kind
                if kind == "lru":
                    return self.lru_lead()
                if kind == "glu":
                    return self.glu_lead()
                if kind == "post":
                    self.root(D)
                for n in range(4):
                    if n < lead.parts:
                        self.part(lead, n)
                    if 1 <= n and n < units:
                        self.conv()
                if kind in ("first", "post", "plain"):
                    self.root(D)
                    self.eng.wait_ge(sems["rs_ready"], self.T.add("rs_ready"))

            def root(self, width):
                self.eng.wait_ge(sems["tot_ready"], self.T.add("tot_ready"))
                ins = nc.scalar.activation(st(ROOT, M), st(TOT, M), ACT.Sqrt, scale=1.0 / width, bias=eps_col)
                ins.then_inc(sems["root_ready"], 1)
                self.T.add("root_ready")

            def part(self, lead, n):
                kind, _, c0, _, th, _ = lead
                T = self.T
                if kind in ("post", "plain"):
                    self.eng.wait_ge(sems["x_ready"], T.add("x_ready"))
                if kind in ("first", "post", "plain"):
                    if T.any("squared"):
                        self.eng.wait_ge(sems["squared"], T.at("squared"))
                    for m in range(M):
                        a = nc.scalar.activation(tmp[:, m], xres[:, m, n * CH:(n + 1) * CH], ACT.Square,
                                                 accum_out=st(SSX + 4 * m + n))
                    a.then_inc(sems["squared"], 1)
                    T.add("squared")
                self.eng.wait_ge(sems["turned"], T.add("turned"))
                src = self.part_psum(n)
                if c0 is None:
                    a = nc.scalar.activation(th[:, 4 * n:4 * n + 4], src, ACT.Copy)
                else:
                    for k in range(4):
                        c = c0 + 4 * n + k
                        a = nc.scalar.activation(th[:, 4 * n + k], src[:, k], ACT.Copy, scale=col[:, c:c + 1])
                a.then_inc(sems["split_hi"], 1)
                T.add("split_hi")
                T.add("split_done")

            def part_psum(self, n):
                if n % 2 == 0:
                    return turn_ps[:]
                return pair[self.T.n["chunk"] % 2][:].rearrange("p m (k s) -> p (m k) s", s=SEQ)

            def lru_decay(self, q):
                T, b = self.T, q % 2
                if q == 0:
                    self.eng.wait_ge(sems["c_lru_ready"], T.add("c_lru_ready"))
                for k in range(4):
                    t = 4 * q + k
                    nc.scalar.activation(lru_a[b][:, k], gate_r[:, t], ACT.Exp, scale=c_lru[:, t:t + 1])
                    a = nc.scalar.activation(gate_r[:, t], gate_r[:, t], ACT.Tanh, scale=c_lru[:, t:t + 1])
                a.then_inc(sems["lru_exp"], 1)
                self.eng.wait_ge(sems["lru_exp"], T.add("lru_exp"))
                nc.scalar.activation(lru_s[b][:], lru_a[b][:], ACT.Square).then_inc(sems["lru_square"], 1)

            def lru_root(self, q):
                self.eng.wait_ge(sems["lru_ratio"], self.T.add("lru_ratio"))
                s = lru_s[q % 2][:]
                nc.scalar.activation(s, s, ACT.Sqrt, scale=-1.0).then_inc(sems["lru_root"], 1)

            def lru_hi(self, q):
                tiles = slice(4 * q, 4 * q + 4)
                self.eng.wait_ge(sems["lru_z"], self.T.add("lru_z"))
                nc.scalar.activation(xt_h[:, tiles], y_br[:, tiles], ACT.Copy).then_inc(sems["split_hi"], 1)
                self.T.add("split_hi")
                self.T.add("split_done")

            def lru_lead(self):
                self.lru_hi(0)
                self.lru_root(1)
                self.conv()
                self.lru_hi(1)
                self.lru_decay(2)
                self.lru_decay(3)
                self.conv()
                self.lru_root(2)
                self.lru_root(3)
                self.lru_hi(2)
                self.conv()
                self.lru_hi(3)

            def gates(self):
                T = self.T
                self.eng.wait_ge(sems["lam_abs"], T.add("lam_abs"))
                nc.scalar.activation(tmp[:, 0, 16:32], tmp[:, 0, 0:16], ACT.Exp).then_inc(sems["lam_exp"], 1)
                T.add("lam_exp")
                for j in range(4):
                    if j < 3:
                        self.conv()
                    else:
                        self.lru_decay(1)
                        self.lru_root(0)
                    for b in range(2):
                        ps, g = self.take_pair(), j // 2
                        if b == 0:
                            self.eng.wait_ge(sems["block_done"], T.add("block_done"))
                        else:
                            self.eng.wait_ge(sems["unit_used"], T.n["unit"] - (1 if j < 3 else 0))
                        for k in range(4):
                            t = 8 * (j % 2) + 4 * b + k
                            c = C_GATE_B + 16 * g + t
                            a = nc.scalar.activation((gate_r, gate_i)[g][:, t],
                                                     ps[:, k // 2, (k % 2) * SEQ:(k % 2 + 1) * SEQ], ACT.Sigmoid,
                                                     bias=col[:, c:c + 1])
                        a.then_inc(sems["psum_free_act"], 1)
                        T.add("psum_free_act")
                    if j == 2:
                        self.eng.wait_ge(sems["psum_free_act"], T.at("psum_free_act"))
                        self.lru_decay(0)
                self.conv()

            def attention(self, kind):
                T = self.T
                items, heads, per = attention_items(kind)
                if kind == "diff":
                    self.eng.wait_ge(sems["lam_dot"], T.add("lam_dot"))
                    nc.scalar.activation(st(LAMS, 2), st(LAMS, 2), ACT.Exp).then_inc(sems["lam_exp"], 1)
                    T.add("lam_exp")

                def out_of_psum(k):
                    pr, m = items[k]
                    self.eng.wait_ge(sems["mixed"], T.add("mixed"))
                    c = pr * P if kind != "dilated" else pr * 2 * P
                    if kind == "diff":
                        nc.scalar.activation((stg, tmp)[m][:].rearrange("p m n -> p (m n)")[:, c:c + P],
                                             pair[0][:, k % 2, 0:P], ACT.Square, accum_out=st(SUB + 8 * m + pr))
                        a = nc.scalar.activation(acc[:, m, c:c + P], pair[0][:, k % 2, 0:P], ACT.Copy)
                    else:
                        c += 1024 if kind == "window" else 0
                        for s in range(2):
                            a = nc.scalar.activation(acc[:, m, c + s * per:c + (s + 1) * per],
                                                     pair[0][:, k % 2, s * per:(s + 1) * per], ACT.Copy,
                                                     scale=st(RSUM + 2 * (k % 4) + s))
                    a.then_inc(sems["mixed_out"], 1)
                    T.add("mixed_out")

                for k, (pr, m) in enumerate(items):
                    self.eng.wait_ge(sems["biased"], T.add("biased"))
                    keys = (m + 1) * P
                    b, q = k % 2, 2 * (k % 2)
                    for s in range(2):
                        sc = scores[:, b, s, 0:keys]
                        a = nc.scalar.activation(sc, sc, ACT.Exp, bias=st(MAXN + q + s),
                                                 accum_out=st(SUMS + q + s))
                    if kind == "window":
                        for s in range(2):
                            a = nc.scalar.activation(st(ESINK + q + s), sink[:, 2 * pr + s:2 * pr + s + 1], ACT.Exp,
                                                     bias=st(MAXN + q + s))
                    a.then_inc(sems["exp_ready"], 1)
                    T.add("exp_ready")
                    if k >= 2:
                        out_of_psum(k - 2)
                out_of_psum(len(items) - 2)
                out_of_psum(len(items) - 1)
                if kind == "diff":
                    self.eng.wait_ge(sems["mixed_out"], T.at("mixed_out"))
                    a = nc.scalar.activation(st(SUB, 16), st(SUB, 16), ACT.Sqrt, scale=1.0 / P, bias=eps_col)
                    a.then_inc(sems["root_ready"], 1)
                    T.add("root_ready")

            def s5_params(self):
                self.eng.wait_ge(sems["s5_asked"], self.T.add("s5_asked"))
                nc.scalar.activation(decay[:], s5[:, 1], ACT.Exp)
                nc.scalar.activation(s5[:, 8], s5[:, 5], ACT.Sin)
                nc.scalar.activation(s5[:, 9], s5[:, 6], ACT.Sin).then_inc(sems["s5_given"], 1)
                self.T.add("s5_given")

            def s5(self):
                T = self.T
                for g in range(8):
                    self.eng.wait_ge(sems["b_turned"], T.add("b_turned"))
                    nc.scalar.activation(b_t[:], turn_all, ACT.Copy).then_inc(sems["b_copied"], 1)
                    T.add("b_copied")
                    self.eng.wait_ge(sems["c_turned"], T.add("c_turned"))
                    nc.scalar.activation(c_t[:, 0], turn_all[:, 0], ACT.Copy)
                    nc.scalar.activation(c_t[:, 1], turn_all[:, 1], ACT.Copy, scale=-1.0).then_inc(sems["c_copied"], 1)
                    T.add("c_copied")
                    if g == 5:
                        self.eng.wait_ge(sems["y_read"], 4)
                        self.gelu_square(0)
                    if g == 6:
                        self.gelu_sigmoid(0)
                    if g == 7:
                        self.eng.wait_ge(sems["y_ready"], 7)
                        self.gelu_hi(0)
                self.conv()
                self.eng.wait_ge(sems["y_done"], T.add("y_done"))
                self.gelu_square(1)
                self.attention_hi(0)
                self.gelu_sigmoid(1)
                self.gelu_hi(1)
                self.attention_hi(1)

            def gelu_square(self, half):
                u = u2[:, 4 * half:4 * half + 4]
                nc.scalar.activation(glu_z[half][:], u, ACT.Square).then_inc(sems["gelu_a"], 1)
                self.T.add("gelu_a")

            def gelu_sigmoid(self, half):
                z = glu_z[half][:]
                self.eng.wait_ge(sems["gelu_b"], self.T.add("gelu_b"))
                nc.scalar.activation(z, z, ACT.Sigmoid).then_inc(sems["gelu_a"], 1)
                self.T.add("gelu_a")

            def gelu_hi(self, half):
                tiles = slice(4 * half, 4 * half + 4)
                self.eng.wait_ge(sems["y_gelu"], self.T.add("y_gelu"))
                nc.scalar.activation(xt_h[:, tiles], u2[:, tiles], ACT.Copy).then_inc(sems["split_hi"], 1)
                self.T.add("split_hi")
                self.T.add("split_done")

            def attention_hi(self, n):
                self.eng.wait_ge(sems["turned"], self.T.add("turned"))
                nc.scalar.activation(xt_h[:, 8 + 4 * n:12 + 4 * n], turn_ps[:], ACT.Copy).then_inc(sems["split_hi"], 1)
                self.T.add("split_hi")
                self.T.add("split_done")

            def glu(self):
                self.conv()
                self.conv()
                self.glu_ps = [self.take_pair(), self.take_pair()]
                self.eng.wait_ge(sems["unit_used"], self.T.at("unit", 2))
                self.glu_gate(0)
                self.conv()

            def glu_gate(self, half):
                flat = self.glu_ps[half][:].rearrange("p m (k s) -> p (m k) s", s=SEQ)
                for e in range(4):
                    c = C_BGLU + 4 * half + e
                    a = nc.scalar.activation(glu_z[half][:, e], flat[:, e], ACT.Sigmoid, bias=col[:, c:c + 1])
                a.then_inc(sems["psum_free_act"], 1)
                self.T.add("psum_free_act")

            def glu_lead(self):
                T = self.T
                self.conv()
                self.eng.wait_ge(sems["unit_used"], T.at("unit", 2))
                self.glu_gate(1)
                self.eng.wait_ge(sems["glu_half"], 2)
                for half in range(2):
                    a = nc.scalar.activation(xt_h[:, 4 * half:4 * half + 4], glu_z[half][:], ACT.Copy)
                a.then_inc(sems["split_hi"], 1)
                T.add("split_hi")
                T.add("split_done")
                self.conv()
                self.conv()

            def final(self):
                self.root(D)
                self.eng.wait_ge(sems["rs_ready"], self.T.add("rs_ready"))
                for m in range(M):
                    y = acc[:, m, D // 2:D]
                    nc.scalar.activation(y, y, ACT.Copy, scale=st(RS + m)).then_inc(sems["out_ready_act"], 1)

        class Vector(Program):
            ungained = None

            def setup(self):
                v = self.eng
                v.wait_ge(sems["loaded"], 16 * N_LOADS)
                for g in range(2):
                    a = nc.vector.tensor_copy(prow[64:96, 2, 64 * g:64 * g + 64],
                                              log_dt[64:96, g:g + 1].to_broadcast([32, 64]))
                a.then_inc(sems["rows_ready"], 1)
                self.T.add("rows_ready")
                nc.vector.memset(eps_col, EPS).then_inc(sems["eps_ready"], 1)
                self.conv()
                self.eng.wait_ge(sems["col_ready"], self.T.add("col_ready"))

            def conv(self, cols=KU * CH):
                T, u = self.T, self.T.n.get("unit", 0)
                slot, r = u % RAW_SLOTS, u % RING
                self.eng.wait_ge(sems["hi_ready"], T.at("unit", -1))
                nc.vector.tensor_tensor(lo[:, r, 0:cols], raw[:, slot, 0:cols], hi[:, r, 0:cols].bitcast(F32),
                                        ALU.subtract).then_inc(sems["lo_ready"], 1)
                T.add("unit")

            def evac(self, kind, ps, done, dst=None, width=CH):
                T, by = self.T, self.BY[kind]
                if by == "psum_free_act":
                    T.add(by)
                    if kind == "relu2":
                        self.eng.wait_ge(sems[by], T.at(by))
                        nc.vector.tensor_tensor(stg[:], stg[:], stg[:], ALU.mult).then_inc(sems["staged"], 1)
                        T.add("staged")
                    elif kind == "gelu":
                        self.eng.wait_ge(sems["gelu_a"], T.add("gelu_a"))
                        ins = nc.vector.tensor_scalar(tmp[:], tmp[:], GELU_3, GELU_1, ALU.mult, ALU.add)
                        ins.then_inc(sems["dve_step"], 1)
                        self.eng.wait_ge(sems["dve_step"], T.add("dve_step"))
                        nc.vector.tensor_tensor(tmp[:], tmp[:], stg[:], ALU.mult).then_inc(sems["gelu_b"], 1)
                        T.add("gelu_b")
                        self.eng.wait_ge(sems["gelu_a"], T.add("gelu_a"))
                        nc.vector.tensor_tensor(stg[:], stg[:], tmp[:], ALU.mult).then_inc(sems["staged"], 1)
                        T.add("staged")
                    elif kind == "rope":
                        self.rope()
                    return
                self.eng.wait_ge(sems["unit_used"], done)
                if kind == "up":
                    self.eng.wait_ge(sems["psum_free_act"], T.at("psum_free_act"))
                if kind == "add":
                    self.eng.wait_ge(sems["acc_zero"], T.at("acc_zero"))
                for m in range(M):
                    if kind == "up":
                        a = nc.vector.scalar_tensor_tensor(stg[:, m], ps[:, m], st(RS + m), stg[:, m],
                                                           ALU.mult, ALU.mult)
                    elif kind == "set":
                        a = nc.vector.tensor_copy(dst[:, m], ps[:, m])
                    else:
                        a = nc.vector.tensor_tensor(dst[:, m], ps[:, m], dst[:, m], ALU.add)
                a.then_inc(sems[by], 1)
                T.add(by)

            def rope(self):
                self.eng.wait_ge(sems["psum_free_act"], self.T.at("psum_free_act"))
                heads = stg[:].rearrange("p m (h d) -> p m h d", d=P)
                x1, x2 = heads[:, :, :, 0:16], heads[:, :, :, 16:32]
                q = tmp[:].rearrange("p m n -> p (m n)")[:, 0:512].rearrange("p (a m h d) -> p a m h d", a=4, m=M, h=4)
                for a, (xx, t) in enumerate(((x1, K_COS), (x2, K_SIN), (x2, K_COS), (x1, K_SIN))):
                    for m in range(M):
                        c = small[:, t + 16 * m:t + 16 * m + 16].unsqueeze(1).to_broadcast([P, 4, 16])
                        ins = nc.vector.tensor_tensor(q[:, a, m], xx[:, m], c, ALU.mult)
                ins.then_inc(sems["dve_step"], 1)
                self.eng.wait_ge(sems["dve_step"], self.T.add("dve_step"))
                for m in range(M):
                    nc.vector.tensor_tensor(x1[:, m], q[:, 0, m], q[:, 1, m], ALU.subtract)
                    ins = nc.vector.tensor_tensor(x2[:, m], q[:, 2, m], q[:, 3, m], ALU.add)
                ins.then_inc(sems["staged"], 1)
                self.T.add("staged")

            def split(self, to, next_cols=0):
                T = self.T
                T.add("turned")
                if to[0] == "conv":
                    return self.causal_conv(to[1], next_cols)
                if to[0] is None:
                    self.eng.wait_ge(sems["turned"], T.at("turned"))
                    a = nc.vector.tensor_copy(to[1], turn_ps[:, 0:to[1].shape[1]])
                else:
                    self.eng.wait_ge(sems["split_hi"], T.add("split_hi"))
                    a = nc.vector.tensor_tensor(to[1], turn_ps[:], to[0].bitcast(F32), ALU.subtract)
                a.then_inc(sems["split_done"], 1)
                T.add("split_done")

            def causal_conv(self, t0, next_cols):
                T = self.T
                self.eng.wait_ge(sems["conv_begun"], T.add("conv_begun"))
                for j in range(3):
                    if j:
                        a.then_inc(sems["dve_step"], 1)
                        self.eng.wait_ge(sems["dve_step"], T.add("dve_step"))
                    if j == 2 and next_cols:
                        self.conv(next_cols)
                    s = 3 - j
                    for k in range(4):
                        c = C_CONV_W + 16 * j + t0 + k
                        a = nc.vector.scalar_tensor_tensor(conv_o[:, k, s:SEQ], turn_ps[:, k, 0:SEQ - s],
                                                           col[:, c:c + 1], conv_o[:, k, s:SEQ], ALU.mult, ALU.add)
                a.then_inc(sems["conv_done"], 1)
                T.add("conv_done")
                self.eng.wait_ge(sems["split_hi"], T.add("split_hi"))
                nc.vector.tensor_tensor(ht_l[:, t0:t0 + 4], conv_o[:], ht_h[:, t0:t0 + 4].bitcast(F32),
                                        ALU.subtract).then_inc(sems["split_done"], 1)
                T.add("split_done")

            def chunk(self, kind, w, units=4, width=CH, prev=None, lead=None, to=None, dst=None, n=0, next_cols=KU * CH,
                      ss=True, more=False, final=False, **_):
                T, ps = self.T, self.take_pair()
                done = T.at("unit", 1)
                if lead:
                    if kind in ("relu2", "silu"):
                        T.add("acc_zero")
                    self.lead(lead, units)
                else:
                    if self.ahead == 1:
                        self.conv(KU * width)
                    if prev:
                        self.evac(prev.kind, prev.ps, done, width=prev.width)
                    for _j in range(2, units):
                        self.conv(KU * width)
                        if self.ungained is not None:
                            self.gained(self.ungained)
                            self.ungained = None
                    if prev:
                        self.split(prev.to, next_cols)
                if next_cols and not (prev and prev.to[0] == "conv"):
                    self.conv(next_cols)
                self.ahead = 1
                if kind in self.TURNED:
                    return Pending(kind, ps, to, width)
                if more:
                    self.conv()
                    self.ahead = 2
                self.evac(kind, ps, T.at("unit", self.ahead if next_cols else 0), dst, width)
                if kind in ("add", "set") and ss:
                    T.add("squared")
                if final and more:
                    self.ungained = n
                elif final:
                    self.gained(n)

            def drain(self, prev):
                self.evac(prev.kind, prev.ps, self.T.at("unit", 1), width=prev.width)
                self.split(prev.to)

            def lead(self, lead, units):
                kind, parts = lead.kind, lead.parts
                if kind == "lru":
                    return self.lru_lead()
                if kind == "glu":
                    return self.glu_lead()
                if kind == "post":
                    self.eng.wait_ge(sems["squared"], self.T.at("squared"))
                    self.norm_factor(SS, RPOST)
                if kind in ("post", "plain"):
                    self.residual(kind, 0)
                    self.residual(kind, 1)
                    self.lo_part(lead, 0)
                    self.residual(kind, 2)
                    self.lo_part(lead, 1)
                    self.conv()
                    self.residual(kind, 3)
                    self.lo_part(lead, 2)
                    self.conv()
                    self.lo_part(lead, 3)
                    self.conv()
                else:
                    for n in range(4):
                        if n < parts:
                            self.lo_part(lead, n)
                        if 1 <= n < units:
                            self.conv()
                if kind in ("first", "post", "plain"):
                    self.eng.wait_ge(sems["squared"], self.T.add("squared", 4))
                    self.norm_factor(SSX, RS, "rs_ready")

            def norm_factor(self, sums, dst, tell=None):
                T = self.T
                nc.vector.tensor_reduce(st(TOT, M), st(sums, 8).rearrange("p (m n) -> p m n", m=M), AX_X,
                                        ALU.add).then_inc(sems["tot_ready"], 1)
                T.add("tot_ready")
                self.eng.wait_ge(sems["root_ready"], T.add("root_ready"))
                ins = nc.vector.reciprocal(st(dst, M), st(ROOT, M))
                if tell:
                    ins.then_inc(sems[tell], 1)
                    T.add(tell)
                else:
                    ins.then_inc(sems["dve_step"], 1)
                    self.eng.wait_ge(sems["dve_step"], T.add("dve_step"))

            def residual(self, kind, n):
                T, cols = self.T, slice(n * CH, (n + 1) * CH)
                if kind == "post":
                    self.eng.wait_ge(sems["gain_ready"], T.add("gain_ready"))
                    for m in range(M):
                        ins = nc.vector.scalar_tensor_tensor(acc[:, m, cols], acc[:, m, cols], st(RPOST + m),
                                                             misc_ps[:, n % 2], ALU.mult, ALU.mult)
                    ins.then_inc(sems["dve_step"], 1)
                    self.eng.wait_ge(sems["dve_step"], T.add("dve_step"))
                elif n == 0:
                    self.eng.wait_ge(sems["psum_free_dve"], T.at("psum_free_dve"))
                ins = nc.vector.tensor_tensor(xres[:, :, cols], xres[:, :, cols], acc[:, :, cols], ALU.add)
                ins.then_inc(sems["x_ready"], 1)
                T.add("x_ready")

            def lo_part(self, lead, n):
                _, _, c0, _, th, tl = lead
                T, src = self.T, Scalar.part_psum(self, n)
                T.add("turned")
                self.eng.wait_ge(sems["split_hi"], T.add("split_hi"))
                if c0 is None:
                    a = nc.vector.tensor_tensor(tl[:, 4 * n:4 * n + 4], src, th[:, 4 * n:4 * n + 4].bitcast(F32),
                                                ALU.subtract)
                else:
                    for k in range(4):
                        t, c = 4 * n + k, c0 + 4 * n + k
                        a = nc.vector.scalar_tensor_tensor(tl[:, t], src[:, k], col[:, c:c + 1],
                                                           th[:, t].bitcast(F32), ALU.mult, ALU.subtract)
                a.then_inc(sems["split_done"], 1)
                T.add("split_done")

            def lru_constant(self):
                T = self.T
                z = [tmp[:, 0, 16 * k:16 * k + 16] for k in range(8)]
                lam = col[:, C_LAM:C_LAM + 16]
                self.eng.wait_ge(sems["split_done"], T.at("split_done"))
                nc.vector.tensor_scalar(z[2], lam, -1.0, None, ALU.mult).then_inc(sems["dve_step"], 1)
                self.eng.wait_ge(sems["dve_step"], T.add("dve_step"))
                nc.vector.tensor_tensor(z[0], lam, z[2], ALU.min).then_inc(sems["lam_abs"], 1)
                T.add("lam_abs")
                self.eng.wait_ge(sems["lam_exp"], T.add("lam_exp"))
                nc.vector.tensor_scalar(z[3], z[1], 2.0, None, ALU.add).then_inc(sems["dve_step"], 1)
                self.eng.wait_ge(sems["dve_step"], T.add("dve_step"))
                nc.vector.reciprocal(z[4], z[3]).then_inc(sems["dve_step"], 1)
                self.eng.wait_ge(sems["dve_step"], T.add("dve_step"))
                nc.vector.tensor_tensor(z[3], z[1], z[4], ALU.mult).then_inc(sems["dve_step"], 1)
                self.eng.wait_ge(sems["dve_step"], T.add("dve_step"))
                nc.vector.tensor_tensor(z[4], z[3], z[3], ALU.mult).then_inc(sems["dve_step"], 1)
                self.eng.wait_ge(sems["dve_step"], T.add("dve_step"))
                nc.vector.tensor_scalar(z[5], z[4], 1.0 / 17, None, ALU.mult).then_inc(sems["dve_step"], 1)
                self.eng.wait_ge(sems["dve_step"], T.add("dve_step"))
                for odd in (15, 13, 11, 9, 7, 5, 3):
                    ins = nc.vector.scalar_tensor_tensor(z[5], z[5], 1.0 / odd, z[4], ALU.add, ALU.mult)
                    ins.then_inc(sems["dve_step"], 1)
                    self.eng.wait_ge(sems["dve_step"], T.add("dve_step"))
                nc.vector.scalar_tensor_tensor(z[5], z[5], 1.0, z[3], ALU.add, ALU.mult).then_inc(sems["dve_step"], 1)
                self.eng.wait_ge(sems["dve_step"], T.add("dve_step"))
                nc.vector.tensor_scalar(z[6], lam, 0.0, 8.0, ALU.min, ALU.mult).then_inc(sems["dve_step"], 1)
                self.eng.wait_ge(sems["dve_step"], T.add("dve_step"))
                ins = nc.vector.scalar_tensor_tensor(c_lru[:], z[5], -16.0, z[6], ALU.mult, ALU.add)
                ins.then_inc(sems["c_lru_ready"], 1)
                T.add("c_lru_ready")

            def lru_ratio(self, q):
                self.eng.wait_ge(sems["lru_square"], self.T.add("lru_square"))
                s, t = lru_s[q % 2][:], gate_r[:, 4 * q:4 * q + 4]
                nc.vector.scalar_tensor_tensor(s, s, 1.0, t, ALU.add, ALU.mult).then_inc(sems["dve_step"], 1)
                self.eng.wait_ge(sems["dve_step"], self.T.add("dve_step"))
                nc.vector.tensor_scalar(s, s, -2.0 ** -116, None, ALU.min).then_inc(sems["lru_ratio"], 1)
                self.T.add("lru_ratio")

            def lru_scan(self, q):
                T, s, tiles = self.T, lru_s[q % 2], slice(4 * q, 4 * q + 4)
                self.eng.wait_ge(sems["gated"], T.add("gated"))
                self.eng.wait_ge(sems["lru_root"], T.add("lru_root"))
                nc.vector.tensor_tensor(s[:], s[:], gate_i[:, tiles], ALU.mult).then_inc(sems["dve_step"], 1)
                self.eng.wait_ge(sems["dve_step"], T.add("dve_step"))
                for k in range(4):
                    a = nc.vector.tensor_tensor_scan(lru_h[:, k], lru_a[q % 2][:, k], s[:, k], 0.0, ALU.mult, ALU.add)
                a.then_inc(sems["dve_step"], 1)
                self.eng.wait_ge(sems["dve_step"], T.add("dve_step"))
                y = y_br[:, tiles]
                nc.vector.tensor_tensor(y, lru_h[:], y, ALU.mult).then_inc(sems["lru_z"], 1)
                T.add("lru_z")

            def lru_lo(self, q):
                tiles = slice(4 * q, 4 * q + 4)
                self.eng.wait_ge(sems["split_hi"], self.T.add("split_hi"))
                a = nc.vector.tensor_tensor(xt_l[:, tiles], y_br[:, tiles], xt_h[:, tiles].bitcast(F32), ALU.subtract)
                a.then_inc(sems["split_done"], 1)
                self.T.add("split_done")

            def lru_lead(self):
                self.lru_lo(0)
                self.lru_scan(1)
                self.conv()
                self.lru_lo(1)
                self.lru_ratio(2)
                self.lru_ratio(3)
                self.conv()
                self.lru_scan(2)
                self.lru_lo(2)
                self.lru_scan(3)
                self.conv()
                self.lru_lo(3)

            def gates(self):
                self.lru_constant()
                for j in range(4):
                    if j < 3:
                        self.conv()
                    for _ in range(2):
                        self.take_pair()
                        self.T.add("psum_free_act")
                self.lru_ratio(0)
                self.lru_ratio(1)
                self.lru_scan(0)
                self.conv()
                self.eng.wait_ge(sems["psum_free_act"], self.T.at("psum_free_act"))

            def attention(self, kind):
                T = self.T
                items, heads, per = attention_items(kind)
                if kind == "diff":
                    self.eng.wait_ge(sems["params_loaded"], 16 * N_PARAM_LOADS)
                    self.eng.wait_ge(sems["s5_ready"], T.add("s5_ready"))
                    for s in range(2):
                        a = nc.vector.tensor_tensor(probs[:, 0, s, 0:64], lamv[:, 2 * s], lamv[:, 2 * s + 1], ALU.mult)
                    a.then_inc(sems["dve_step"], 1)
                    self.eng.wait_ge(sems["dve_step"], T.add("dve_step"))
                    ins = nc.vector.tensor_reduce(st(LAMS, 2), probs[:, 0, :, 0:64], AX_X, ALU.add)
                    ins.then_inc(sems["lam_dot"], 1)
                    T.add("lam_dot")
                    self.eng.wait_ge(sems["lam_exp"], T.add("lam_exp"))
                    nc.vector.scalar_tensor_tensor(st(LAM), st(LAMS + 1), -LAMBDA_INIT, st(LAMS), ALU.add, ALU.subtract)
                    ins = nc.vector.tensor_scalar(subg[:], subg[:], 1.0 - LAMBDA_INIT, None, ALU.mult)
                    ins.then_inc(sems["dve_step"], 1)
                    self.eng.wait_ge(sems["dve_step"], T.add("dve_step"))
                if kind == "window":
                    nc.vector.tensor_scalar(nsink, sink[:], -1.0, None, ALU.mult).then_inc(sems["dve_step"], 1)
                    self.eng.wait_ge(sems["dve_step"], T.add("dve_step"))
                if kind == "dilated":
                    self.eng.wait_ge(sems["masks_loaded"], 32)
                scale = (P if kind == "dilated" else 64) ** -0.5
                which = {"diff": 0, "window": 1, "dilated": 0}[kind]

                def bias(k):
                    pr, m = items[k]
                    b, keys, q = k % 2, (m + 1) * P, 2 * (k % 2)
                    self.eng.wait_ge(sems["scores_ready"], T.add("scores_ready"))
                    if k >= 2:
                        self.eng.wait_ge(sems["probs_turned"], T.add("probs_turned"))
                    mk = mask[:, which, SEQ - keys:SEQ] if m == 0 else mask[:, which]
                    nc.vector.scalar_tensor_tensor(
                        scores[:, b, :, 0:keys], score_ps[b][:, :, 0:keys], scale,
                        mk.unsqueeze(1).to_broadcast([P, 2, keys]), ALU.mult, ALU.add).then_inc(sems["dve_step"], 1)
                    self.eng.wait_ge(sems["dve_step"], T.add("dve_step"))
                    a = nc.vector.tensor_reduce(st(MAXN + q, 2), scores[:, b, :, 0:keys], AX_X, ALU.max, negate=True)
                    if kind == "window":
                        a.then_inc(sems["dve_step"], 1)
                        self.eng.wait_ge(sems["dve_step"], T.add("dve_step"))
                        a = nc.vector.tensor_tensor(st(MAXN + q, 2), st(MAXN + q, 2), nsink[:, 2 * pr:2 * pr + 2],
                                                    ALU.min)
                    a.then_inc(sems["biased"], 1)
                    T.add("biased")

                def normalise(k):
                    pr, m = items[k]
                    b, keys, q, r = k % 2, (m + 1) * P, 2 * (k % 2), RSUM + 2 * (k % 4)
                    self.eng.wait_ge(sems["exp_ready"], T.add("exp_ready"))
                    sc, pb = scores[:, b, :, 0:keys], probs[:, b, :, 0:keys]
                    if kind == "diff":
                        nc.vector.reciprocal(st(r, 2), st(SUMS + q, 2)).then_inc(sems["dve_step"], 1)
                        self.eng.wait_ge(sems["dve_step"], T.add("dve_step"))
                        nc.vector.tensor_scalar(pb[:, 0], sc[:, 0], st(r), None, ALU.mult)
                        nc.vector.tensor_tensor(st(r + 1), st(r + 1), st(LAM), ALU.mult).then_inc(sems["dve_step"], 1)
                        self.eng.wait_ge(sems["dve_step"], T.add("dve_step"))
                        a = nc.vector.scalar_tensor_tensor(pb[:, 0], sc[:, 1], st(r + 1), pb[:, 0], ALU.mult, ALU.add)
                    elif kind == "window":
                        nc.vector.tensor_tensor(st(SUMS + q, 2), st(SUMS + q, 2), st(ESINK + q, 2),
                                                ALU.add).then_inc(sems["dve_step"], 1)
                        self.eng.wait_ge(sems["dve_step"], T.add("dve_step"))
                        a = nc.vector.reciprocal(st(r, 2), st(SUMS + q, 2))
                    else:
                        mk = mask[:, 1, SEQ - keys:SEQ] if m == 0 else mask[:, 1]
                        nc.vector.tensor_tensor(pb, sc, mk.unsqueeze(1).to_broadcast([P, 2, keys]),
                                                ALU.mult).then_inc(sems["dve_step"], 1)
                        self.eng.wait_ge(sems["dve_step"], T.add("dve_step"))
                        nc.vector.tensor_reduce(st(SUMS + q, 2), pb, AX_X, ALU.add).then_inc(sems["dve_step"], 1)
                        self.eng.wait_ge(sems["dve_step"], T.add("dve_step"))
                        a = nc.vector.reciprocal(st(r, 2), st(SUMS + q, 2))
                    a.then_inc(sems["probs_ready"], 1)
                    T.add("probs_ready")
                def copy_turned(k):
                    m = items[k][1]
                    n = heads * (m + 1)
                    if k >= len(items) - 2:
                        self.eng.wait_ge(sems["probs_turned"], T.add("probs_turned"))
                    if k >= 2:
                        self.eng.wait_ge(sems["mixed"], T.add("mixed"))
                    nc.vector.tensor_copy(probs_t[:, k % 2, 0:n],
                                          turn_ps[:, 2 * (k % 2):2 * (k % 2) + 2].rearrange(
                                              "p a (b c) -> p (a b) c", c=P)[:, 0:n]).then_inc(sems["probs_copied"], 1)
                    T.add("probs_copied")

                bias(0)
                for k in range(len(items)):
                    if k + 1 < len(items):
                        bias(k + 1)
                    normalise(k)
                    if k:
                        copy_turned(k - 1)
                copy_turned(len(items) - 1)
                T.add("mixed", 2)
                T.add("mixed_out", len(items))
                if kind == "diff":
                    self.eng.wait_ge(sems["root_ready"], T.add("root_ready"))
                    nc.vector.reciprocal(st(SUB, 16), st(SUB, 16)).then_inc(sems["head_factors"], 1)
                else:
                    self.eng.wait_ge(sems["mixed_out"], T.at("mixed_out"))
                    nc.vector.memset(unused, 0.0).then_inc(sems["mix_ready"], 1)
                    T.add("mix_ready")

            def s5_params(self):
                self.eng.wait_ge(sems["s5_asked"], self.T.add("s5_asked"))
                nc.vector.reciprocal(s5[:, 11], s5[:, 10]).then_inc(sems["s5_recip"], 1)

            def s5(self):
                T = self.T
                for g in range(8):
                    rot = rots[g % 2]
                    c, s = rot[:, 0], rot[:, 1]
                    xr, xi = (ps[:].rearrange("p m (k s) -> p (m k) s", s=SEQ) for ps in pair)
                    self.eng.wait_ge(sems["bu_ready"], T.add("bu_ready"))
                    self.eng.wait_ge(sems["rot_ready"], T.add("rot_ready"))
                    if g:
                        self.eng.wait_ge(sems["h_ready"], T.at("h_ready"))
                    nc.vector.tensor_tensor(t_1[:], xr, c, ALU.mult)
                    nc.vector.tensor_tensor(t_2[:], xi, s, ALU.mult)
                    nc.vector.tensor_tensor(g_im[:], xi, c, ALU.mult)
                    nc.vector.tensor_tensor(g_re[:], xr, s, ALU.mult).then_inc(sems["bu_used"], 1)
                    self.eng.wait_ge(sems["bu_used"], T.add("bu_used"))
                    nc.vector.tensor_tensor(t_1[:], t_1[:], t_2[:], ALU.add)
                    nc.vector.tensor_tensor(g_im[:], g_im[:], g_re[:], ALU.subtract).then_inc(sems["dve_step"], 1)
                    self.eng.wait_ge(sems["dve_step"], T.add("dve_step"))
                    for src, dst in ((t_1, t_2), (g_im, g_re)):
                        for j in range(4):
                            t = 4 * g + j
                            a = nc.vector.tensor_tensor_scan(dst[:, j], decay[:, t:t + 1].to_broadcast([P, SEQ]),
                                                             src[:, j], 0.0, ALU.mult, ALU.add)
                    a.then_inc(sems["dve_step"], 1)
                    self.eng.wait_ge(sems["dve_step"], T.add("dve_step"))
                    if g >= 2:
                        self.eng.wait_ge(sems["y_ready"], T.at("y_ready", 1))
                    h_re, h_im = states[g % 2]
                    nc.vector.tensor_tensor(h_re[:], t_2[:], c, ALU.mult)
                    nc.vector.tensor_tensor(t_1[:], g_re[:], s, ALU.mult)
                    nc.vector.tensor_tensor(g_im[:], t_2[:], s, ALU.mult)
                    nc.vector.tensor_tensor(h_im[:], g_re[:], c, ALU.mult).then_inc(sems["rot_used"], 1)
                    self.eng.wait_ge(sems["rot_used"], T.add("rot_used"))
                    nc.vector.tensor_tensor(h_re[:], h_re[:], t_1[:], ALU.subtract)
                    nc.vector.tensor_tensor(h_im[:], h_im[:], g_im[:], ALU.add).then_inc(sems["h_ready"], 1)
                    T.add("h_ready")
                    T.add("y_ready")
                    if g:
                        self.skip(g - 1, 1)
                    if g == 5:
                        self.gelu_scale(0)
                    if g == 6:
                        self.gelu_apply(0)
                    if g == 7:
                        self.gelu_lo(0)
                self.conv()
                self.skip(7, 0)
                self.gelu_scale(1)
                self.attention_lo(0)
                self.gelu_apply(1)
                self.gelu_lo(1)
                self.attention_lo(1)

            def gelu_scale(self, half):
                T, z, u = self.T, glu_z[half][:], u2[:, 4 * half:4 * half + 4]
                self.eng.wait_ge(sems["gelu_a"], T.add("gelu_a"))
                nc.vector.tensor_scalar(z, z, GELU_3, GELU_1, ALU.mult, ALU.add).then_inc(sems["dve_step"], 1)
                self.eng.wait_ge(sems["dve_step"], T.add("dve_step"))
                nc.vector.tensor_tensor(z, z, u, ALU.mult).then_inc(sems["gelu_b"], 1)
                T.add("gelu_b")

            def gelu_apply(self, half):
                u = u2[:, 4 * half:4 * half + 4]
                self.eng.wait_ge(sems["gelu_a"], self.T.add("gelu_a"))
                nc.vector.tensor_tensor(u, u, glu_z[half][:], ALU.mult).then_inc(sems["y_gelu"], 1)
                self.T.add("y_gelu")

            def gelu_lo(self, half):
                tiles = slice(4 * half, 4 * half + 4)
                self.eng.wait_ge(sems["split_hi"], self.T.add("split_hi"))
                a = nc.vector.tensor_tensor(xt_l[:, tiles], u2[:, tiles], xt_h[:, tiles].bitcast(F32), ALU.subtract)
                a.then_inc(sems["split_done"], 1)
                self.T.add("split_done")

            def attention_lo(self, n):
                tiles = slice(8 + 4 * n, 12 + 4 * n)
                self.T.add("turned")
                self.eng.wait_ge(sems["split_hi"], self.T.add("split_hi"))
                a = nc.vector.tensor_tensor(xt_l[:, tiles], turn_ps[:], xt_h[:, tiles].bitcast(F32), ALU.subtract)
                a.then_inc(sems["split_done"], 1)
                self.T.add("split_done")

            def skip(self, g, back):
                self.eng.wait_ge(sems["y_ready"], self.T.at("y_ready", back))
                c = C_DSKIP + g
                a = nc.vector.scalar_tensor_tensor(u2[:, g], u2[:, g], col[:, c:c + 1], misc_ps[:, g % 2, 0:SEQ],
                                                   ALU.mult, ALU.add)
                if g == 7:
                    a.then_inc(sems["y_done"], 1)
                    self.T.add("y_done")
                else:
                    a.then_inc(sems["y_read"], 1)
                    self.T.add("y_read")

            def glu(self):
                self.conv()
                self.conv()
                self.take_pair()
                self.take_pair()
                self.glu_product(0)
                self.conv()

            def glu_product(self, half):
                z = glu_z[half][:]
                self.eng.wait_ge(sems["psum_free_act"], self.T.add("psum_free_act"))
                nc.vector.tensor_tensor(z, z, u2[:, 4 * half:4 * half + 4], ALU.mult).then_inc(sems["glu_half"], 1)
                self.T.add("glu_half")

            def glu_lead(self):
                T = self.T
                self.conv()
                self.glu_product(1)
                self.eng.wait_ge(sems["split_hi"], T.add("split_hi"))
                for half in range(2):
                    tiles = slice(4 * half, 4 * half + 4)
                    a = nc.vector.tensor_tensor(xt_l[:, tiles], glu_z[half][:], xt_h[:, tiles].bitcast(F32),
                                                ALU.subtract)
                a.then_inc(sems["split_done"], 1)
                T.add("split_done")
                self.conv()
                self.conv()

            def gained(self, n):
                T, cols = self.T, slice(n * CH, (n + 1) * CH)
                self.eng.wait_ge(sems["psum_free_dve"], T.at("psum_free_dve"))
                nc.vector.tensor_tensor(xres[:, :, cols], xres[:, :, cols], acc[:, :, cols], ALU.add
                                        ).then_inc(sems["x_ready"], 1)
                self.eng.wait_ge(sems["x_ready"], T.add("x_ready"))
                T.add("squared")
                self.eng.wait_ge(sems["gain_ready"], T.add("gain_ready"))
                nc.vector.tensor_tensor(acc[:, :, cols], xres[:, :, cols],
                                        misc_ps[:, n % 2].unsqueeze(1).to_broadcast([P, M, CH]), ALU.mult
                                        ).then_inc(sems["gained"], 1)
                T.add("gained")

            def final(self):
                T = self.T
                self.eng.wait_ge(sems["squared"], T.at("squared"))
                self.norm_factor(SSX, RS, "rs_ready")
                self.eng.wait_ge(sems["rs_ready"], T.at("rs_ready"))
                for m in range(M):
                    y = acc[:, m, 0:D // 2]
                    nc.vector.tensor_scalar(y, y, st(RS + m), None, ALU.mult).then_inc(sems["out_ready_dve"], 1)

        class Tensor(Program):
            def setup(self):
                pe = self.eng
                pe.wait_ge(sems["loaded"], 16 * N_LOADS)
                self.eng.wait_ge(sems["rows_ready"], self.T.add("rows_ready"))
                for k, n in enumerate((P, 112, 96)):
                    a = nc.tensor.transpose(misc_ps[:, 0, k * P:k * P + n], prow[0:n, k], ident[0:n, 0:n])
                a.then_inc(sems["params_turned"], 1)
                self.T.add("params_turned")

            def unit(self, xh, xl, ps, t0, first, last, width):
                T = self.T
                r = T.n.get("unit", 0) % RING
                self.eng.wait_ge(sems["lo_ready"], T.at("unit", -1))
                h, l = (w[:, r, 0:KU * width].rearrange("p (t n) -> p t n", t=KU) for w in (hi, lo))
                for k in range(KU):
                    for m in range(M):
                        tok = slice(m * P, (m + 1) * P)
                        s, e = first and k == 0, last and k == KU - 1
                        to = ps[:, m, 0:width]
                        nc.tensor.matmul(to, xh[:, t0 + k, tok], h[:, k], start=s, stop=False)
                        nc.tensor.matmul(to, xl[:, t0 + k, tok], h[:, k], start=False, stop=False)
                        mm = nc.tensor.matmul(to, xh[:, t0 + k, tok], l[:, k], start=False, stop=e)
                mm.then_inc(sems["unit_used"], 1)
                T.add("unit")

            def pair_free(self):
                for name in ("psum_free_act", "psum_free_dve"):
                    if self.T.any(name, 1 if self.last_by == name else 0):
                        self.eng.wait_ge(sems[name], self.T.at(name, 1 if self.last_by == name else 0))

            last_by = None

            def turn(self, prev):
                self.eng.wait_ge(sems[self.STAGED[prev.kind]], self.T.at(self.STAGED[prev.kind]))
                self.eng.wait_ge(sems["split_done"], self.T.at("split_done"))
                tiles = prev.to[2] if len(prev.to) > 2 else 4
                for k in range(tiles):
                    for m in range(M):
                        a = nc.tensor.transpose(turn_ps[:, k, m * P:(m + 1) * P], stg[:, m, k * P:(k + 1) * P],
                                                ident[:])
                a.then_inc(sems["turned"], 1)
                self.T.add("turned")
                self.T.add("split_done")

            def chunk(self, kind, w, x=None, units=4, width=CH, prev=None, lead=None, to=None, n=0, x_tiles=None,
                      final=False, **_):
                T, ps = self.T, self.take_pair()
                self.pair_free()
                if lead:
                    self.lead_first(lead)
                for j in range(units):
                    if prev and j == min(2, units - 2):
                        self.turn(prev)
                    if prev and kind == "add" and j == units - 1:
                        self.eng.wait_ge(sems["split_done"], T.at("split_done"))
                    if lead and j < lead.parts:
                        done = T.n["lead_base"] + j + 1
                        self.eng.wait_ge(sems["split_done"], done)
                    if lead and lead.kind == "glu" and j in (0, 2):
                        self.eng.wait_ge(sems["split_done"], T.n["lead_base"] + 1 + j // 2)
                    self.unit(x[0], x[1], ps, x_tiles[j] if x_tiles else KU * j, j == 0, j == units - 1, width)
                    if lead and lead.kind == "post" and j == 0:
                        self.gain(lead.gain_row, 3)
                    if lead and lead.kind != "lru" and j < 2 and j + 2 < lead.parts:
                        self.turn_part(lead, j + 2)
                self.last_by = self.BY[kind]
                T.add(self.last_by)
                if final:
                    self.spread_final_gain(n)
                if kind in ("relu2", "gelu", "rope"):
                    T.add("staged")
                return Pending(kind, ps, to, width) if kind in self.TURNED else None

            def drain(self, prev):
                self.turn(prev)

            def lead_first(self, lead):
                T, kind = self.T, lead.kind
                T.n["lead_base"] = T.n.get("split_done", 0)
                if kind == "glu":
                    T.add("split_done", 2)
                    return
                if kind == "lru":
                    T.add("split_done", 4)
                    return
                if kind == "turn":
                    self.eng.wait_ge(sems["mix_ready"], T.add("mix_ready"))
                    self.eng.wait_ge(sems["normed"], 1)
                if kind == "post":
                    self.gain(lead.gain_row, 0)
                    self.gain(lead.gain_row, 1)
                self.turn_part(lead, 0)
                if kind == "post":
                    self.gain(lead.gain_row, 2)
                if lead.parts > 1:
                    self.turn_part(lead, 1)

            def gain(self, row0, n):
                T = self.T
                if n == 0:
                    self.eng.wait_ge(sems["params_loaded"], 16 * N_PARAM_LOADS)
                    T.n["gain_base"] = T.n.get("x_ready", 0)
                else:
                    if n >= 2:
                        self.eng.wait_ge(sems["x_ready"], T.n["gain_base"] + n - 1)
                r = row0 + n
                nc.tensor.matmul(misc_ps[:, n % 2], ident[0:G_ROWS, r:r + 1].to_broadcast([G_ROWS, P]),
                                 grows[0:G_ROWS], start=True, stop=True).then_inc(sems["gain_ready"], 1)
                T.add("gain_ready")

            def turn_part(self, lead, n):
                T, kind = self.T, lead.kind
                if kind in ("post", "plain"):
                    self.eng.wait_ge(sems["x_ready"], T.add("x_ready"))
                if n >= 2:
                    self.eng.wait_ge(sems["split_done"], T.n["lead_base"] + n - 1)
                elif n == 0:
                    if T.any("split_done"):
                        self.eng.wait_ge(sems["split_done"], T.at("split_done"))
                else:
                    if T.any("psum_free_act"):
                        self.eng.wait_ge(sems["psum_free_act"], T.at("psum_free_act"))
                    if T.any("psum_free_dve"):
                        self.eng.wait_ge(sems["psum_free_dve"], T.at("psum_free_dve"))
                src = acc if kind == "turn" else xres
                to = Scalar.part_psum(self, n)
                for k in range(4):
                    for m in range(M):
                        c = n * CH + k * P
                        a = nc.tensor.transpose(to[:, k, m * P:(m + 1) * P], src[:, m, c:c + P], ident[:])
                a.then_inc(sems["turned"], 1)
                T.add("turned")
                T.add("split_done")

            def gates(self):
                T = self.T
                for j in range(4):
                    r = T.n["unit"] % RING
                    self.eng.wait_ge(sems["lo_ready"], T.at("unit", -1))
                    h, l = (w[:, r].rearrange("p (n t e) -> p n t e", n=4, t=2) for w in (hi, lo))
                    for b in range(2):
                        ps = self.take_pair()
                        self.pair_free()
                        for k in range(2):
                            n = 2 * b + k
                            for e in range(2):
                                to, out_cols = ps[:, k, e * SEQ:(e + 1) * SEQ], slice(e * P, (e + 1) * P)
                                for t in range(2):
                                    x = 8 * (j % 2) + 2 * n + t
                                    xh, xl = ht_h[:, x], ht_l[:, x]
                                    nc.tensor.matmul(to, h[:, n, t, out_cols], xh, start=t == 0, stop=False)
                                    nc.tensor.matmul(to, h[:, n, t, out_cols], xl, start=False, stop=False)
                                    a = nc.tensor.matmul(to, l[:, n, t, out_cols], xh, start=False, stop=t == 1)
                        if b == 0:
                            a.then_inc(sems["block_done"], 1)
                            T.add("block_done")
                        else:
                            a.then_inc(sems["unit_used"], 1)
                            T.add("unit")
                        self.last_by = "psum_free_act"
                        T.add("psum_free_act")
                self.eng.wait_ge(sems["psum_free_act"], T.at("psum_free_act"))

            def attention(self, kind):
                T = self.T
                items, heads, per = attention_items(kind)
                self.eng.wait_ge(sems["split_done"], T.at("split_done"))
                self.eng.wait_ge(sems["psum_free_act"], T.at("psum_free_act"))
                if kind != "diff":
                    self.eng.wait_ge(sems["mixed_out"], T.at("mixed_out"))

                def score(k):
                    pr, m = items[k]
                    keys, tok = (m + 1) * P, slice(m * P, (m + 1) * P)
                    if k >= 2:
                        self.eng.wait_ge(sems["biased"], T.add("biased"))
                    for s in range(2):
                        half = slice(64 * s, 64 * s + 64)
                        if kind == "diff":
                            q, kk = qk0[half, pr, tok], qk0[half, 8 + pr, 0:keys]
                        elif kind == "window":
                            q, kk = qk0[half, 16 + pr, tok], k_swa[half, int(s != pr // 4), 0:keys]
                        else:
                            q, kk = qk2[:, 2 * pr + s, tok], qk2[:, 8 + 2 * pr + s, 0:keys]
                        a = nc.tensor.matmul(score_ps[k % 2][:, s, 0:keys], q, kk, start=True, stop=True)
                    a.then_inc(sems["scores_ready"], 1)
                    T.add("scores_ready")

                def turn_probs(k):
                    m = items[k][1]
                    self.eng.wait_ge(sems["probs_ready"], T.add("probs_ready"))
                    src = scores if kind == "window" else probs
                    to = turn_ps[:, 2 * (k % 2):2 * (k % 2) + 2].rearrange("p a (b c) -> p (a b) c", c=P)
                    for s in range(heads):
                        for t in range(m + 1):
                            a = nc.tensor.transpose(to[:, s * (m + 1) + t], src[:, k % 2, s, t * P:(t + 1) * P],
                                                    ident[:])
                    a.then_inc(sems["probs_turned"], 1)
                    T.add("probs_turned")

                def mix(k):
                    pr, m = items[k]
                    self.eng.wait_ge(sems["probs_copied"], T.add("probs_copied"))
                    if k >= 2:
                        self.eng.wait_ge(sems["mixed_out"], T.add("mixed_out"))
                    for s in range(heads):
                        for t in range(m + 1):
                            if kind == "diff":
                                v = v0[:, t, pr * P:(pr + 1) * P]
                            elif kind == "window":
                                v = v_swa[:, t, 64 * (pr // 4):64 * (pr // 4) + 64]
                            else:
                                v = v2[:, t, (2 * pr + s) * P:(2 * pr + s + 1) * P]
                            a = nc.tensor.matmul(pair[0][:, k % 2, s * per:s * per + per],
                                                 probs_t[:, k % 2, s * (m + 1) + t], v, start=t == 0, stop=t == m)
                    a.then_inc(sems["mixed"], 1)
                    T.add("mixed")

                score(0)
                score(1)
                for k in range(len(items)):
                    if k + 2 < len(items):
                        score(k + 2)
                    turn_probs(k)
                    if k:
                        mix(k - 1)
                mix(len(items) - 1)
                T.add("mixed_out", 2)
                self.eng.wait_ge(sems["biased"], T.add("biased", 2))
                self.eng.wait_ge(sems["mixed_out"], T.at("mixed_out"))

            def s5(self):
                T = self.T

                def turn_b(g):
                    self.eng.wait_ge(sems["b_padded"], T.add("b_padded"))
                    if T.any("c_copied"):
                        self.eng.wait_ge(sems["c_copied"], T.at("c_copied"))
                    for ri in range(2):
                        for j in range(4):
                            a = nc.tensor.transpose(turn_all[:, ri, j], b_pad[:, ri, j], ident[:])
                    a.then_inc(sems["b_turned"], 1)
                    T.add("b_turned")

                def turn_c(g):
                    self.eng.wait_ge(sems["c_padded"], T.add("c_padded"))
                    self.eng.wait_ge(sems["b_copied"], T.at("b_copied"))
                    for ri in range(2):
                        for j in range(4):
                            a = nc.tensor.transpose(turn_all[:, ri, j], c_pad[:, ri, j], ident[:])
                    a.then_inc(sems["c_turned"], 1)
                    T.add("c_turned")
                    T.add("c_copied")

                def bu(g):
                    self.eng.wait_ge(sems["b_copied"], T.add("b_copied"))
                    if T.any("bu_used"):
                        self.eng.wait_ge(sems["bu_used"], T.at("bu_used"))
                    for ri in range(2):
                        to = pair[ri][:].rearrange("p m (k s) -> p (m k) s", s=SEQ)
                        for j in range(4):
                            a = nc.tensor.matmul(to[:, j], b_t[:, ri, j], u2[:, g], start=True, stop=True)
                    a.then_inc(sems["bu_ready"], 1)
                    T.add("bu_ready")
                    T.add("bu_used")

                def y(g):
                    self.eng.wait_ge(sems["h_ready"], T.add("h_ready"))
                    self.eng.wait_ge(sems["c_copied"], T.at("c_copied"))
                    if g >= 2:
                        self.eng.wait_ge(sems["y_read"], T.add("y_read"))
                    for j in range(4):
                        for ri, h in enumerate(states[g % 2]):
                            a = nc.tensor.matmul(misc_ps[:, g % 2, 0:SEQ], c_t[:, ri, j], h[:, j],
                                                 start=j == 0 and ri == 0, stop=j == 3 and ri == 1)
                    a.then_inc(sems["y_ready"], 1)
                    T.add("y_ready")

                turn_b(0)
                bu(0)
                turn_c(0)
                for g in range(8):
                    if g < 7:
                        turn_b(g + 1)
                        bu(g + 1)
                    y(g)
                    if g < 7:
                        turn_c(g + 1)
                self.eng.wait_ge(sems["bu_used"], T.at("bu_used"))
                self.eng.wait_ge(sems["mix_ready"], T.add("mix_ready"))
                self.turn_attention(0)

            def turn_attention(self, n):
                for k in range(4):
                    for m in range(M):
                        c = n * CH + k * P
                        a = nc.tensor.transpose(turn_ps[:, k, m * P:(m + 1) * P], acc[:, m, c:c + P], ident[:])
                a.then_inc(sems["turned"], 1)

            def glu(self):
                T = self.T
                for half in range(2):
                    ps = self.take_pair()
                    flat = ps[:].rearrange("p m (k s) -> p (m k) s", s=SEQ)
                    for kk in range(2):
                        r = T.n["unit"] % RING
                        self.eng.wait_ge(sems["lo_ready"], T.at("unit", -1))
                        if half == 0:
                            self.eng.wait_ge(sems["split_done"], T.add("split_done", 1 + kk))
                        h, l = (w[:, r].rearrange("p (t n) -> p t n", t=KU) for w in (hi, lo))
                        for e in range(4):
                            cols = slice(e * P, (e + 1) * P)
                            for k in range(KU):
                                t = KU * kk + k
                                first, last = kk == 0 and k == 0 and e % 2 == 0, kk == 1 and k == KU - 1
                                nc.tensor.matmul(flat[:, e], h[:, k, cols], xt_h[:, t], start=first, stop=False,
                                                 skip_group_check=True)
                                nc.tensor.matmul(flat[:, e], h[:, k, cols], xt_l[:, t], start=False, stop=False,
                                                 skip_group_check=True)
                                a = nc.tensor.matmul(flat[:, e], l[:, k, cols], xt_h[:, t], start=False, stop=last,
                                                     skip_group_check=True)
                        a.then_inc(sems["unit_used"], 1)
                        T.add("unit")
                        if half == 0 and kk == 0:
                            self.eng.wait_ge(sems["split_done"], T.at("split_done", -1))
                            self.turn_attention(1)
                    self.last_by = "psum_free_act"
                    T.add("psum_free_act")

            def spread_final_gain(self, n):
                if n >= 2:
                    self.eng.wait_ge(sems["gained"], self.T.add("gained"))
                r = G_FINAL + n
                nc.tensor.matmul(misc_ps[:, n % 2], ident[0:G_ROWS, r:r + 1].to_broadcast([G_ROWS, P]),
                                 grows[0:G_ROWS], start=True, stop=True).then_inc(sems["gain_ready"], 1)

        class Pool(Program):
            def tt(self, out, a, b, op):
                nc.gpsimd.tensor_tensor(out, a, b, op).then_inc(sems["pool_step"], 1)
                self.eng.wait_ge(sems["pool_step"], self.T.add("pool_step"))

            def ts(self, out, a, s1, s2, op0, op1=ALU.bypass):
                nc.gpsimd.tensor_scalar(out, a, s1, s2, op0, op1).then_inc(sems["pool_step"], 1)
                self.eng.wait_ge(sems["pool_step"], self.T.add("pool_step"))

            def cmul(self, dst, a, b, t):
                self.tt(t[0], a[0], b[0], ALU.mult)
                self.tt(t[1], a[1], b[1], ALU.mult)
                self.tt(t[0], t[0], t[1], ALU.subtract)
                self.tt(t[1], a[0], b[1], ALU.mult)
                self.tt(dst[1], a[1], b[0], ALU.mult)
                self.tt(dst[1], dst[1], t[1], ALU.add)
                nc.gpsimd.tensor_copy(dst[0], t[0]).then_inc(sems["pool_step"], 1)
                self.eng.wait_ge(sems["pool_step"], self.T.add("pool_step"))

            def setup(self):
                T = self.T
                self.eng.wait_ge(sems["col_ready"], T.add("col_ready"))
                dt, zr, zi, k, q, th, th2, _, sn, sh, den, rden, ar, ai, nr, fr, fi, pr, pi, t1, t2, t3 = (
                    s5[:, n] for n in range(22))
                are, aim = col[:, C_ARE:C_ARE + 32], col[:, C_AIM:C_AIM + 32]
                self.tt(zr, are, dt, ALU.mult)
                self.tt(zi, aim, dt, ALU.mult)
                magic = 1.5 * 2.0 ** 23
                self.ts(k, zi, 1.0 / (2.0 * math.pi), magic, ALU.mult, ALU.add)
                self.ts(k, k, magic, None, ALU.subtract)
                c1, c2 = 6.28125, 1.93500518798828125e-3
                c3 = 2.0 * math.pi - c1 - c2
                self.ts(th, k, c1, None, ALU.mult)
                self.tt(th, zi, th, ALU.subtract)
                for c in (c2, c3):
                    self.ts(q, k, c, None, ALU.mult)
                    self.tt(th, th, q, ALU.subtract)
                self.ts(th, th, 3.14159, -3.14159, ALU.min, ALU.max)
                self.ts(th2, th, 0.5, None, ALU.mult)
                self.tt(t1, are, are, ALU.mult)
                self.tt(t2, aim, aim, ALU.mult)
                nc.gpsimd.tensor_tensor(den, t1, t2, ALU.add).then_inc(sems["s5_asked"], 1)
                T.add("s5_asked")
                self.eng.wait_ge(sems["s5_given"], T.add("s5_given"))
                self.eng.wait_ge(sems["s5_recip"], T.add("s5_recip"))
                self.eng.wait_ge(sems["params_loaded"], 16 * N_PARAM_LOADS)
                cs = th2
                self.tt(t1, sh, sh, ALU.mult)
                self.ts(cs, t1, -2.0, 1.0, ALU.mult, ALU.add)
                self.tt(ar, decay[:], cs, ALU.mult)
                self.tt(ai, decay[:], sn, ALU.mult)
                self.ts(nr, ar, 1.0, None, ALU.subtract)
                self.tt(t1, nr, are, ALU.mult)
                self.tt(t2, ai, aim, ALU.mult)
                self.tt(t1, t1, t2, ALU.add)
                self.tt(fr, t1, rden, ALU.mult)
                self.tt(t1, ai, are, ALU.mult)
                self.tt(t2, nr, aim, ALU.mult)
                self.tt(t1, t1, t2, ALU.subtract)
                self.tt(fi, t1, rden, ALU.mult)

                def spread(a, n):
                    return a.unsqueeze(2).to_broadcast([P, SSM_TILES, n])

                self.cmul((b_bar[:, 0], b_bar[:, 1]), (b_raw[:, 0], b_raw[:, 1]), (spread(fr, 16), spread(fi, 16)),
                          (s5_t[:, 0], s5_t[:, 1]))
                nc.gpsimd.tensor_copy(pr, cs).then_inc(sems["pool_step"], 1)
                self.eng.wait_ge(sems["pool_step"], T.add("pool_step"))
                nc.gpsimd.tensor_copy(pi, sn).then_inc(sems["pool_step"], 1)
                self.eng.wait_ge(sems["pool_step"], T.add("pool_step"))
                for level in range(2):
                    re, im = pw[:, level, 0], pw[:, level, 1]
                    nc.gpsimd.memset(re[:, :, 0:1], 1.0)
                    nc.gpsimd.memset(im[:, :, 0:1], 0.0).then_inc(sems["pool_step"], 1)
                    self.eng.wait_ge(sems["pool_step"], T.add("pool_step"))
                    for e in range(4):
                        n = 2 ** e
                        self.cmul((re[:, :, n:2 * n], im[:, :, n:2 * n]), (re[:, :, 0:n], im[:, :, 0:n]),
                                  (spread(pr, n), spread(pi, n)), (s5_t[:, 0, :, 0:n], s5_t[:, 1, :, 0:n]))
                        self.tt(t1, pr, pr, ALU.mult)
                        self.tt(t2, pi, pi, ALU.mult)
                        self.tt(t3, pr, pi, ALU.mult)
                        self.tt(pr, t1, t2, ALU.subtract)
                        self.ts(pi, t3, 2.0, None, ALU.mult)
                nc.gpsimd.tensor_copy(t1, pr).then_inc(sems["s5_ready"], 1)
                T.add("s5_ready")

            @contextmanager
            def loop(self, trips, **stride):
                with self.T.loop(None, trips, **stride):
                    yield 0

            def gates(self):
                T = self.T
                T.add("psum_free_act", 4)
                for q in range(4):
                    tiles = slice(4 * q, 4 * q + 4)
                    self.eng.wait_ge(sems["psum_free_act"], T.add("psum_free_act"))
                    if q:
                        self.eng.wait_ge(sems["gated"], T.at("gated"))
                    self.tt(xc_4[:], ht_h[:, tiles].bitcast(F32), ht_l[:, tiles].bitcast(F32), ALU.add)
                    nc.gpsimd.tensor_tensor(gate_i[:, tiles], gate_i[:, tiles], xc_4[:], ALU.mult
                                            ).then_inc(sems["gated"], 1)
                    T.add("gated")

            def glu(self):
                self.T.add("psum_free_act", 2)

            def chunk(self, kind, w, lead=None, **_):
                self.T.add(self.BY[kind])
                if lead and lead.kind in ("post", "plain"):
                    self.T.add("x_ready", 4)
                    if kind in ("relu2", "silu"):
                        self.eng.wait_ge(sems["x_ready"], self.T.at("x_ready"))
                        nc.gpsimd.memset(acc[:], 0.0).then_inc(sems["acc_zero"], 1)
                        self.T.add("acc_zero")

            def pad_b(self, g):
                T = self.T
                if T.any("b_turned"):
                    self.eng.wait_ge(sems["b_turned"], T.at("b_turned"))
                for ri in range(2):
                    a = nc.gpsimd.tensor_tensor(
                        b_pad[:, ri].rearrange("p j (c q) -> p j c q", q=16),
                        b_bar[:, ri, 4 * g:4 * g + 4].unsqueeze(2).to_broadcast([P, 4, 8, 16]),
                        small[:, K_BM:K_BM + 32].rearrange("p (j c) -> p j c", j=4).unsqueeze(3).to_broadcast(
                            [P, 4, 8, 16]), ALU.mult)
                a.then_inc(sems["b_padded"], 1)
                T.add("b_padded")
                T.add("b_turned")

            def pad_c(self, g):
                T = self.T
                if T.any("c_turned"):
                    self.eng.wait_ge(sems["c_turned"], T.at("c_turned"))
                for ri in range(2):
                    a = nc.gpsimd.tensor_tensor(
                        c_pad[:, ri].rearrange("p j (c n) -> p (j c) n", n=64),
                        c_all[:, ri, g].unsqueeze(1).to_broadcast([P, 8, 64]),
                        small[:, K_CM:K_CM + 8].unsqueeze(2).to_broadcast([P, 8, 64]), ALU.mult)
                a.then_inc(sems["c_padded"], 1)
                T.add("c_padded")
                T.add("c_turned")

            def attention(self, kind):
                if kind == "dilated":
                    self.eng.wait_ge(sems["psum_free_act"], self.T.at("psum_free_act"))
                    self.rotation(0)
                if kind == "diff":
                    self.eng.wait_ge(sems["head_factors"], 1)
                    o = [acc[:, m, 0:1024].rearrange("p (h d) -> p h d", d=P) for m in range(M)]
                    for m in range(M):
                        a = nc.gpsimd.tensor_tensor(
                            o[m], o[m], st(SUB + 8 * m, 8).unsqueeze(2).to_broadcast([P, 8, P]), ALU.mult)
                    a.then_inc(sems["pool_step"], 1)
                    self.eng.wait_ge(sems["pool_step"], self.T.add("pool_step"))
                    for m in range(M):
                        a = nc.gpsimd.tensor_tensor(o[m], o[m], subg[:].unsqueeze(1).to_broadcast([P, 8, P]), ALU.mult)
                    a.then_inc(sems["normed"], 1)

            def rotation(self, g):
                T = self.T
                if T.any("rot_ready"):
                    self.eng.wait_ge(sems["rot_ready"], T.at("rot_ready"))
                if g >= 2:
                    self.eng.wait_ge(sems["rot_used"], T.add("rot_used"))
                to = rots[g % 2]
                re, im = (to[:, k].rearrange("p j (a b) -> p j a b", b=16) for k in range(2))
                t1, t2 = (rot_t[:, k].rearrange("p j (a b) -> p j a b", b=16) for k in range(2))
                tiles = slice(4 * g, 4 * g + 4)
                fr, fi = (pw[:, 0, k, tiles].unsqueeze(2).to_broadcast([P, 4, 16, 16]) for k in range(2))
                cr, ci = (pw[:, 1, k, tiles].unsqueeze(3).to_broadcast([P, 4, 16, 16]) for k in range(2))
                nc.gpsimd.tensor_tensor(re, cr, fr, ALU.mult)
                nc.gpsimd.tensor_tensor(t1, ci, fi, ALU.mult)
                nc.gpsimd.tensor_tensor(im, ci, fr, ALU.mult)
                nc.gpsimd.tensor_tensor(t2, cr, fi, ALU.mult).then_inc(sems["pool_step"], 1)
                self.eng.wait_ge(sems["pool_step"], T.add("pool_step"))
                nc.gpsimd.tensor_tensor(re, re, t1, ALU.subtract)
                nc.gpsimd.tensor_tensor(im, im, t2, ALU.add).then_inc(sems["rot_ready"], 1)
                T.add("rot_ready")

            def s5(self):
                self.eng.wait_ge(sems["mix_ready"], self.T.add("mix_ready", 2))
                self.eng.wait_ge(sems["c_loaded"], 32)
                for g in range(8):
                    self.pad_b(g)
                    if g:
                        self.rotation(g)
                    self.pad_c(g)

        XT, HT = (xt_h, xt_l), (ht_h, ht_l)

        def acc_cols(n):
            return acc[:, :, n * CH:(n + 1) * CH]

        def ht_part(j):
            return ht_h[:, 4 * j:4 * j + 4], ht_l[:, 4 * j:4 * j + 4]

        def mlp_group(e, w1, w2, g, lead=None):
            prev = None
            for j in range(4):
                prev = e.chunk("relu2", (w1, 0, g * D + j * CH), x=XT, to=ht_part(j), prev=prev,
                               lead=lead if j == 0 else None)
            for n in range(NCH):
                e.chunk("add", (w2, g * KT, n * CH), x=HT, dst=acc_cols(n), n=n, prev=prev if n == 0 else None,
                        more=n < NCH - 1)

        MLP_STRIDE = dict(unit=32, chunk=8, raw0=128, raw1=128, raw2=128, raw3=128, psum_free_act=4, psum_free_dve=4,
                          staged=4, turned=4, split_hi=4, split_done=4, squared=4)

        def mlp_stage(e, layer, lead):
            mlp_group(e, w_mlp1[layer], w_mlp2[layer], 0, lead)
            with e.loop(3, **MLP_STRIDE) as g:
                mlp_group(e, w_mlp1[layer], w_mlp2[layer], g + 1)

        def swiglu_group(e, g, hidden, lead=None, last=False):
            prev = None
            for j in range(hidden):
                c = g * D + j * CH
                e.chunk("silu", (w_gate2, 0, c), x=XT, prev=prev, lead=lead if j == 0 else None, more=True)
                prev = e.chunk("up", (w_up2, 0, c), x=XT, to=ht_part(j))
            for n in range(NCH):
                e.chunk("add", (w_down2, g * KT, n * CH), x=HT, dst=acc_cols(n), n=n, units=hidden, ss=False,
                        prev=prev if n == 0 else None, more=n < NCH - 1, final=last,
                        next_cols=0 if last and n == NCH - 1 else KU * CH)

        def model(e):
            e.setup()
            prev = None
            for c in range(9):
                w = (w_even_in, 0, c * CH)
                if c == 3:
                    e.s5_params()
                if c in (4, 5):
                    prev = e.chunk("tokens", w, x=XT, prev=prev, dst=v0[:, :, (c - 4) * CH:(c - 3) * CH], more=True)
                elif c == 8:
                    prev = e.chunk("kv", w, x=XT, prev=prev, width=SEQ, to=(None, k_swa[:], 2))
                else:
                    t = 4 * c if c < 4 else 16 + 4 * (c - 6)
                    prev = e.chunk("copy", w, x=XT, prev=prev, to=(None, qk0[:, t:t + 4]),
                                   lead=Lead("first", None, C_PRE_MIX, 4, *XT) if c == 0 else None,
                                   next_cols=KU * SEQ if c == 7 else KU * CH)
            e.drain(prev)
            e.attention("diff")
            e.attention("window")
            for n in range(NCH):
                e.chunk("set", (w_even_out, 0, n * CH), x=XT, dst=acc_cols(n), n=n, more=n < NCH - 1,
                        lead=Lead("turn", None, None, 4, *XT) if n == 0 else None)
            mlp_stage(e, 0, Lead("post", G_POST_MIX, C_PRE_MLP, 4, *XT))
            prev = None
            for c in range(8):
                kind, to = ("gelu", (None, y_br[:, 4 * c:4 * c + 4])) if c < 4 else ("copy", ("conv", 4 * (c - 4)))
                prev = e.chunk(kind, (w_odd_in, 0, c * CH), x=XT, prev=prev, to=to,
                               lead=Lead("post", G_POST_MLP, C_PRE_MIX + KT, 4, *XT) if c == 0 else None)
            e.drain(prev)
            e.gates()
            for n in range(NCH):
                e.chunk("set", (w_odd_out, 0, n * CH), x=XT, dst=acc_cols(n), n=n, more=n < NCH - 1,
                        lead=Lead("lru", None, None, 4, *XT) if n == 0 else None)
            mlp_stage(e, 1, Lead("post", G_POST_MIX + NCH, C_PRE_MLP + KT, 4, *XT))
            e.dilated_masks()
            prev = None
            for c in range(8):
                w, lead = (w_in2, 0, c * CH), Lead("post", G_POST_MLP + NCH, C_NORM1, 4, *XT) if c == 0 else None
                if c in (4, 5):
                    prev = e.chunk("tokens", w, x=XT, prev=prev, dst=v2[:, :, (c - 4) * CH:(c - 3) * CH], more=True)
                elif c < 4:
                    prev = e.chunk("rope", w, x=XT, prev=prev, to=(None, qk2[:, 4 * c:4 * c + 4]), lead=lead)
                else:
                    prev = e.chunk("copy", w, x=XT, prev=prev, to=(None, u2[:, 4 * (c - 6):4 * (c - 6) + 4]))
            e.drain(prev)
            e.attention("dilated")
            e.s5()
            e.glu()
            for n in range(NCH):
                e.chunk("set", (w_out2, 0, n * CH), x=XT, dst=acc_cols(n), n=n, ss=False, more=n < NCH - 1,
                        x_tiles=(8, 12, 0, 4), lead=Lead("glu", None, None, 0, *XT) if n == 0 else None)
            swiglu_group(e, 0, 4, lead=Lead("plain", None, C_NORM2, 4, *XT))
            swiglu_group(e, 1, 4)
            swiglu_group(e, 2, 3, last=True)
            e.final()

        block = ctx.enter_context(nc.Block())

        @block.sync
        def _(sp):
            model(Sync(sp))

        @block.scalar
        def _(act):
            model(Scalar(act))

        @block.vector
        def _(dve):
            model(Vector(dve))

        @block.tensor
        def _(pe):
            model(Tensor(pe))

        @block.gpsimd
        def _(pool):
            model(Pool(pool))


def shape_constants():
    f32 = np.float32
    q, k = np.arange(P)[:, None], np.arange(SEQ)[None, :]
    dist = q + P - k
    causal = dist >= 0
    count = ((dist <= 128).astype(int) + (dist % 4 == 0) + (dist % 16 == 0)) * causal
    masks = [np.where(causal, 0.0, MASKED), np.where(causal & (dist < 128), 0.0, MASKED),
             np.where(count > 0, 0.0, MASKED), count]
    inv_freq = f32(500000.0) ** (-np.arange(0, 32, 2, dtype=f32) / f32(32))
    angle = np.arange(SEQ, dtype=f32)[:, None] * inv_freq[None, :]
    tables = [np.concatenate([t[0:P], t[P:]], axis=1) for t in (np.cos(angle), np.sin(angle))]
    p = np.arange(P)[:, None]
    j, c = np.divmod(np.arange(32), 8)
    b_place = (c // 2 == j) & (c % 2 == p // 64)
    j, par = np.divmod(np.arange(8), 2)
    c_place = p // 16 == 2 * j + par
    return np.concatenate([np.eye(P)] + masks + tables + [b_place, c_place], axis=1).astype(f32)


_INS = ("x even_w_in even_lam_q1 even_lam_k1 even_lam_q2 even_lam_k2 even_subln_g even_sinks even_w_out odd_w_in "
        "odd_conv_w odd_conv_b odd_gate_w odd_gate_b odd_lru_lambda odd_w_out pre_mix_g post_mix_g pre_mlp_g "
        "post_mlp_g mlp_w1 mlp_w2 norm1_g_2 w_in_2 a_re_2 a_im_2 log_dt_2 b_re_2 b_im_2 c_re_2 c_im_2 d_skip_2 "
        "w_glu_2 b_glu_2 w_out_2 norm2_g_2 w_gate_2 w_up_2 w_down_2 final_g_2").split()


def kernel(**inputs):
    import concourse.bacc as bacc
    from concourse.bass_utils import run_bass_kernel_spmd

    nc = bacc.Bacc("TRN2", target_bir_lowering=False, num_devices=1)
    arrays = {f"in_{name}": np.ascontiguousarray(inputs[name]) for name in _INS}
    arrays["in_consts"] = shape_constants()
    aps = {name[3:]: nc.dram_tensor(name, a.shape, mybir.dt.from_np(a.dtype), kind="ExternalInput").ap()
           for name, a in arrays.items()}
    out = nc.dram_tensor("out", (1, SEQ, D), F32, kind="ExternalOutput").ap()
    build(nc, aps, out)
    return run_bass_kernel_spmd(nc, [arrays], core_ids=[0]).results[0]["out"]
```
